# Optimizing a Trainium2 kernel written in Bass

```python
import math
import jax, jax.numpy as jnp
from jax import lax
import numpy as np

D_MODEL = 1024
BATCH = 1
SEQ = 256
DEPTH = 1
DEC_BATCH = 8
DEC_SEQ = 4
PAST_LEN = 2048
PAGE_SIZE = 128

HG_HEADS = 4
HG_DK = 128
HG_DV = 128
HG_WIDTH_K = HG_HEADS * HG_DK
HG_WIDTH_V = HG_HEADS * HG_DV
HG_CHUNK = 64
AT_HEADS = 8
AT_DH = 64
AT_WIDTH = AT_HEADS * AT_DH
MOBA_BLOCK = 256
MOBA_TOPK = 3
Q_BLOCK = 128
ROPE_THETA = 10000.0
D_FF = -(-8 * D_MODEL // (3 * 256)) * 256
EPS = 1e-6
IN_SIZES = (HG_WIDTH_K, HG_WIDTH_K, HG_WIDTH_V, HG_WIDTH_V, AT_WIDTH, AT_WIDTH, AT_WIDTH, D_MODEL, D_MODEL)
IN_COLS = sum(IN_SIZES)

kernel_name = "hybrid_hgrn2_moba_decoder_step"

def rmsnorm(x, w):
    xf = x.astype(jnp.float32)
    y = xf * lax.rsqrt(jnp.mean(xf * xf, axis=-1, keepdims=True) + EPS)
    return (y * w.astype(jnp.float32)).astype(x.dtype)

def rope(x, pos):
    half = x.shape[-1] // 2
    inv = ROPE_THETA ** (-jnp.arange(half, dtype=jnp.float32) / half)
    ang = pos.astype(jnp.float32)[:, None] * inv[None, :]
    cos = jnp.cos(ang)[None, :, None, :]
    sin = jnp.sin(ang)[None, :, None, :]
    xf = x.astype(jnp.float32)
    x1, x2 = xf[..., :half], xf[..., half:]
    return jnp.concatenate([x1 * cos - x2 * sin, x2 * cos + x1 * sin], axis=-1).astype(x.dtype)

def hgrn2_recurrence(q, k, v, logf, s0, chunk):
    B, T, H, _ = q.shape
    n = T // chunk

    def to_chunks(a):
        return a.astype(jnp.float32).reshape(B, n, chunk, H, a.shape[-1]).transpose(1, 0, 3, 2, 4)

    qc, kc, vc, gc = to_chunks(q), to_chunks(k), to_chunks(v), to_chunks(logf)
    causal = jnp.tril(jnp.ones((chunk, chunk), dtype=bool))[None, None, :, :, None]

    def step(S, inp):
        qi, ki, vi, gi = inp
        b = jnp.cumsum(gi, axis=2)
        o_inter = jnp.einsum('bhtd,bhde->bhte', qi * jnp.exp(b), S)
        diff = b[:, :, :, None, :] - b[:, :, None, :, :]
        decay = jnp.exp(jnp.where(causal, diff, -jnp.inf))
        a = jnp.einsum('bhtd,bhsd,bhtsd->bhts', qi, ki, decay)
        o = o_inter + jnp.einsum('bhts,bhse->bhte', a, vi)
        b_last = b[:, :, -1, :]
        S_new = jnp.exp(b_last)[..., None] * S + jnp.einsum('bhsd,bhse->bhde', ki * jnp.exp(b_last[:, :, None, :] - b), vi)
        return S_new, o

    S, o = lax.scan(step, s0.astype(jnp.float32), (qc, kc, vc, gc))
    o = o.transpose(1, 0, 3, 2, 4).reshape(B, T, H, v.shape[-1])
    return o, S

def moba_attend(q, k, v, q_pos):
    B, L, H, dh = k.shape
    nb = -(-L // MOBA_BLOCK)
    pad = nb * MOBA_BLOCK - L

    def blocks(a):
        if pad:
            a = jnp.pad(a, ((0, 0), (0, pad), (0, 0), (0, 0)))
        return a.reshape(B, nb, MOBA_BLOCK, H, dh)

    kb, vb = blocks(k), blocks(v)
    kmean = jnp.mean(kb.astype(jnp.float32), axis=2)
    ksel = max(1, min(MOBA_TOPK, nb - 1))
    scale = dh ** -0.5
    gather_sel = jax.vmap(jax.vmap(lambda a_bh, s_bh: a_bh[s_bh], in_axes=(2, 0)), in_axes=(0, 0))

    def chunk_fn(args):
        qc, pc = args
        Qc = qc.shape[1]
        qh = qc.astype(jnp.float32).transpose(0, 2, 1, 3) * scale
        own = pc // MOBA_BLOCK
        gate = jnp.einsum('bhqd,bnhd->bhqn', qh, kmean)
        past_ok = jnp.arange(nb)[None, :] < own[:, None]
        gate = jnp.where(past_ok[None, None], gate, -jnp.inf)
        _, sel = lax.top_k(gate, ksel)
        sel_ok = sel < own[None, None, :, None]
        k_sel = gather_sel(kb, sel).astype(jnp.float32)
        v_sel = gather_sel(vb, sel).astype(jnp.float32)
        k_own = kb[:, own].astype(jnp.float32)
        v_own = vb[:, own].astype(jnp.float32)
        s_sel = jnp.einsum('bhqd,bhqkld->bhqkl', qh, k_sel)
        s_sel = jnp.where(sel_ok[..., None], s_sel, -jnp.inf).reshape(B, H, Qc, ksel * MOBA_BLOCK)
        kpos_own = own[:, None] * MOBA_BLOCK + jnp.arange(MOBA_BLOCK)[None, :]
        s_own = jnp.einsum('bhqd,bqlhd->bhql', qh, k_own)
        s_own = jnp.where((kpos_own <= pc[:, None])[None, None], s_own, -jnp.inf)
        p = jax.nn.softmax(jnp.concatenate([s_sel, s_own], axis=-1), axis=-1)
        p_sel = p[..., :ksel * MOBA_BLOCK].reshape(B, H, Qc, ksel, MOBA_BLOCK)
        p_own = p[..., ksel * MOBA_BLOCK:]
        o = jnp.einsum('bhqkl,bhqkld->bhqd', p_sel, v_sel) + jnp.einsum('bhql,bqlhd->bhqd', p_own, v_own)
        return o.transpose(0, 2, 1, 3).astype(qc.dtype)

    Tq = q.shape[1]
    if Tq > Q_BLOCK and Tq % Q_BLOCK == 0:
        nq = Tq // Q_BLOCK
        qs = q.reshape(B, nq, Q_BLOCK, H, dh).transpose(1, 0, 2, 3, 4)
        ps = q_pos.reshape(nq, Q_BLOCK)
        o = lax.map(chunk_fn, (qs, ps))
        return o.transpose(1, 0, 2, 3, 4).reshape(B, Tq, H, dh)
    return chunk_fn((q, q_pos))

def hybrid_layer(x, c, pos0, s0, k_past, v_past, lb, w_ada, b_ada, g_pre1, g_post1, w_in, g_onorm,
                 w_proj_a, w_proj_b, w_out, g_pre2, g_post2, w_gu, w_down):
    B, T, _ = x.shape
    mod = jnp.dot(jax.nn.silu(c), w_ada) + b_ada
    sh1, sc1, gt1, sh2, sc2, gt2 = [m[:, None, :] for m in jnp.split(mod, 6, axis=-1)]
    h = rmsnorm(x, g_pre1) * (1.0 + sc1) + sh1
    proj = jnp.dot(h, w_in)
    splits = np.cumsum(IN_SIZES)[:-1].tolist()
    hq, hf, hi, hg, aq, ak, av, ua, ub = jnp.split(proj, splits, axis=-1)
    f = lb + (1.0 - lb) * jax.nn.sigmoid(hf.astype(jnp.float32))
    logf = jnp.log(f)
    kin = 1.0 - f
    chunk = HG_CHUNK if T % HG_CHUNK == 0 else T
    o_a, s_new = hgrn2_recurrence(hq.reshape(B, T, HG_HEADS, HG_DK), kin.reshape(B, T, HG_HEADS, HG_DK),
                                  hi.reshape(B, T, HG_HEADS, HG_DV), logf.reshape(B, T, HG_HEADS, HG_DK), s0, chunk)
    o_a = rmsnorm(o_a, g_onorm) * jax.nn.silu(hg.reshape(B, T, HG_HEADS, HG_DV).astype(jnp.float32))
    o_a = o_a.reshape(B, T, HG_WIDTH_V).astype(x.dtype)
    pos = pos0 + jnp.arange(T, dtype=jnp.int32)
    q = rope(aq.reshape(B, T, AT_HEADS, AT_DH), pos)
    k = rope(ak.reshape(B, T, AT_HEADS, AT_DH), pos)
    v = av.reshape(B, T, AT_HEADS, AT_DH)
    k_all = jnp.concatenate([k_past.astype(k.dtype), k], axis=1)
    v_all = jnp.concatenate([v_past.astype(v.dtype), v], axis=1)
    o_b = moba_attend(q, k_all, v_all, pos).reshape(B, T, AT_WIDTH)
    merged = jax.nn.sigmoid(ua) * jnp.dot(o_a, w_proj_a) + jax.nn.sigmoid(ub) * jnp.dot(o_b, w_proj_b)
    x = x + gt1 * rmsnorm(jnp.dot(merged, w_out), g_post1)
    h = rmsnorm(x, g_pre2) * (1.0 + sc2) + sh2
    g_, u_ = jnp.split(jnp.dot(h, w_gu), 2, axis=-1)
    x = x + gt2 * rmsnorm(jnp.dot(jax.nn.silu(g_) * u_, w_down), g_post2)
    return x, s_new, k, v

def setup_inputs(seed: int = 0) -> dict:
    key = jax.random.key(seed)
    ks = jax.random.split(key, 24)
    f32 = jnp.float32
    n_pages = PAST_LEN // PAGE_SIZE
    n_pool = (5 * DEC_BATCH * n_pages + 3) // 4

    def nrm(k, shape, scale):
        return jax.random.normal(k, shape, f32) * scale

    def gain(k, shape):
        return 1.0 + 0.02 * jax.random.normal(k, shape, f32)

    page_table = jax.random.permutation(ks[7], n_pool)[:DEC_BATCH * n_pages].reshape(DEC_BATCH, n_pages).astype(jnp.int32)
    return {
        "x_prompt": nrm(ks[0], (BATCH, SEQ, D_MODEL), 1.0),
        "x_sample": nrm(ks[1], (DEC_BATCH, DEC_SEQ, D_MODEL), 1.0),
        "c_prompt": nrm(ks[2], (BATCH, D_MODEL), 1.0),
        "c_sample": nrm(ks[3], (DEC_BATCH, D_MODEL), 1.0),
        "state_hgrn": nrm(ks[4], (DEPTH, DEC_BATCH, HG_HEADS, HG_DK, HG_DV), 0.5),
        "cache_k": nrm(ks[5], (DEPTH, n_pool, PAGE_SIZE, AT_HEADS, AT_DH), 1.0),
        "cache_v": nrm(ks[6], (DEPTH, n_pool, PAGE_SIZE, AT_HEADS, AT_DH), 1.0),
        "page_table": page_table,
        "hg_lb": nrm(ks[8], (DEPTH + 1, HG_WIDTH_K), 1.0),
        "w_ada": nrm(ks[9], (DEPTH, D_MODEL, 6 * D_MODEL), 0.5 * D_MODEL ** -0.5),
        "b_ada": nrm(ks[10], (DEPTH, 6 * D_MODEL), 0.01),
        "g_pre1": gain(ks[11], (DEPTH, D_MODEL)),
        "g_post1": gain(ks[12], (DEPTH, D_MODEL)),
        "w_in": nrm(ks[13], (DEPTH, D_MODEL, IN_COLS), D_MODEL ** -0.5),
        "g_onorm": gain(ks[14], (DEPTH, HG_DV)),
        "w_proj_a": nrm(ks[15], (DEPTH, HG_WIDTH_V, D_MODEL), HG_WIDTH_V ** -0.5),
        "w_proj_b": nrm(ks[16], (DEPTH, AT_WIDTH, D_MODEL), AT_WIDTH ** -0.5),
        "w_out": nrm(ks[17], (DEPTH, D_MODEL, D_MODEL), D_MODEL ** -0.5),
        "g_pre2": gain(ks[18], (DEPTH, D_MODEL)),
        "g_post2": gain(ks[19], (DEPTH, D_MODEL)),
        "w_gu": nrm(ks[20], (DEPTH, D_MODEL, 2 * D_FF), D_MODEL ** -0.5),
        "w_down": nrm(ks[21], (DEPTH, D_FF, D_MODEL), D_FF ** -0.5),
    }

def reference(x_prompt, x_sample, c_prompt, c_sample, state_hgrn, cache_k, cache_v, page_table, hg_lb,
              w_ada, b_ada, g_pre1, g_post1, w_in, g_onorm, w_proj_a, w_proj_b, w_out, g_pre2, g_post2,
              w_gu, w_down):
    bp = x_prompt.shape[0]
    bs = x_sample.shape[0]
    n_pages = page_table.shape[1]
    lb_all = jnp.cumsum(jax.nn.softmax(hg_lb.astype(jnp.float32), axis=0), axis=0)
    xp, xs = x_prompt, x_sample
    sp_l, ss_l, kp_l, vp_l, ks_l, vs_l = [], [], [], [], [], []
    for l in range(DEPTH):
        w = (w_ada[l], b_ada[l], g_pre1[l], g_post1[l], w_in[l], g_onorm[l], w_proj_a[l], w_proj_b[l],
             w_out[l], g_pre2[l], g_post2[l], w_gu[l], w_down[l])
        s0 = jnp.zeros((bp, HG_HEADS, HG_DK, HG_DV), jnp.float32)
        empty = jnp.zeros((bp, 0, AT_HEADS, AT_DH), xp.dtype)
        xp, sp, kp, vp = hybrid_layer(xp, c_prompt, 0, s0, empty, empty, lb_all[l], *w)
        k_past = cache_k[l][page_table].reshape(bs, n_pages * PAGE_SIZE, AT_HEADS, AT_DH)
        v_past = cache_v[l][page_table].reshape(bs, n_pages * PAGE_SIZE, AT_HEADS, AT_DH)
        xs, ss, ksn, vsn = hybrid_layer(xs, c_sample, PAST_LEN, state_hgrn[l], k_past, v_past, lb_all[l], *w)
        sp_l.append(sp.astype(state_hgrn.dtype))
        ss_l.append(ss.astype(state_hgrn.dtype))
        kp_l.append(kp.astype(cache_k.dtype))
        vp_l.append(vp.astype(cache_v.dtype))
        ks_l.append(ksn.astype(cache_k.dtype))
        vs_l.append(vsn.astype(cache_v.dtype))
    return (xp, xs, jnp.stack(sp_l), jnp.stack(ss_l), jnp.stack(kp_l), jnp.stack(vp_l), jnp.stack(ks_l), jnp.stack(vs_l))


_drawn_inputs = setup_inputs


def setup_inputs(seed=0):
    import zlib

    import numpy as np

    out = dict(_drawn_inputs(seed))
    spreads = {}
    factors = {'g_pre1': 2.971, 'g_post1': 8.0, 'g_onorm': 8.0, 'g_pre2': 22.618, 'g_post2': 31.822}
    for name, (base, spread) in spreads.items():
        noise = np.random.default_rng([zlib.crc32(name.encode()), seed]).standard_normal(out[name].shape)
        drawn = base * np.exp(spread * noise) if base else spread * noise
        out[name] = __import__('jax').numpy.asarray(drawn.astype(out[name].dtype))
    for name, factor in factors.items():
        out[name] = (out[name] * factor).astype(out[name].dtype)
    return out
```

```python
from contextlib import ExitStack

import numpy as np
import concourse.bass as bass
from concourse import mybir

F32 = mybir.dt.float32
F32R = mybir.dt.float32r
I32 = mybir.dt.int32
U8 = mybir.dt.uint8
ALU = mybir.AluOpType
ACT = mybir.ActivationFunctionType
AX = mybir.AxisListType.X

P = 128
D = 1024
DT = D // P
TP = 256
NSEQ, TS = 8, 4
TSA = NSEQ * TS
T = TP + TSA
CC = 1 + NSEQ
HH, DK = 4, 128
AH, DH = 8, 64
PAIRS = AH // 2
PAST, PAGE = 2048, 128
NPG = PAST // PAGE
MB = 256
NB = PAST // MB
TOPK = 3
DFF = 2816
EPS = 1e-6
NEG = -1.0e30
INW = 5632
PT_ = INW // P
HQ, HF, HI, HG, AQ, AK, AV, UA, UB = 0, 4, 8, 12, 16, 20, 24, 28, 36
NSLOT = 4
BK = 4
BC = 512
KEYS = PAST + 32
SW = KEYS // 4 + 24
SW = 17 * 32
LEVELS = [64, 32, 16, 8, 4, 2, 1]

R_ADA, R_PRE1, R_POST1, R_PRE2, R_POST2, R_LB, R_ON, R_ALL = 0, 48, 56, 64, 72, 80, 88, 89


def constants():
    p = np.arange(P)
    c = {}
    c["ident"] = np.eye(P)
    c["foldc"] = np.zeros((P, CC))
    for i in range(2 * CC):
        c["foldc"][i, i % CC] = 1
    c["ones"] = np.ones((P, P))
    c["eps"] = np.full((P, 1), EPS)
    c["fold"] = (p[:, None] % 32 == p[None, :] % 32).astype(float)
    swap = np.zeros((P, P))
    swap[p ^ 32, p] = 1
    c["swap"] = swap
    for s in range(4):
        c[f"spread{s}"] = c["fold"] * (p[:, None] // 32 == s)
    half = DH // 2
    pos = np.concatenate([np.arange(TP), np.tile(PAST + np.arange(TS), NSEQ)]).astype(np.float32)
    inv = np.float32(10000.0) ** (-np.arange(half, dtype=np.float32) / np.float32(half))
    ang = pos[None, :] * inv[p % half][:, None]
    c["cos"] = np.cos(ang)
    c["sin"] = np.sin(ang) * np.where(p % DH < half, -1.0, 1.0)[:, None]
    start = np.ones(T)
    start[[0, P]] = 0
    start[TP::TS] = 0
    c["carry"] = np.tile(start, (P, 1))
    c["causal"] = np.where(p[None, :] <= p[:, None], 0.0, NEG)
    own = np.full((P, NSEQ, TSA), NEG)
    for r in range(32):
        for b in range(NSEQ):
            for k in range(r % TS + 1):
                own[r, b, b * TS + k] = 0
    c["own"] = own.reshape(P, -1)
    tie = (np.arange(NB)[None, :] < np.arange(NB)[:, None]).astype(float)
    c["tie"] = np.tile(tie.reshape(1, -1), (P, 1))
    c["ownhead"] = (p[:, None] % 32 // TS == np.arange(AH)[None, :]).astype(float)
    c["sumheads"] = ((p[:, None] // 32 == np.arange(16)[None, :] // TS) & (p[:, None] % TS == np.arange(16)[None, :] % TS)).astype(float)
    c["seq"] = (p[:, None] // TS == np.arange(NSEQ)[None, :]).astype(float)
    at, n = {}, 0
    c["pad"] = np.zeros((P, -sum(v.shape[1] for v in c.values()) % 8))
    for k, v in c.items():
        at[k] = (n, n + v.shape[1])
        n += v.shape[1]
    return np.concatenate(list(c.values()), 1).astype(np.float32), at


def level_masks():
    s, t = np.arange(P)[:, None], np.arange(P)[None, :]
    lv = [(s // (2 * m) == t // (2 * m)) & (s % (2 * m) < m) & (t % (2 * m) >= m) for m in LEVELS]
    return np.stack(lv + [s == t], 1).astype(np.int32)


def build(nc, inp, out):
    _, at = constants()
    NCONST = max(e for _, e in at.values())
    FIRST = at["eps"][1]

    base = (nc.sbuf_base + 31) // 32 * 32
    place = {}

    def sb(name, shape, dt=F32, over=None, off=0):
        nonlocal base
        size = int(np.prod(shape[1:])) * (1 if dt == U8 else 4)
        if over is None:
            o = base
            base += (size + 31) // 32 * 32
        else:
            o = place[over][0] + off
            assert off + size <= place[over][1], (name, off + size, place[over])
        place[name] = (o, size)
        return nc.alloc_sbuf_tensor_at(name, shape, dt, offset=o)

    const = sb("const", [P, NCONST])

    def C(name, rows=P):
        a, e = at[name]
        return const[0:rows, a:e]

    lvl = sb("lvl", [P, 8, P], U8)
    cols = sb("cols", [P, R_ALL])
    modT = sb("modT", [P, 48, CC])
    gain = sb("gain", [P, DT, CC])
    cst = sb("cst", [P, DT, 2 * CC], F32R)
    cs = sb("cs", [P, DT, CC])
    lbt = sb("lbt", [P, 6, HH])
    rs = sb("rs", [P, T])
    xT = sb("xT", [P, DT, T])
    stat = sb("stat", [P, 400])
    nmx = sb("nmx", [P, 2, 2])
    den = sb("den", [P, 2, 2])
    vtok = sb("vtok", [P, 3, AH * DH])
    pgt = sb("pgt", [1, NSEQ * NPG], I32)
    ring = sb("ring", [P, NSLOT, BK * BC])
    sb("split_area", [P, 4 * BK * BC])
    sb("proj_area", [P, PT_, T])
    sb("a_area", [P, 2, DT, T])
    sb("s_area", [P, 2, DT, T])
    sb("w_area", [P, 2, 16, P])
    TB = T * 4

    w_hi = sb("w_hi", [P, 2, BK, BC], F32R, "split_area")
    w_lo = sb("w_lo", [P, 2, BK, BC], F32R, "split_area", 2 * BK * BC * 4)
    KT = sb("KT", [P, 2, 8, 512], F32, "split_area")
    proj = sb("proj", [P, PT_, T], F32, "proj_area")
    xtok = sb("xtok", [P, 3, D], F32, "proj_area")
    prow = sb("prow", [P, P], F32, "proj_area", 3 * D * 4)
    crow = sb("crow", [CC, D], F32, "proj_area", 3 * D * 4 + P * 4)
    h_hi = sb("h_hi", [P, DT, T], F32R, "a_area")
    h_lo = sb("h_lo", [P, DT, T], F32R, "a_area", DT * TB)
    h32 = sb("h32", [P, DT, T], F32, "s_area")
    sq = sb("sq", [P, DT, T], F32, "s_area", DT * TB)
    arow = sb("arow", [2 * CC, BC], F32, "w_area")
    lvl_i = sb("lvl_i", [P, 8, P], I32, "w_area", BC * 4)
    Qrep = sb("Qrep", [P, PAIRS, 4, TSA], F32, "a_area")
    Qbd = sb("Qbd", [P, PAIRS, NSEQ, 32], F32, "a_area", 2048)
    ktok = sb("ktok", [P, 3, AH * DH], F32, "a_area", 6144)
    cmp1 = sb("cmp1", [P, NSEQ, NB, NB], F32, "a_area", 6144)
    cmp2 = sb("cmp2", [P, NSEQ, NB, NB], F32, "a_area", 8192)
    S = sb("S", [P, NSEQ, SW], F32, "s_area")
    Wq = sb("Wq", [P, 2, 16, P], F32, "w_area")
    Pt = sb("Pt", [P, NSEQ, SW // 32, 32], F32, "a_area")
    hb = sb("hb", [P, HH, T], F32, "split_area")
    hx = [sb(f"hx{i}", [P, HH, T], F32, "split_area", (1 + i) * HH * TB) for i in range(2)]
    hqt = sb("hqt", [P, HH, T], F32, "split_area", 3 * HH * TB)
    hkt = sb("hkt", [P, HH, T], F32, "split_area", 4 * HH * TB)
    hktok = sb("hktok", [P, 2, HH, DK], F32, "split_area", 5 * HH * TB)
    hvtok = sb("hvtok", [P, 2, HH, DK], F32, "split_area", 5 * HH * TB + 4096)
    S0 = sb("S0", [P, NSEQ, HH, DK], F32, "w_area")
    hA = sb("hA", [P, 2, HH, P], F32, "s_area")
    D0 = sb("D0", [P, HH, DK], F32, "s_area", 4096)
    Sfin = sb("Sfin", [P, HH, DK], F32, "s_area", 6144)
    hks = sb("hks", [TSA, HH, DK], F32, "s_area", 8192)
    hvs = sb("hvs", [TSA, HH, DK], F32, "s_area", 10240)
    vms = sb("vms", [TSA, NSEQ, DK], F32, "s_area", 12288)
    hAs = sb("hAs", [TSA, HH, TSA], F32, "s_area", 16384)
    om = sb("om", [P, AH, DH], F32, "s_area", 12288)
    pa = sb("pa", [P, 2, 384], F32, "proj_area", AV * TB)
    paT = sb("paT", [P, 384], F32, "proj_area", AV * TB + 3072)
    oa_hi = sb("oa_hi", [P, HH, T], F32R, "a_area")
    oa_lo = sb("oa_lo", [P, HH, T], F32R, "a_area", HH * TB)
    ob_hi = sb("ob_hi", [P, PAIRS, T], F32R, "a_area", 2 * HH * TB)
    ob_lo = sb("ob_lo", [P, PAIRS, T], F32R, "a_area", 3 * HH * TB)
    m_hi = sb("m_hi", [P, DT, T], F32R, "s_area")
    m_lo = sb("m_lo", [P, DT, T], F32R, "s_area", DT * TB)
    f_hi = sb("f_hi", [P, DFF // P, T], F32R, "proj_area")
    f_lo = sb("f_lo", [P, DFF // P, T], F32R, "proj_area", DFF // P * TB)
    y2 = sb("y2", [P, DT, T], F32, "w_area")
    fa = sb("fa", [P, 2, T], F32, "w_area", DT * TB)
    fu = sb("fu", [P, 2, T], F32, "w_area", DT * TB + 2 * TB)
    ytok = sb("ytok", [P, 3, D], F32, "s_area")
    assert base <= nc.sbuf_usable_end, base

    ps = nc.alloc_psum_tensor("ps", [P, 8, 512], F32)
    made = {}

    def sem(name):
        if name not in made:
            made[name] = nc.alloc_semaphore(name)
        return made[name]

    def over(ap, axis, n):
        a = ap.unsqueeze(axis)
        shape = list(a.shape)
        shape[axis] = n
        return a.broadcast_to(shape)

    ident, ones, fold = C("ident"), C("ones"), C("fold")
    pools = {k: inp[k] for k in ("cache_k", "cache_v")}
    AQK = PAIRS
    NA = 46
    SAMP = slice(TP, T)

    A_ORDER = [("ada", g) for g in range(4)] + [("in", 0)]
    for i in range(7):
        A_ORDER += [("ada", 4 + i), ("in", 1 + i)]
    A_ORDER += [("ada", 11), ("in", 8), ("in", 9), ("in", 10)]
    KV_SLOT = [(NA + j) % NSLOT for j in range(4)]
    B0 = NA + 64

    def w_src(name, row, col, rows=BK * P, width=BC):
        return inp[name][0, bass.ds(row, rows), bass.ds(col, width)].rearrange("(k p) n -> p k n", p=P)

    def slot4(s):
        return ring[:, s, :].rearrange("p (k n) -> p k n", n=BC)

    block = nc.Block()
    with block:

        @block.sync
        def _(sp):
            n = 0
            for kind, g in A_ORDER[:5]:
                for k in range(2):
                    if n >= NSLOT:
                        sp.wait_ge(sem("lo_split"), n - NSLOT + 1)
                    sp.dma_start(slot4(n % NSLOT), w_src("w_" + kind, k * BK * P, g * BC)).then_inc(sem(f"a_landed{n % NSLOT}"), 16)
                    n += 1
            with sp.Fori(0, 7) as i:
                for j, (kind, g0, k) in enumerate([("ada", 4, 0), ("ada", 4, 1), ("in", 1, 0), ("in", 1, 1)]):
                    s = (n + j) % NSLOT
                    sp.wait_ge(sem("lo_split"), i * 4 + (n + j - NSLOT + 1))
                    sp.dma_start(slot4(s), w_src("w_" + kind, k * BK * P, (i + g0) * BC)).then_inc(sem(f"a_landed{s}"), 16)
            n += 28
            for kind, g in A_ORDER[19:]:
                for k in range(2):
                    sp.wait_ge(sem("lo_split"), n - NSLOT + 1)
                    sp.dma_start(slot4(n % NSLOT), w_src("w_" + kind, k * BK * P, g * BC)).then_inc(sem(f"a_landed{n % NSLOT}"), 16)
                    n += 1
            assert n == NA

            def page(pool, idx, s, q):
                pg = sp.value_load(pgt[0:1, bass.ds(idx, 1)], min_val=0, max_val=pools[pool].shape[1] - 1)
                return pools[pool][0, bass.ds(pg, 1), :, :].rearrange("o p n -> p (o n)")

            sp.wait_ge(sem("table_landed"), 16)
            with sp.Fori(0, NSEQ) as b:
                for j in range(4):
                    sp.wait_ge(sem("key_slots"), b * 4 + (j + 1))
                    for q in range(4):
                        sp.dma_start(ring[:, KV_SLOT[j], q * 512:(q + 1) * 512], page("cache_k", b * NPG + (4 * j + q), KV_SLOT[j], q))\
                            .then_inc(sem(f"k_landed{j}"), 16)
            sp.wait_ge(sem("kt_used"), 2 * NSEQ + 3)
            for g in range(4):
                sp.dma_start(S0[:, 2 * g:2 * g + 2], inp["state_hgrn"][0, 2 * g:2 * g + 2].rearrange("b h d e -> d b h e")).then_inc(sem("s0_landed"), 16)
            with sp.Fori(0, NSEQ) as b:
                for j in range(4):
                    sp.wait_ge(sem("value_slots"), b * 4 + (j + 1))
                    for q in range(4):
                        sp.dma_start(ring[:, KV_SLOT[j], q * 512:(q + 1) * 512], page("cache_v", b * NPG + (4 * j + q), KV_SLOT[j], q))\
                            .then_inc(sem(f"v_landed{j}"), 16)
            n = B0
            for cg in range(2):
                for name in ("w_proj_a", "w_proj_b"):
                    sp.wait_ge(sem("value_slots"), NSLOT + n - NSLOT - (NA + 32) + 1)
                    sp.dma_start(slot4(n % NSLOT), w_src(name, 0, cg * BC)).then_inc(sem(f"b_landed{n % NSLOT}"), 16)
                    n += 1
            for cg in range(2):
                for k in range(2):
                    sp.wait_ge(sem("lo_split"), n - NSLOT - 64 + 1)
                    sp.dma_start(slot4(n % NSLOT), w_src("w_out", k * BK * P, cg * BC)).then_inc(sem(f"b_landed{n % NSLOT}"), 16)
                    n += 1

            def load_gu(n_of, s, g, k):
                sp.wait_ge(sem("lo_split"), n_of)
                for half in range(2):
                    sp.dma_start(slot4(s)[:, :, half * 256:(half + 1) * 256], w_src("w_gu", k * BK * P, half * DFF + g * 256, width=256))\
                        .then_inc(sem(f"gu_landed{s}"), 16)

            for k in range(2):
                load_gu(n - NSLOT - 64 + 1, n % NSLOT, 0, k)
                n += 1
            with sp.Fori(0, 5) as i:
                for j in range(4):
                    load_gu(i * 4 + (n + j - NSLOT - 64 + 1), (n + j) % NSLOT, i * 2 + (1 + j // 2), j % 2)
            n += 20
            for cg in range(2):
                for c in range(6):
                    rows = min(BK, DFF // P - BK * c)
                    sp.wait_ge(sem("lo_split"), n - NSLOT - 64 + 1)
                    sp.dma_start(slot4(n % NSLOT)[:, 0:rows, :], w_src("w_down", c * BK * P, cg * BC, rows=rows * P))\
                        .then_inc(sem(f"d_landed{n % NSLOT}"), 16)
                    n += 1
            for tt in range(3):
                sp.wait_ge(sem("y_tok"), tt + 1)
                if tt < 2:
                    sp.dma_start(out["y_prompt"][0, tt * P:(tt + 1) * P, :], ytok[:, tt, :]).then_inc(sem("y_stored"), 16)
                else:
                    sp.dma_start(out["y_sample"].rearrange("b t d -> (b t) d"), ytok[0:TSA, 2, :]).then_inc(sem("y_stored"), 16)
            sp.wait_ge(sem("y_stored"), 48)

        @block.gpsimd
        def _(pool):
            pool.wait_ge(sem("lvl_landed"), 16)
            pool.tensor_copy(lvl[:, :, :], lvl_i[:, :, :]).then_inc(sem("lvl_ready"), 1)
            pool.wait_ge(sem("lvl_ready"), 1)
            pool.wait_ge(sem("mod_rows_turned"), 12)
            pool.memset(Wq[:, :, :, :], 0.0).then_inc(sem("wq_zero"), 1)
            pool.wait_ge(sem("wq_zero"), 1)
            pool.wait_ge(sem("q_spread"), 1)
            with pool.Fori(0, NSEQ // 2) as i:
                for bb in range(2):
                    pool.wait_ge(sem("kt_used"), i * 4 + (2 * bb + 1))
                    for a in range(4):
                        rows = slice(32 * a, 32 * a + 32)
                        for h in range(AH):
                            ins = pool.tensor_copy(
                                Wq[rows, bb, 2 * h:2 * h + 2, a * 32 + h * TS:a * 32 + (h + 1) * TS],
                                Qrep[rows, h // 2, 2 * (h % 2):2 * (h % 2) + 2, bass.ds(i * (2 * TS) + bb * TS, TS)])
                    ins.then_inc(sem("wq_ready"), 1)
            pool.wait_ge(sem("v_tok"), 1)
            pool.dma_start(out["v_prompt"][0, 0].rearrange("(t p) h d -> p t (h d)", p=P), vtok[:, 0:2, :]).then_inc(sem("v_stored"), 16)
            pool.dma_start(out["v_sample"][0].rearrange("b t h d -> (b t) (h d)"), vtok[0:TSA, 2, :]).then_inc(sem("v_stored"), 16)
            pool.wait_ge(sem("v_stored"), 32)
            pool.wait_ge(sem("k_stored"), 32)
            pool.wait_ge(sem("state_p"), 1)
            pool.dma_start(out["state_p"][0, 0].rearrange("h d e -> d h e"), Sfin[:, :, :]).then_inc(sem("st_stored"), 16)
            for g in range(2):
                pool.wait_ge(sem("state_s"), HH)
                pool.dma_start(out["state_s"][0, 4 * g:4 * g + 4].rearrange("b h d e -> d b h e"), S0[:, 4 * g:4 * g + 4]).then_inc(sem("st_stored"), 16)
            pool.wait_ge(sem("st_stored"), 48)

        @block.scalar
        def _(act):
            step = [0]

            def link(ins):
                step[0] += 1
                ins.then_inc(sem("act_step"), 1)
                act.wait_ge(sem("act_step"), step[0])

            act.dma_start(const[:, 0:FIRST], inp["const"][:, 0:FIRST]).then_inc(sem("const0_landed"), 16)
            act.dma_start(crow[0:1, :], inp["c_prompt"]).then_inc(sem("c_landed"), 16)
            act.dma_start(crow[1:CC, :], inp["c_sample"]).then_inc(sem("c_landed"), 16)
            act.dma_start(prow[R_ADA:R_ADA + 48, :], inp["b_ada"].rearrange("o (r n) -> (o r) n", n=P)).then_inc(sem("par_landed"), 16)
            for r, name in ((R_PRE1, "g_pre1"), (R_POST1, "g_post1"), (R_PRE2, "g_pre2"), (R_POST2, "g_post2")):
                act.dma_start(prow[r:r + 8, :], inp[name].rearrange("o (r n) -> (o r) n", n=P)).then_inc(sem("par_landed"), 16)
            act.dma_start(prow[R_LB:R_LB + 8, :], inp["hg_lb"].rearrange("o (r n) -> (o r) n", n=P)).then_inc(sem("par_landed"), 16)
            act.dma_start(prow[R_ON:R_ON + 1, :], inp["g_onorm"]).then_inc(sem("par_landed"), 16)
            act.dma_start(xtok[:, 0:2, :], inp["x_prompt"][0].rearrange("(t p) d -> p t d", p=P)).then_inc(sem("x_landed"), 16)
            act.dma_start(xtok[0:TSA, 2, :], inp["x_sample"].rearrange("b t d -> (b t) d")).then_inc(sem("x_landed"), 16)
            act.dma_start(pgt[:, :], inp["page_table"].rearrange("(o a) b -> o (a b)", o=1)).then_inc(sem("table_landed"), 16)
            act.dma_start(const[:, FIRST:], inp["const"][:, FIRST:]).then_inc(sem("const1_landed"), 16)
            act.dma_start(lvl_i[:, :, :], inp["lvl"]).then_inc(sem("lvl_landed"), 16)

            act.wait_ge(sem("rows_turned"), 1)
            act.activation(cols[:, :], ps[:, 6, 0:R_ALL], ACT.Copy).then_inc(sem("cols_ready"), 1)
            act.wait_ge(sem("rows_turned"), 2)
            link(act.activation(cs[:, :, :], ps[:, 7, 0:DT * CC].rearrange("p (k c) -> p k c", c=CC), ACT.Silu))
            act.activation(cst[:, :, 0:CC], cs[:, :, :], ACT.Copy).then_inc(sem("c_hi"), 1)

            def hi(w, landed, s, count, par, rows=BK):
                act.wait_ge(sem(f"{landed}{s}"), count)
                if not isinstance(w, int) or w >= 2:
                    act.wait_ge(sem("w_used"), w - 1)
                act.activation(w_hi[:, par, 0:rows, :], slot4(s)[:, 0:rows, :], ACT.Copy).then_inc(sem("hi_split"), 1)

            def hi_a(n):
                hi(n, "a_landed", n % NSLOT, 16 * (n // NSLOT + 1), n % 2)

            def evac_ada(g, w):
                act.wait_ge(sem("w_used"), w + 1)
                if not isinstance(g, int) or g >= 1:
                    act.wait_ge(sem("mod_rows_turned"), g)
                act.activation(arow[:, :], ps[0:2 * CC, 4, :], ACT.Copy).then_inc(sem("ada_rows"), 1)

            def evac_in(g, w):
                for j in range(4):
                    if j < 3:
                        act.wait_ge(sem("tile_done"), g * 3 + (j + 1))
                    else:
                        act.wait_ge(sem("w_used"), w + 1)
                    act.activation(proj[:, bass.ds(g * 4 + j, 1), :], ps[:, j:j + 1, 0:T], ACT.Copy).then_inc(sem("tile_out"), 1)

            hi_a(0)
            hi_a(1)
            for k in range(DT):
                act.wait_ge(sem("x_turned"), k + 1)
                act.activation(xT[:, k, :], ps[:, k % 4, 0:T], ACT.Copy).then_inc(sem("x_ready"), 1)
            for g in range(1, 4):
                hi_a(2 * g)
                evac_ada(g - 1, 2 * g - 1)
                hi_a(2 * g + 1)
            act.wait_ge(sem("x_sum"), 1)
            act.wait_ge(sem("const0_landed"), 16)
            act.activation(rs[:, :], ps[:, 7, 0:T], ACT.Sqrt, scale=1.0 / D, bias=C("eps")).then_inc(sem("root"), 1)
            evac_ada(3, 7)
            act.wait_ge(sem("h_ready"), 1)
            act.activation(h_hi[:, :, :], h32[:, :, :], ACT.Copy).then_inc(sem("h_hi"), 1)
            hi_a(8)
            hi_a(9)
            with act.Fori(0, 7) as i:
                hi(i * 4 + 10, "a_landed", 2, i * 16 + 48, 0)
                evac_in(i, i * 4 + 9)
                hi(i * 4 + 11, "a_landed", 3, i * 16 + 48, 1)
                hi(i * 4 + 12, "a_landed", 0, i * 16 + 64, 0)
                evac_ada(i + 4, i * 4 + 11)
                hi(i * 4 + 13, "a_landed", 1, i * 16 + 64, 1)
            hi_a(38)
            evac_in(7, 37)
            hi_a(39)
            hi_a(40)
            evac_ada(11, 39)
            hi_a(41)
            hi_a(42)
            evac_in(8, 41)
            hi_a(43)
            hi_a(44)
            evac_in(9, 43)
            hi_a(45)
            evac_in(10, 45)

            act.wait_ge(sem("tile_out"), 44)
            act.activation(proj[:, HF:HF + 4, :], proj[:, HF:HF + 4, :], ACT.Sigmoid).then_inc(sem("sig_f"), 1)
            act.wait_ge(sem("v_turned"), 1)
            act.activation(vtok[:, 0:2, :], ps[:, 0:2, :], ACT.Copy)
            act.activation(vtok[0:TSA, 2, :], ps[0:TSA, 2, :], ACT.Copy).then_inc(sem("v_tok"), 1)
            act.wait_ge(sem("k_turned_tok"), 1)
            act.activation(ktok[:, 0:2, :], ps[:, 4:6, :], ACT.Copy)
            act.activation(ktok[0:TSA, 2, :], ps[0:TSA, 6, :], ACT.Copy).then_inc(sem("k_tok"), 1)
            act.wait_ge(sem("k_tok"), 1)
            act.dma_start(out["k_prompt"][0, 0].rearrange("(t p) h d -> p t (h d)", p=P), ktok[:, 0:2, :]).then_inc(sem("k_stored"), 16)
            act.dma_start(out["k_sample"][0].rearrange("b t h d -> (b t) (h d)"), ktok[0:TSA, 2, :]).then_inc(sem("k_stored"), 16)
            act.activation(proj[:, UA:UA + 16, :], proj[:, UA:UA + 16, :], ACT.Sigmoid).then_inc(sem("sig_u"), 1)
            act.activation(proj[:, HG:HG + 4, :], proj[:, HG:HG + 4, :], ACT.Silu).then_inc(sem("silu_g"), 1)

            act.nop().then_inc(sem("scores_out"), 2)
            with act.Fori(0, NSEQ // 2) as i:
                for bb in range(2):
                    act.wait_ge(sem("kt_used"), i * 4 + (2 * bb + 5))
                    act.activation(S[:, bass.ds(i * 2 + bb, 1), 0:512], ps[:, bb:bb + 1, :], ACT.Copy).then_inc(sem("scores_out"), 1)
            act.wait_ge(sem("s_shifted"), 1)
            for b in range(NSEQ):
                act.activation(S[:, b, :], S[:, b, :], ACT.Exp, accum_out=stat[:, 320 + b:321 + b]).then_inc(sem("s_exp"), 1)

            act.wait_ge(sem("lb_arg"), 1)
            act.activation(lbt[:, 1:3, :], lbt[:, 1:3, :], ACT.Exp).then_inc(sem("lb_exp"), 1)
            act.wait_ge(sem("f_ready"), 1)
            act.activation(hkt[:, :, :], proj[:, HF:HF + 4, :], ACT.Ln).then_inc(sem("logf"), 1)
            act.wait_ge(sem("b_ready"), 1)
            act.activation(hqt[:, :, :], hb[:, :, :], ACT.Exp).then_inc(sem("eb"), 1)
            act.wait_ge(sem("kd_ready"), 1)
            act.activation(hkt[:, :, :], hkt[:, :, :], ACT.Exp).then_inc(sem("ekd"), 1)
            act.wait_ge(sem("h_turned"), 1)
            act.activation(hktok[:, :, :, :], ps[:, 2:4, :].rearrange("p t (h d) -> p t h d", h=HH), ACT.Copy)
            act.activation(hvtok[:, :, :, :], ps[:, 4:6, :].rearrange("p t (h d) -> p t h d", h=HH), ACT.Copy)
            act.activation(hks[:, :, :], ps[0:TSA, 6, :].rearrange("p (h d) -> p h d", h=HH), ACT.Copy)
            act.activation(hvs[:, :, :], ps[0:TSA, 7, :].rearrange("p (h d) -> p h d", h=HH), ACT.Copy).then_inc(sem("h_tok"), 1)
            for li, m in enumerate(LEVELS):
                r = TP if m > 2 else T
                act.wait_ge(sem("lv_diff"), li + 1)
                act.activation(hx[li % 2][:, :, 0:r], hx[li % 2][:, :, 0:r], ACT.Exp).then_inc(sem("lv_exp"), 1)
            act.wait_ge(sem("d_done"), 1)
            act.activation(D0[:, :, :], ps[:, 2, :].rearrange("p (h d) -> p h d", h=HH), ACT.Copy).then_inc(sem("d0_ready"), 1)
            act.wait_ge(sem("o_done"), 1)
            for t in range(2):
                act.activation(hb[:, :, t * P:(t + 1) * P], ps[:, 4 + t, :].rearrange("p (h d) -> p h d", h=HH), ACT.Copy)
            link(act.activation(hb[:, :, SAMP], ps[:, 6, 0:HH * TSA].rearrange("p (h d) -> p h d", h=HH), ACT.Copy))
            act.activation(hx[0][:, :, :], hb[:, :, :], ACT.Square).then_inc(sem("o_sq"), 1)
            act.wait_ge(sem("o_sum"), 1)
            for t in range(2):
                act.activation(hx[1][:, :, t * P:(t + 1) * P], ps[:, 4 + t, :].rearrange("p (h d) -> p h d", h=HH), ACT.Sqrt, scale=1.0 / DK, bias=C("eps"))
            act.activation(hx[1][:, :, SAMP], ps[:, 6, 0:HH * TSA].rearrange("p (h d) -> p h d", h=HH), ACT.Sqrt, scale=1.0 / DK, bias=C("eps")).then_inc(sem("o_root"), 1)

            def pa_out(h):
                act.wait_ge(sem("pa_turned"), h + 1)
                if h >= 1:
                    act.wait_ge(sem("pv_done"), h)
                act.activation(paT[:, :], ps[:, 6 + h % 2, 0:384], ACT.Copy).then_inc(sem("paT_ready"), 1)
                if h % 2 == 1:
                    act.wait_ge(sem("pv_done"), h + 1)
                    act.activation(proj[:, AQ + h // 2, 0:TP], ps[:, (h // 2) % 2, 0:TP], ACT.Copy).then_inc(sem("ob_p"), 1)

            for h in range(AH):
                act.wait_ge(sem("pa_masked"), h + 1)
                for t in range(2):
                    a, e = (0, P) if t == 0 else (P, 3 * P)
                    ins = act.activation(pa[:, h % 2, a:e], pa[:, h % 2, a:e], ACT.Exp, bias=nmx[:, h % 2, t:t + 1], accum_out=den[:, h % 2, t:t + 1])
                ins.then_inc(sem("pa_exp"), 1)
                if h >= 1:
                    pa_out(h - 1)
            pa_out(AH - 1)

            def hi_b(w, landed="b_landed", rows=BK, first=110, step=16):
                n = w + 64
                hi(w, landed, n % NSLOT, step * ((n - first - (n - first) % NSLOT) // NSLOT + 1), w % 2, rows)

            act.wait_ge(sem("oa_ready"), 1)
            act.wait_ge(sem("value_slots"), NSLOT + 32)
            act.wait_ge(sem("ob_s"), 2)
            act.activation(oa_hi[:, :, :], proj[:, HQ:HQ + 4, :], ACT.Copy).then_inc(sem("oab_hi"), 1)
            act.wait_ge(sem("ob_p"), PAIRS)
            act.activation(ob_hi[:, :, :], proj[:, AQ:AQ + 4, :], ACT.Copy).then_inc(sem("oab_hi"), 1)

            def m_split(cg):
                act.wait_ge(sem("merged"), cg + 1)
                act.activation(m_hi[:, 4 * cg:4 * cg + 4, :], proj[:, UA + 4 * cg:UA + 4 * cg + 4, :], ACT.Copy).then_inc(sem("m_hi"), 1)

            def y_evac(cg):
                for j in range(4 * cg, 4 * cg + 4):
                    if j % 4 < 3:
                        act.wait_ge(sem("y1_done"), 3 * cg + j % 4 + 1)
                    else:
                        act.wait_ge(sem("w_used"), 52 + 2 * cg)
                    act.activation(proj[:, j, :], ps[:, j % 4, 0:T], ACT.Copy).then_inc(sem("y1_out"), 1)

            act.wait_ge(sem("st_stored"), 48)
            hi_b(46)
            hi_b(47)
            hi_b(48)
            m_split(0)
            hi_b(49)
            hi_b(50)
            m_split(1)
            hi_b(51)
            hi_b(52)
            y_evac(0)
            hi_b(53)
            hi(54, "gu_landed", 2, 32, 0)
            y_evac(1)
            hi(55, "gu_landed", 3, 32, 1)
            act.wait_ge(sem("y1_sum"), 1)
            act.activation(rs[:, :], ps[:, 4, 0:T], ACT.Sqrt, scale=1.0 / D, bias=C("eps")).then_inc(sem("root"), 1)
            act.wait_ge(sem("x1_ready"), 1)
            act.activation(sq[:, :, :], xT[:, :, :], ACT.Square).then_inc(sem("x1_sq"), 1)
            act.wait_ge(sem("x1_sum"), 1)
            act.activation(rs[:, :], ps[:, 5, 0:T], ACT.Sqrt, scale=1.0 / D, bias=C("eps")).then_inc(sem("root"), 1)
            act.wait_ge(sem("h_ready"), 2)
            act.activation(h_hi[:, :, :], h32[:, :, :], ACT.Copy).then_inc(sem("h_hi"), 1)

            def gates(g, base):
                act.wait_ge(sem("gu_done"), g * 3 + 2)
                act.wait_ge(sem("fu_ready"), g + 1)
                act.activation(fa[:, :, :], ps[:, base:base + 2, 0:T], ACT.Silu).then_inc(sem("silu_done"), 1)

            def f_split(g):
                act.wait_ge(sem("fu_ready"), g + 2)
                act.activation(f_hi[:, bass.ds(g * 2, 2), :], fu[:, :, :], ACT.Copy).then_inc(sem("f_hi"), 1)

            with act.Fori(0, 5) as i:
                hi(i * 4 + 56, "gu_landed", 0, i * 32 + 32, 0)
                gates(i * 2, 0)
                hi(i * 4 + 57, "gu_landed", 1, i * 32 + 32, 1)
                f_split(i * 2)
                hi(i * 4 + 58, "gu_landed", 2, i * 32 + 64, 0)
                gates(i * 2 + 1, 4)
                hi(i * 4 + 59, "gu_landed", 3, i * 32 + 64, 1)
                f_split(i * 2 + 1)

            def hi_d(i):
                hi_b(76 + i, "d_landed", 2 if i % 6 == 5 else BK, 140)

            def y2_evac(cg):
                for j in range(4):
                    if j < 3:
                        act.wait_ge(sem("y2_done"), 3 * cg + j + 1)
                    else:
                        act.wait_ge(sem("w_used"), 82 + 6 * cg)
                    act.activation(y2[:, 4 * cg + j, :], ps[:, 4 * (1 - cg) + j, 0:T], ACT.Copy).then_inc(sem("y2_out"), 1)

            hi_d(0)
            gates(10, 0)
            hi_d(1)
            f_split(10)
            for i in range(2, 7):
                hi_d(i)
            y2_evac(0)
            for i in range(7, 12):
                hi_d(i)
            y2_evac(1)
            act.wait_ge(sem("y2_sum"), 1)
            act.activation(rs[:, :], ps[:, 4, 0:T], ACT.Sqrt, scale=1.0 / D, bias=C("eps")).then_inc(sem("root"), 1)
            for tt in range(3):
                rows = P if tt < 2 else TSA
                act.wait_ge(sem("y_turned"), tt + 1)
                b0 = (0, 2, 5)[tt]
                act.activation(ytok[0:rows, tt, :], ps[0:rows, b0:b0 + 2, :], ACT.Copy).then_inc(sem("y_tok"), 1)

        @block.vector
        def _(dve):
            step = [0]

            def link(ins):
                step[0] += 1
                ins.then_inc(sem("dve_step"), 1)
                dve.wait_ge(sem("dve_step"), step[0])

            def lo(w, s, par, rows=BK):
                dve.wait_ge(sem("hi_split"), w + 1)
                dve.tensor_tensor(w_lo[:, par, 0:rows, :], slot4(s)[:, 0:rows, :], w_hi[:, par, 0:rows, :].bitcast(F32), ALU.subtract).then_inc(sem("lo_split"), 1)

            def lo_a(n):
                lo(n, n % NSLOT, n % 2)

            def mod_add(g):
                dve.wait_ge(sem("mod_rows_turned"), g + 1)
                dve.tensor_tensor(modT[:, bass.ds(g * 4, 4), :], ps[:, 5, 0:4 * CC].rearrange("p (k c) -> p k c", c=CC),
                                  over(cols[:, bass.ds(g * 4 + R_ADA, 4)], 2, CC), ALU.add).then_inc(sem("mod_ready"), 1)

            def scaled(dst, src, g, s, res):
                for k in range(DT):
                    if res is None:
                        ins = dve.tensor_scalar(dst[:, k, 0:TP], src[:, k, 0:TP], g[:, k, 0:1], s[:, k, 0:1], ALU.mult, ALU.add)
                    else:
                        ins = dve.scalar_tensor_tensor(dst[:, k, 0:TP], src[:, k, 0:TP], g[:, k, 0:1], res[:, k, 0:TP], ALU.mult, ALU.add)
                v = src[:, :, SAMP].rearrange("p k (b t) -> p k b t", t=TS)
                link(dve.tensor_tensor(v, v, over(g[:, :, 1:CC], 3, TS), ALU.mult))
                other = over(s[:, :, 1:CC], 3, TS) if res is None else res[:, :, SAMP].rearrange("p k (b t) -> p k b t", t=TS)
                return dve.tensor_tensor(dst[:, :, SAMP].rearrange("p k (b t) -> p k b t", t=TS), v, other, ALU.add)

            def part(k):
                return modT[:, 8 * k:8 * k + 8, :]

            dve.wait_ge(sem("c_hi"), 1)
            dve.tensor_tensor(cst[:, :, CC:2 * CC], cs[:, :, :], cst[:, :, 0:CC].bitcast(F32), ALU.subtract).then_inc(sem("c_lo"), 1)
            lo_a(0)
            lo_a(1)
            dve.wait_ge(sem("x_ready"), DT)
            dve.tensor_tensor(sq[:, :, :], xT[:, :, :], xT[:, :, :], ALU.mult).then_inc(sem("x_sq"), 1)
            for g in range(1, 4):
                lo_a(2 * g)
                lo_a(2 * g + 1)
                mod_add(g - 1)
            dve.wait_ge(sem("root"), 1)
            link(dve.reciprocal(rs[:, :], rs[:, :]))
            link(dve.tensor_tensor(sq[:, :, :], xT[:, :, :], over(rs[:, :], 1, DT), ALU.mult))
            mod_add(3)
            dve.wait_ge(sem("mod_ready"), 4)
            link(dve.scalar_tensor_tensor(gain[:, :, :], part(1), 1.0, over(cols[:, R_PRE1:R_PRE1 + DT], 2, CC), ALU.add, ALU.mult))
            scaled(h32, sq, gain, part(0), None).then_inc(sem("h_ready"), 1)
            dve.wait_ge(sem("h_hi"), 1)
            dve.tensor_tensor(h_lo[:, :, :], h32[:, :, :], h_hi[:, :, :].bitcast(F32), ALU.subtract).then_inc(sem("h_lo"), 1)
            lo_a(8)
            lo_a(9)
            with dve.Fori(0, 7) as i:
                lo(i * 4 + 10, 2, 0)
                lo(i * 4 + 11, 3, 1)
                lo(i * 4 + 12, 0, 0)
                lo(i * 4 + 13, 1, 1)
                mod_add(i + 4)
            for n in range(38, 42):
                lo_a(n)
            mod_add(11)
            for n in range(42, 46):
                lo_a(n)
            dve.wait_ge(sem("lo_split"), NA)
            dve.nop().then_inc(sem("key_slots"), NSLOT)

            cosb, sinb = over(C("cos"), 1, 4), over(C("sin"), 1, 4)
            dve.wait_ge(sem("const1_landed"), 16)
            for j, (t0, scale) in enumerate(((AQ, DH ** -0.5), (AK, 1.0))):
                dve.wait_ge(sem("swapped"), j + 1)
                x = proj[:, t0:t0 + 4, :]
                link(dve.scalar_tensor_tensor(sq[:, 4 * j:4 * j + 4, :], ps[:, 4 * j:4 * j + 4, 0:T], scale, sinb, ALU.mult, ALU.mult))
                dve.nop().then_inc(sem("swap_used"), 1)
                link(dve.scalar_tensor_tensor(x, x, scale, cosb, ALU.mult, ALU.mult))
                dve.tensor_tensor(x, x, sq[:, 4 * j:4 * j + 4, :], ALU.add).then_inc(sem("roped"), 1)
            dve.wait_ge(sem("w_used"), NA)
            link(dve.memset(Qbd[:, :, :, :], 0.0))
            dve.wait_ge(sem("roped"), 1)
            for pair in range(PAIRS):
                for hl in range(2):
                    rows = slice(64 * hl, 64 * hl + 64)
                    c = (2 * pair + hl) * TS
                    ins = dve.tensor_copy(Qbd[rows, pair, :, c:c + TS], proj[rows, AQ + pair, SAMP].rearrange("p (b t) -> p b t", t=TS))
            ins.then_inc(sem("q_blocks"), 1)
            dve.wait_ge(sem("spread_done"), 1)
            dve.tensor_copy(Qrep[:, :, :, :].rearrange("p a s t -> p s a t"), ps[:, 3, :].rearrange("p (s a t) -> p s a t", s=4, a=PAIRS)).then_inc(sem("q_spread"), 1)
            dve.wait_ge(sem("own_scored"), 1)
            link(dve.memset(S[:, :, 512:SW], NEG))
            dve.tensor_tensor(S[0:32, :, 512:SW], ps[0:32, 7, 0:256].rearrange("p (b k) -> p b k", b=NSEQ),
                              C("own", 32).rearrange("p (b k) -> p b k", b=NSEQ), ALU.add).then_inc(sem("own_out"), 1)

            with dve.Fori(0, NSEQ // 2) as i:
                for bb in range(2):
                    for j in range(4):
                        dve.wait_ge(sem(f"k_landed{j}"), i * 128 + (bb + 1) * 64)
                        if j % 2 == 0:
                            dve.wait_ge(sem("kt_used"), i * 4 + (2 * bb + j // 2 + 2))
                        dve.transpose(KT[:, j // 2, 4 * (j % 2):4 * (j % 2) + 4, :], ring[:, KV_SLOT[j], :].rearrange("p (g n) -> p g n", n=512))\
                            .then_inc(sem("key_slots"), 1)
            dve.wait_ge(sem("key_slots"), NSLOT + 32)
            dve.nop().then_inc(sem("value_slots"), NSLOT)

            cached = S[:, :, 0:512].rearrange("p b (n k) -> p b n k", n=NB)
            def st(k, n=NSEQ * NB):
                return stat[:, k:k + n]
            gpart, gate, pen, bmax = st(0), st(64), st(128), st(192)
            rmax, lane4, omax, shift = st(256, 8), st(264, 32), st(296, 8), st(304, 8)
            rden, total = st(312, 8), st(320, 8)
            bn = "p (b n) -> p b n"
            dve.wait_ge(sem("scores_out"), NSEQ + 2)
            dve.tensor_reduce(gpart.rearrange(bn, b=NSEQ), cached, AX, ALU.add).then_inc(sem("gate_parts"), 1)
            dve.tensor_reduce(bmax.rearrange(bn, b=NSEQ), cached, AX, ALU.max)
            dve.tensor_reduce(omax, S[:, :, 512:SW], AX, ALU.max)
            dve.wait_ge(sem("gate_sum"), 1)
            link(dve.tensor_copy(gate, ps[:, 2, 0:64]))
            g3 = gate.rearrange(bn, b=NSEQ)
            g_m, g_n = over(g3, 2, NB), over(g3, 3, NB)
            dve.wait_ge(sem("k_stored"), 32)
            link(dve.tensor_tensor(cmp1[:, :, :, :], g_m, g_n, ALU.is_gt))
            link(dve.tensor_tensor(cmp2[:, :, :, :], g_m, g_n, ALU.is_equal))
            link(dve.tensor_tensor(cmp2[:, :, :, :], cmp2[:, :, :, :], over(C("tie").rearrange("p (n m) -> p n m", n=NB), 1, NSEQ), ALU.mult))
            link(dve.tensor_tensor(cmp1[:, :, :, :], cmp1[:, :, :, :], cmp2[:, :, :, :], ALU.add))
            link(dve.tensor_reduce(pen.rearrange(bn, b=NSEQ), cmp1[:, :, :, :], AX, ALU.add))
            link(dve.tensor_scalar(pen, pen, TOPK - 0.5, NEG, ALU.is_gt, ALU.mult))
            link(dve.tensor_tensor(bmax, bmax, pen, ALU.add))
            link(dve.tensor_reduce(rmax, bmax.rearrange(bn, b=NSEQ), AX, ALU.max))
            link(dve.tensor_tensor(rmax, rmax, omax, ALU.max))
            for a in range(4):
                ins = dve.tensor_copy(lane4[0:32, 8 * a:8 * a + 8], rmax[32 * a:32 * a + 32, :])
            link(ins)
            dve.tensor_reduce(rmax[0:32, :], lane4[0:32, :].rearrange("p (a b) -> p b a", a=4), AX, ALU.max).then_inc(sem("row_max"), 1)
            dve.wait_ge(sem("max_spread"), 1)
            link(dve.tensor_scalar(shift, ps[:, 2, 64:72], -1.0, None, ALU.mult))
            link(dve.tensor_tensor(pen.rearrange(bn, b=NSEQ), pen.rearrange(bn, b=NSEQ), over(shift, 2, NB), ALU.add))
            dve.tensor_tensor(cached, cached, over(pen.rearrange(bn, b=NSEQ), 3, 64), ALU.add)
            dve.tensor_tensor(S[:, :, 512:SW], S[:, :, 512:SW], over(shift, 2, 32), ALU.add).then_inc(sem("s_shifted"), 1)

            lb0, lb1 = cols[:, R_LB:R_LB + 4], cols[:, R_LB + 4:R_LB + 8]
            link(dve.tensor_tensor(lbt[:, 0, :], lb0, lb1, ALU.max))
            dve.tensor_tensor(lbt[:, 1, :], lb0, lbt[:, 0, :], ALU.subtract)
            dve.tensor_tensor(lbt[:, 2, :], lb1, lbt[:, 0, :], ALU.subtract).then_inc(sem("lb_arg"), 1)

            dve.wait_ge(sem("probs_sum"), 1)
            link(dve.reciprocal(rden, ps[:, 2, 128:136]))
            link(dve.tensor_tensor(S[:, :, :], S[:, :, :], over(rden, 2, SW), ALU.mult))
            dve.transpose(Pt[:, :, :, :], S[:, :, :]).then_inc(sem("probs_ready"), 1)

            dve.wait_ge(sem("lb_exp"), 1)
            link(dve.tensor_tensor(lbt[:, 3, :], lbt[:, 1, :], lbt[:, 2, :], ALU.add))
            link(dve.reciprocal(lbt[:, 3, :], lbt[:, 3, :]))
            link(dve.tensor_tensor(lbt[:, 4, :], lbt[:, 1, :], lbt[:, 3, :], ALU.mult))
            link(dve.tensor_scalar(lbt[:, 5, :], lbt[:, 4, :], -1.0, 1.0, ALU.mult, ALU.add))
            dve.wait_ge(sem("sig_f"), 1)
            for h in range(HH):
                ins = dve.tensor_scalar(proj[:, HF + h, :], proj[:, HF + h, :], lbt[:, 5, h:h + 1], lbt[:, 4, h:h + 1], ALU.mult, ALU.add)
            ins.then_inc(sem("f_ready"), 1)
            dve.wait_ge(sem("logf"), 1)
            kin, q = proj[:, HF:HF + 4, :], proj[:, HQ:HQ + 4, :]
            dve.tensor_scalar(kin, kin, -1.0, 1.0, ALU.mult, ALU.add)
            dve.wait_ge(sem("lvl_ready"), 1)
            for h in range(HH):
                ins = dve.tensor_tensor_scan(hb[:, h, :], C("carry"), hkt[:, h, :], 0.0, ALU.mult, ALU.add)
            ins.then_inc(sem("b_ready"), 1)
            dve.wait_ge(sem("b_ready"), 1)
            bp, bs = hb[:, :, 0:TP].rearrange("p h (n k) -> p h n k", k=P), hb[:, :, SAMP].rearrange("p h (n k) -> p h n k", k=TS)
            kp, ks = hkt[:, :, 0:TP].rearrange("p h (n k) -> p h n k", k=P), hkt[:, :, SAMP].rearrange("p h (n k) -> p h n k", k=TS)
            dve.tensor_tensor(kp, bp[:, :, :, P - 1:P].broadcast_to([P, HH, 2, P]), bp, ALU.subtract)
            dve.tensor_tensor(ks, bs[:, :, :, TS - 1:TS].broadcast_to([P, HH, NSEQ, TS]), bs, ALU.subtract).then_inc(sem("kd_ready"), 1)

            def diff(li):
                m, x = LEVELS[li], hx[li % 2]
                r = TP if m > 2 else T
                bv = hb[:, :, 0:r].rearrange("p h (n k) -> p h n k", k=2 * m)
                xv = x[:, :, 0:r].rearrange("p h (n k) -> p h n k", k=2 * m)
                mid = bv[:, :, :, m - 1:m].broadcast_to([P, HH, r // (2 * m), m])
                if li >= 2:
                    dve.wait_ge(sem("gram_done"), li)
                dve.tensor_tensor(xv[:, :, :, m:2 * m], bv[:, :, :, m:2 * m], mid, ALU.subtract)
                dve.tensor_tensor(xv[:, :, :, 0:m], mid, bv[:, :, :, 0:m], ALU.subtract).then_inc(sem("lv_diff"), 1)

            def scale_level(li):
                m, x = LEVELS[li], hx[li % 2]
                r = TP if m > 2 else T
                dve.wait_ge(sem("lv_exp"), li + 1)
                for half, src in ((1, q), (0, kin)):
                    sv = src[:, :, 0:r].rearrange("p h (n k) -> p h n k", k=2 * m)[:, :, :, half * m:half * m + m]
                    xv = x[:, :, 0:r].rearrange("p h (n k) -> p h n k", k=2 * m)[:, :, :, half * m:half * m + m]
                    ins = dve.tensor_tensor(xv, xv, sv, ALU.mult)
                ins.then_inc(sem("lv_ready"), 1)

            def keep(gi):
                dve.wait_ge(sem("gram_done"), gi + 1)
                if gi:
                    dve.wait_ge(sem("kept"), gi)
                li = gi - 1
                mask = lvl[:, 7 if gi == 0 else li, :]
                b0 = 2 + 2 * (gi % 2)
                ins = dve.copy_predicated(hA[:, :, :, :].rearrange("p t h s -> p (t h) s"), over(mask, 1, 2 * HH),
                                          ps[:, b0:b0 + 2, :].rearrange("p t (h s) -> p (t h) s", h=HH))
                if gi == 0 or LEVELS[li] <= 2:
                    link(ins)
                    ins = dve.copy_predicated(hAs[:, :, :], over(mask[0:TSA, 0:TSA], 1, HH),
                                              ps[0:TSA, 6 + gi % 2, 0:HH * TSA].rearrange("p (h s) -> p h s", h=HH))
                ins.then_inc(sem("kept"), 1)

            dve.wait_ge(sem("eb"), 1)
            dve.wait_ge(sem("probs_ready"), 1)
            dve.memset(hA[:, :, :, :], 0.0)
            link(dve.memset(hAs[:, :, :], 0.0))
            dve.tensor_copy(stat[:, 328:332], hqt[:, :, TP - 1])
            link(dve.tensor_copy(stat[:, 332:332 + HH * NSEQ].rearrange("p (h b) -> p h b", h=HH),
                                 hqt[:, :, SAMP].rearrange("p h (b t) -> p h b t", t=TS)[:, :, :, TS - 1]))
            dve.tensor_tensor(hqt[:, :, :], hqt[:, :, :], q, ALU.mult).then_inc(sem("qt_ready"), 1)
            diff(0)
            dve.wait_ge(sem("ekd"), 1)
            dve.tensor_tensor(hkt[:, :, :], hkt[:, :, :], kin, ALU.mult).then_inc(sem("kt_ready"), 1)
            diff(1)
            for li in range(7):
                scale_level(li)
                keep(li)
                if li + 2 < 7:
                    diff(li + 2)
            keep(7)
            for h in range(HH):
                dve.wait_ge(sem("h_tok"), 1)
                if h >= 1:
                    dve.wait_ge(sem("ds_done"), h)
                dve.tensor_tensor(vms[:, :, :], over(hvs[:, h, :], 1, NSEQ), over(C("seq", TSA), 2, DK), ALU.mult).then_inc(sem("vm_ready"), 1)
                if h == 0:
                    dve.wait_ge(sem("s0_landed"), 64)
                    dve.wait_ge(sem("o_done"), 1)
                eb = over(stat[:, 332 + NSEQ * h:332 + NSEQ * (h + 1)], 2, DK)
                link(dve.tensor_tensor(S0[:, :, h, :], S0[:, :, h, :], eb, ALU.mult))
                dve.wait_ge(sem("ds_done"), h + 1)
                dve.tensor_tensor(S0[:, :, h, :], S0[:, :, h, :], ps[:, 2:4, :].rearrange("p t (b e) -> p (t b) e", e=DK), ALU.add).then_inc(sem("state_s"), 1)
                if h == 0:
                    for hh in range(HH):
                        ins = dve.scalar_tensor_tensor(Sfin[:, hh, :], D0[:, hh, :], stat[:, 328 + hh:329 + hh], ps[:, 7, hh * DK:(hh + 1) * DK], ALU.mult, ALU.add)
                    ins.then_inc(sem("state_p"), 1)
            dve.wait_ge(sem("o_root"), 1)
            link(dve.reciprocal(hx[1][:, :, :], hx[1][:, :, :]))
            link(dve.tensor_tensor(hb[:, :, :], hb[:, :, :], hx[1][:, :, :], ALU.mult))
            dve.wait_ge(sem("silu_g"), 1)
            dve.scalar_tensor_tensor(proj[:, HQ:HQ + 4, :], hb[:, :, :], cols[:, R_ON:R_ON + 1], proj[:, HG:HG + 4, :], ALU.mult, ALU.mult).then_inc(sem("oa_ready"), 1)

            def sample_out(g):
                dve.wait_ge(sem("v_summed"), g + 1)
                dve.tensor_tensor(om[:, :, :], ps[:, g, :].rearrange("p (h d) -> p h d", h=AH), over(C("ownhead"), 2, DH), ALU.mult).then_inc(sem("om_ready"), 1)
                dve.wait_ge(sem("ob_turned"), g + 1)
                dve.tensor_copy(proj[:, AQ:AQ + 4, TP + 16 * g:TP + 16 * g + 16], ps[:, 7, 0:64].rearrange("p (a t) -> p a t", a=PAIRS)).then_inc(sem("ob_s"), 1)

            sample_out(0)
            sample_out(1)

            def pa_mask(h):
                bank = 2 + h % 4
                if h >= 2:
                    dve.wait_ge(sem("pa_turned"), h - 1)
                dve.wait_ge(sem("pa_scored"), h + 1)
                dve.tensor_tensor(pa[:, h % 2, 0:P], ps[:, bank, 0:P], C("causal"), ALU.add)
                dve.tensor_copy(pa[:, h % 2, P:2 * P], ps[:, bank, P:2 * P])
                link(dve.tensor_tensor(pa[:, h % 2, 2 * P:3 * P], ps[:, bank, 2 * P:3 * P], C("causal"), ALU.add))
                dve.tensor_reduce(nmx[:, h % 2, 0:1], pa[:, h % 2, 0:P], AX, ALU.max, negate=True)
                dve.tensor_reduce(nmx[:, h % 2, 1:2], pa[:, h % 2, P:3 * P], AX, ALU.max, negate=True).then_inc(sem("pa_masked"), 1)

            def pa_norm(h):
                dve.wait_ge(sem("pa_exp"), h + 1)
                link(dve.reciprocal(den[:, h % 2, :], den[:, h % 2, :]))
                dve.tensor_scalar(pa[:, h % 2, 0:P], pa[:, h % 2, 0:P], den[:, h % 2, 0:1], None, ALU.mult)
                dve.tensor_scalar(pa[:, h % 2, P:3 * P], pa[:, h % 2, P:3 * P], den[:, h % 2, 1:2], None, ALU.mult).then_inc(sem("pa_ready"), 1)

            dve.wait_ge(sem("v_tok"), 1)
            for h in range(AH):
                pa_mask(h)
                if h >= 1:
                    pa_norm(h - 1)
            pa_norm(AH - 1)

            dve.wait_ge(sem("oab_hi"), 1)
            dve.tensor_tensor(oa_lo[:, :, :], proj[:, HQ:HQ + 4, :], oa_hi[:, :, :].bitcast(F32), ALU.subtract).then_inc(sem("oab_lo"), 1)
            dve.wait_ge(sem("oab_hi"), 2)
            dve.tensor_tensor(ob_lo[:, :, :], proj[:, AQ:AQ + 4, :], ob_hi[:, :, :].bitcast(F32), ALU.subtract).then_inc(sem("oab_lo"), 1)

            def lo_b(w, rows=BK):
                lo(w, (w + 64) % NSLOT, w % 2, rows)

            def merge(cg):
                ua, ub = proj[:, UA + 4 * cg:UA + 4 * cg + 4, :], proj[:, UB + 4 * cg:UB + 4 * cg + 4, :]
                dve.wait_ge(sem("w_used"), 46 + 2 * cg + 2)
                dve.tensor_tensor(ua, ps[:, 0:4, 0:T], ua, ALU.mult)
                link(dve.tensor_tensor(ub, ps[:, 4:8, 0:T], ub, ALU.mult))
                dve.tensor_tensor(ua, ua, ub, ALU.add).then_inc(sem("merged"), 1)
                dve.wait_ge(sem("m_hi"), cg + 1)
                dve.tensor_tensor(m_lo[:, 4 * cg:4 * cg + 4, :], ua, m_hi[:, 4 * cg:4 * cg + 4, :].bitcast(F32), ALU.subtract).then_inc(sem("m_lo"), 1)

            def y1_squares(cg):
                dve.wait_ge(sem("y1_out"), 4 * cg + 4)
                y = proj[:, 4 * cg:4 * cg + 4, :]
                dve.tensor_tensor(proj[:, 8 + 4 * cg:12 + 4 * cg, :], y, y, ALU.mult).then_inc(sem("y1_sq"), 1)

            dve.wait_ge(sem("sig_u"), 1)
            lo_b(46)
            lo_b(47)
            lo_b(48)
            merge(0)
            lo_b(49)
            lo_b(50)
            merge(1)
            lo_b(51)
            lo_b(52)
            y1_squares(0)
            lo_b(53)
            lo_b(54)
            y1_squares(1)
            lo_b(55)
            dve.wait_ge(sem("root"), 2)
            link(dve.reciprocal(rs[:, :], rs[:, :]))
            link(dve.tensor_tensor(gain[:, :, :], part(2), over(cols[:, R_POST1:R_POST1 + DT], 2, CC), ALU.mult))
            link(dve.tensor_tensor(proj[:, 8:16, :], proj[:, 0:8, :], over(rs[:, :], 1, DT), ALU.mult))
            scaled(xT, proj[:, 8:16, :], gain, None, xT).then_inc(sem("x1_ready"), 1)
            link(dve.scalar_tensor_tensor(gain[:, :, :], part(4), 1.0, over(cols[:, R_PRE2:R_PRE2 + DT], 2, CC), ALU.add, ALU.mult))
            dve.wait_ge(sem("root"), 3)
            link(dve.reciprocal(rs[:, :], rs[:, :]))
            link(dve.tensor_tensor(sq[:, :, :], xT[:, :, :], over(rs[:, :], 1, DT), ALU.mult))
            scaled(h32, sq, gain, part(3), None).then_inc(sem("h_ready"), 1)
            dve.wait_ge(sem("h_hi"), 2)
            dve.tensor_tensor(h_lo[:, :, :], h32[:, :, :], h_hi[:, :, :].bitcast(F32), ALU.subtract).then_inc(sem("h_lo"), 1)

            def product(g, base):
                dve.wait_ge(sem("silu_done"), g + 1)
                dve.wait_ge(sem("w_used"), g * 2 + 56)
                dve.wait_ge(sem("f_lo"), g + 1)
                dve.tensor_tensor(fu[:, :, :], ps[:, base + 2:base + 4, 0:T], fa[:, :, :], ALU.mult).then_inc(sem("fu_ready"), 1)

            def f_lower(g):
                dve.wait_ge(sem("f_hi"), g + 1)
                dve.tensor_tensor(f_lo[:, bass.ds(g * 2, 2), :], fu[:, :, :], f_hi[:, bass.ds(g * 2, 2), :].bitcast(F32), ALU.subtract).then_inc(sem("f_lo"), 1)

            dve.nop().then_inc(sem("fu_ready"), 1)
            dve.nop().then_inc(sem("f_lo"), 1)
            with dve.Fori(0, 5) as i:
                lo(i * 4 + 56, 0, 0)
                product(i * 2, 0)
                lo(i * 4 + 57, 1, 1)
                f_lower(i * 2)
                lo(i * 4 + 58, 2, 0)
                product(i * 2 + 1, 4)
                lo(i * 4 + 59, 3, 1)
                f_lower(i * 2 + 1)

            def y2_squares(cg):
                dve.wait_ge(sem("y2_out"), 4 * cg + 4)
                y = y2[:, 4 * cg:4 * cg + 4, :]
                dve.tensor_tensor(sq[:, 4 * cg:4 * cg + 4, :], y, y, ALU.mult).then_inc(sem("y2_sq"), 1)

            def lo_d(i):
                lo_b(76 + i, 2 if i % 6 == 5 else BK)

            lo_d(0)
            product(10, 0)
            lo_d(1)
            f_lower(10)
            for i in range(2, 7):
                lo_d(i)
            lo_d(7)
            y2_squares(0)
            for i in range(8, 12):
                lo_d(i)
            y2_squares(1)
            link(dve.tensor_tensor(gain[:, :, :], part(5), over(cols[:, R_POST2:R_POST2 + DT], 2, CC), ALU.mult))
            dve.wait_ge(sem("root"), 4)
            link(dve.reciprocal(rs[:, :], rs[:, :]))
            link(dve.tensor_tensor(y2[:, :, :], y2[:, :, :], over(rs[:, :], 1, DT), ALU.mult))
            scaled(xT, y2, gain, None, xT).then_inc(sem("x2_ready"), 1)

        @block.tensor
        def _(pe):
            def three(dst, w, kt, lhs, x_hi, x_lo, first, last):
                h, l = lhs
                pe.matmul(dst, h, x_hi, start=first, stop=False)
                pe.matmul(dst, h, x_lo, start=False, stop=False)
                return pe.matmul(dst, l, x_hi, start=False, stop=last)

            def ada(w, par, k, g=None):
                pe.wait_ge(sem("lo_split"), w + 1)
                if k == 0 and g is not None:
                    pe.wait_ge(sem("ada_rows"), g)
                for kt in range(BK):
                    c = k * BK + kt
                    pe.matmul(ps[0:2 * CC, 4, :], cst[:, c, :], w_hi[:, par, kt, :], start=c == 0, stop=False)
                    ins = pe.matmul(ps[0:2 * CC, 4, :], cst[:, c, :], w_lo[:, par, kt, :], start=False, stop=c == DT - 1)
                ins.then_inc(sem("w_used"), 1)

            def turn_ada(g):
                pe.wait_ge(sem("ada_rows"), g + 1)
                if not isinstance(g, int) or g >= 1:
                    pe.wait_ge(sem("mod_ready"), g)
                for j in range(4):
                    ins = pe.matmul(ps[:, 5, j * CC:(j + 1) * CC], arow[:, j * P:(j + 1) * P], C("foldc", 2 * CC), start=True, stop=True)
                ins.then_inc(sem("mod_rows_turned"), 1)

            def dense(w, par, x_hi, x_lo, kts, first, last, done, bank0=0, free=None, rows=BK):
                pe.wait_ge(sem("lo_split"), w + 1)
                for j in range(4):
                    if free is not None:
                        pe.wait_ge(sem(free[0]), free[1] + (j + 1 if len(free) == 2 else free[2][j]))
                    for kt in range(rows):
                        ins = three(ps[:, bank0 + j, 0:T], None, None, (w_hi[:, par, kt, j * P:(j + 1) * P], w_lo[:, par, kt, j * P:(j + 1) * P]),
                                    x_hi[:, kts + kt, :], x_lo[:, kts + kt, :], first and kt == 0, last and kt == rows - 1)
                    if j == 3:
                        ins.then_inc(sem("w_used"), 1)
                    elif last:
                        ins.then_inc(sem(done), 1)

            pe.wait_ge(sem("const0_landed"), 16)
            pe.wait_ge(sem("par_landed"), 112)
            pe.transpose(ps[:, 6, 0:R_ALL], prow[0:R_ALL, :], C("ident", R_ALL)[:, 0:R_ALL]).then_inc(sem("rows_turned"), 1)
            pe.wait_ge(sem("c_landed"), 32)
            for k in range(DT):
                ins = pe.transpose(ps[:, 7, k * CC:(k + 1) * CC], crow[:, k * P:(k + 1) * P], C("ident", CC)[:, 0:CC])
            ins.then_inc(sem("rows_turned"), 1)
            pe.wait_ge(sem("c_lo"), 1)
            ada(0, 0, 0)
            ada(1, 1, 1)
            pe.wait_ge(sem("x_landed"), 32)
            for k in range(DT):
                if k >= 4:
                    pe.wait_ge(sem("x_ready"), k - 3)
                for tt in range(3):
                    rows = P if tt < 2 else TSA
                    ins = pe.transpose(ps[:, k % 4, tt * P:tt * P + rows], xtok[0:rows, tt, k * P:(k + 1) * P], C("ident", rows)[:, 0:rows])
                ins.then_inc(sem("x_turned"), 1)
            for g in range(1, 4):
                ada(2 * g, 0, 0, g)
                turn_ada(g - 1)
                ada(2 * g + 1, 1, 1)
                if g == 1:
                    pe.wait_ge(sem("x_sq"), 1)
                    for k in range(DT):
                        ins = pe.matmul(ps[:, 7, 0:T], ones, sq[:, k, :], start=k == 0, stop=k == DT - 1)
                    ins.then_inc(sem("x_sum"), 1)
            turn_ada(3)
            pe.wait_ge(sem("h_lo"), 1)
            dense(8, 0, h_hi, h_lo, 0, True, False, "tile_done")
            dense(9, 1, h_hi, h_lo, 4, False, True, "tile_done")
            with pe.Fori(0, 7) as i:
                ada(i * 4 + 10, 0, 0, i + 4)
                ada(i * 4 + 11, 1, 1)
                dense(i * 4 + 12, 0, h_hi, h_lo, 0, True, False, "tile_done", free=("tile_out", i * 4))
                turn_ada(i + 4)
                dense(i * 4 + 13, 1, h_hi, h_lo, 4, False, True, "tile_done")
            ada(38, 0, 0, 11)
            ada(39, 1, 1)
            dense(40, 0, h_hi, h_lo, 0, True, False, "tile_done", free=("tile_out", 28))
            turn_ada(11)
            dense(41, 1, h_hi, h_lo, 4, False, True, "tile_done")
            for g in (9, 10):
                dense(24 + 2 * g, 0, h_hi, h_lo, 0, True, False, "tile_done", free=("tile_out", 4 * g - 4))
                dense(25 + 2 * g, 1, h_hi, h_lo, 4, False, True, "tile_done")

            pe.wait_ge(sem("tile_out"), 44)
            pe.wait_ge(sem("mod_ready"), 12)
            pe.wait_ge(sem("const1_landed"), 16)
            for j, t0 in enumerate((AQ, AK)):
                for k in range(4):
                    ins = pe.matmul(ps[:, 4 * j + k, 0:T], C("swap"), proj[:, t0 + k, :], start=True, stop=True)
                ins.then_inc(sem("swapped"), 1)
            pe.wait_ge(sem("swap_used"), 1)
            for tt in range(3):
                rows = P if tt < 2 else TSA
                for a in range(PAIRS):
                    ins = pe.transpose(ps[0:rows, tt, a * P:(a + 1) * P], proj[:, AV + a, tt * P:tt * P + rows], ident)
            ins.then_inc(sem("v_turned"), 1)
            pe.wait_ge(sem("roped"), 1)
            for s in range(4):
                ins = pe.matmul(ps[:, 3, s * P:(s + 1) * P], C(f"spread{s}"), proj[:, AQ:AQ + 4, SAMP], start=True, stop=True)
            ins.then_inc(sem("spread_done"), 1)
            pe.wait_ge(sem("roped"), 2)
            for tt in range(3):
                rows = P if tt < 2 else TSA
                for a in range(PAIRS):
                    ins = pe.transpose(ps[0:rows, 4 + tt, a * P:(a + 1) * P], proj[:, AK + a, tt * P:tt * P + rows], ident)
            ins.then_inc(sem("k_turned_tok"), 1)
            pe.wait_ge(sem("q_blocks"), 1)
            for b in range(NSEQ):
                for a in range(PAIRS):
                    ins = pe.matmul(ps[0:32, 7, b * TSA:(b + 1) * TSA], Qbd[:, a, b, :], proj[:, AK + a, SAMP], start=a == 0, stop=a == PAIRS - 1)
            ins.then_inc(sem("own_scored"), 1)

            pe.wait_ge(sem("v_tok"), 1)
            pe.nop().then_inc(sem("kt_used"), 3)
            with pe.Fori(0, NSEQ // 2) as i:
                for bb in range(2):
                    pe.wait_ge(sem("wq_ready"), i * 2 + (bb + 1))
                    pe.wait_ge(sem("scores_out"), i * 2 + (bb + 1))
                    for half in range(2):
                        pe.wait_ge(sem("key_slots"), i * 8 + (4 * bb + 2 * half + 2 + NSLOT))
                        for c in range(16):
                            ins = pe.matmul(ps[:, bb, half * 256:(half + 1) * 256], Wq[:, bb, c, :], KT[:, half, :, c * 32:(c + 1) * 32],
                                            start=c == 0, stop=c == 15)
                        ins.then_inc(sem("kt_used"), 1)

            pe.wait_ge(sem("gate_parts"), 1)
            pe.matmul(ps[:, 2, 0:64], fold, stat[:, 0:64], start=True, stop=True).then_inc(sem("gate_sum"), 1)
            pe.wait_ge(sem("row_max"), 1)
            pe.matmul(ps[:, 2, 64:72], fold[0:32, :], stat[0:32, 256:264], start=True, stop=True).then_inc(sem("max_spread"), 1)
            pe.wait_ge(sem("s_exp"), NSEQ)
            pe.matmul(ps[:, 2, 128:136], fold, stat[:, 320:328], start=True, stop=True).then_inc(sem("probs_sum"), 1)

            def values(b):
                rows = slice(32 * (b % 4), 32 * (b % 4) + 32)
                for j in range(4):
                    pe.wait_ge(sem(f"v_landed{j}"), 64 * (b + 1))
                    for q in range(4):
                        ins = pe.matmul(ps[rows, b // 4, :], Pt[:, b, 4 * j + q, :], ring[:, KV_SLOT[j], q * 512:(q + 1) * 512],
                                        start=j + q == 0, stop=False)
                    ins.then_inc(sem("value_slots"), 1)
                ins = pe.matmul(ps[rows, b // 4, :], Pt[0:32, b, 16, :], vtok[0:32, 2, :], start=False, stop=True)
                if b % 4 == 3:
                    ins.then_inc(sem("v_summed"), 1)

            def turn_hgrn():
                pe.wait_ge(sem("kt_ready"), 1)
                for x, b0 in ((hkt, 2), (proj[:, HI:HI + 4, :], 4)):
                    for tt in range(3):
                        rows = P if tt < 2 else TSA
                        bank = b0 + tt if tt < 2 else 6 + (b0 // 4)
                        for h in range(HH):
                            ins = pe.transpose(ps[0:rows, bank, h * P:(h + 1) * P], x[:, h, tt * P:tt * P + rows], ident)
                ins.then_inc(sem("h_turned"), 1)

            def gram(gi):
                li = gi - 1
                if gi == 0:
                    pe.wait_ge(sem("h_tok"), 1)
                else:
                    pe.wait_ge(sem("lv_ready"), li + 1)
                if gi >= 2:
                    pe.wait_ge(sem("kept"), gi - 1)
                left, right = (proj[:, HF:HF + 4, :], proj[:, HQ:HQ + 4, :]) if gi == 0 else (hx[li % 2], hx[li % 2])
                for tt in range(2):
                    for h in range(HH):
                        ins = pe.matmul(ps[:, 2 + 2 * (gi % 2) + tt, h * P:(h + 1) * P], left[:, h, tt * P:(tt + 1) * P], right[:, h, tt * P:(tt + 1) * P], start=True, stop=True)
                if gi == 0 or LEVELS[li] <= 2:
                    for h in range(HH):
                        ins = pe.matmul(ps[0:TSA, 6 + gi % 2, h * TSA:(h + 1) * TSA], left[:, h, SAMP], right[:, h, SAMP], start=True, stop=True)
                ins.then_inc(sem("gram_done"), 1)

            def hgrn_states():
                pe.wait_ge(sem("kept"), 8)
                for tt, bank in ((0, 2), (1, 7)):
                    for h in range(HH):
                        ins = pe.matmul(ps[:, bank, h * DK:(h + 1) * DK], hktok[:, tt, h, :], hvtok[:, tt, h, :], start=True, stop=True)
                ins.then_inc(sem("d_done"), 1)

            def hgrn_out():
                pe.wait_ge(sem("d0_ready"), 1)
                pe.wait_ge(sem("qt_ready"), 1)
                pe.wait_ge(sem("s0_landed"), 64)
                for h in range(HH):
                    for tt in range(2):
                        dst = ps[:, 4 + tt, h * P:(h + 1) * P]
                        pe.matmul(dst, hvtok[:, tt, h, :], hA[:, tt, h, :], start=True, stop=tt == 0)
                        if tt:
                            pe.matmul(dst, D0[:, h, :], hqt[:, h, P:TP], start=False, stop=True)
                    pe.matmul(ps[:, 6, h * TSA:(h + 1) * TSA], hvs[:, h, :], hAs[:, h, :], start=True, stop=False, skip_group_check=True)
                    for b in range(NSEQ):
                        c = h * TSA + b * TS
                        ins = pe.matmul(ps[:, 6, c:c + TS], S0[:, b, h, :], hqt[:, h, TP + b * TS:TP + (b + 1) * TS], start=False, stop=b == NSEQ - 1, skip_group_check=True)
                ins.then_inc(sem("o_done"), 1)

            def sample_states(h):
                pe.wait_ge(sem("vm_ready"), h + 1)
                if h >= 1:
                    pe.wait_ge(sem("state_s"), h)
                for g in range(2):
                    ins = pe.matmul(ps[:, 2 + g, :], hks[:, h, :], vms[:, 4 * g:4 * g + 4, :], start=True, stop=True)
                ins.then_inc(sem("ds_done"), 1)

            def o_sum():
                pe.wait_ge(sem("o_sq"), 1)
                for tt in range(3):
                    n = P if tt < 2 else TSA
                    ins = pe.matmul(ps[:, 4 + tt, 0:HH * n], ones, hx[0][:, :, tt * P:tt * P + n], start=True, stop=True)
                ins.then_inc(sem("o_sum"), 1)

            def sample_out(g):
                pe.wait_ge(sem("om_ready"), g + 1)
                if g:
                    pe.wait_ge(sem("ob_s"), 1)
                else:
                    pe.wait_ge(sem("state_p"), 1)
                for a in range(PAIRS):
                    ins = pe.matmul(ps[:, 7, a * 16:(a + 1) * 16], om[:, 2 * a:2 * a + 2, :], C("sumheads"), start=True, stop=True)
                ins.then_inc(sem("ob_turned"), 1)

            pe.wait_ge(sem("probs_ready"), 1)
            values(0)
            turn_hgrn()
            gram(0)
            values(1)
            gram(1)
            gram(2)
            values(2)
            gram(3)
            gram(4)
            values(3)
            gram(5)
            gram(6)
            values(4)
            gram(7)
            hgrn_states()
            values(5)
            hgrn_out()
            sample_states(0)
            values(6)
            for h in range(1, HH):
                sample_states(h)
            values(7)
            o_sum()
            sample_out(0)
            sample_out(1)

            def pa_scores(h):
                rows = slice(64 * (h % 2), 64 * (h % 2) + 64)
                bank = 2 + h % 4
                if h >= 4:
                    pe.wait_ge(sem("pa_masked"), h - 3)
                qt, kt = proj[rows, AQ + h // 2, :], proj[rows, AK + h // 2, :]
                pe.matmul(ps[:, bank, 0:P], qt[:, 0:P], kt[:, 0:P], start=True, stop=True)
                pe.matmul(ps[:, bank, P:3 * P], qt[:, P:TP], kt[:, 0:TP], start=True, stop=True).then_inc(sem("pa_scored"), 1)

            def pa_turn(h):
                pe.wait_ge(sem("pa_ready"), h + 1)
                if h >= 2:
                    pe.wait_ge(sem("paT_ready"), h - 1)
                for c in range(3):
                    ins = pe.transpose(ps[:, 6 + h % 2, c * P:(c + 1) * P], pa[:, h % 2, c * P:(c + 1) * P], ident)
                ins.then_inc(sem("pa_turned"), 1)

            def pa_values(h):
                pe.wait_ge(sem("paT_ready"), h + 1)
                if h >= 4 and h % 2 == 0:
                    pe.wait_ge(sem("ob_p"), h // 2 - 1)
                rows = slice(64 * (h % 2), 64 * (h % 2) + 64)
                bank = (h // 2) % 2
                v = lambda tt: vtok[:, tt, h * DH:(h + 1) * DH]
                pe.matmul(ps[rows, bank, 0:P], v(0), paT[:, 0:P], start=True, stop=True)
                pe.matmul(ps[rows, bank, P:TP], v(0), paT[:, P:2 * P], start=True, stop=False)
                pe.matmul(ps[rows, bank, P:TP], v(1), paT[:, 2 * P:3 * P], start=False, stop=True).then_inc(sem("pv_done"), 1)

            pe.wait_ge(sem("ob_s"), 2)
            pe.wait_ge(sem("state_s"), HH)
            pe.wait_ge(sem("o_root"), 1)
            pa_scores(0)
            pa_scores(1)
            for h in range(AH):
                if h + 2 < AH:
                    pa_scores(h + 2)
                pa_turn(h)
                if h >= 1:
                    pa_values(h - 1)
            pa_values(AH - 1)

            for cg in range(2):
                for j, (x_hi, x_lo) in enumerate(((oa_hi, oa_lo), (ob_hi, ob_lo))):
                    w = 46 + 2 * cg + j
                    if cg == 0:
                        pe.wait_ge(sem("oab_lo"), j + 1)
                        if j == 0:
                            pe.wait_ge(sem("ob_p"), PAIRS)
                    else:
                        pe.wait_ge(sem("merged"), 1)
                    dense(w, w % 2, x_hi, x_lo, 0, True, True, "ab_tiles", 4 * j)
            pe.wait_ge(sem("merged"), 2)
            pe.wait_ge(sem("m_lo"), 2)

            def sum_squares(src, which, first, last, bank, done):
                for k in which:
                    ins = pe.matmul(ps[:, bank, 0:T], ones, src[:, k, :], start=k == first, stop=k == last)
                if which[-1] == last:
                    ins.then_inc(sem(done), 1)

            y1sq = proj[:, 8:16, :]
            dense(50, 0, m_hi, m_lo, 0, True, False, "y1_done")
            dense(51, 1, m_hi, m_lo, 4, False, True, "y1_done")
            dense(52, 0, m_hi, m_lo, 0, True, False, "y1_done", free=("y1_out", 0))
            pe.wait_ge(sem("y1_sq"), 1)
            sum_squares(y1sq, range(0, 4), 0, 7, 4, "y1_sum")
            dense(53, 1, m_hi, m_lo, 4, False, True, "y1_done")
            pe.wait_ge(sem("y1_sq"), 2)
            sum_squares(y1sq, range(4, 8), 0, 7, 4, "y1_sum")
            pe.wait_ge(sem("x1_sq"), 1)
            sum_squares(sq, range(0, 8), 0, 7, 5, "x1_sum")
            pe.wait_ge(sem("h_lo"), 2)

            pe.wait_ge(sem("y1_out"), 8)
            dense(54, 0, h_hi, h_lo, 0, True, False, "gu_done")
            dense(55, 1, h_hi, h_lo, 4, False, True, "gu_done")
            pe.wait_ge(sem("root"), 3)
            with pe.Fori(0, 5) as i:
                pe.wait_ge(sem("fu_ready"), i * 2 + 1)
                dense(i * 4 + 56, 0, h_hi, h_lo, 0, True, False, "gu_done", 4)
                dense(i * 4 + 57, 1, h_hi, h_lo, 4, False, True, "gu_done", 4)
                pe.wait_ge(sem("fu_ready"), i * 2 + 2)
                dense(i * 4 + 58, 0, h_hi, h_lo, 0, True, False, "gu_done")
                dense(i * 4 + 59, 1, h_hi, h_lo, 4, False, True, "gu_done")
            for cg in range(2):
                for c in range(6):
                    w = 76 + 6 * cg + c
                    if cg == 0:
                        pe.wait_ge(sem("f_lo"), min(2 * c + 3, 12))
                        if c == 0:
                            pe.wait_ge(sem("fu_ready"), 11)
                    elif c == 0:
                        pe.wait_ge(sem("fu_ready"), 12)
                    dense(w, w % 2, f_hi, f_lo, 4 * c, c == 0, c == 5, "y2_done", 4 * (1 - cg), rows=2 if c == 5 else BK)
                    if cg == 1 and c == 1:
                        pe.wait_ge(sem("y2_sq"), 1)
                        sum_squares(sq, range(0, 4), 0, 7, 4, "y2_sum")
            pe.wait_ge(sem("y2_sq"), 2)
            sum_squares(sq, range(4, 8), 0, 7, 4, "y2_sum")
            pe.wait_ge(sem("x2_ready"), 1)
            pe.wait_ge(sem("y2_out"), 8)
            pe.wait_ge(sem("root"), 4)
            for tt, b0 in ((0, 0), (1, 2), (2, 5)):
                rows = P if tt < 2 else TSA
                for k in range(DT):
                    ins = pe.transpose(ps[0:rows, b0 + k // 4, (k % 4) * P:(k % 4 + 1) * P], xT[:, k, tt * P:tt * P + rows], ident)
                ins.then_inc(sem("y_turned"), 1)


INPUTS = ["x_prompt", "x_sample", "c_prompt", "c_sample", "state_hgrn", "cache_k", "cache_v", "page_table", "hg_lb",
          "w_ada", "b_ada", "g_pre1", "g_post1", "w_in", "g_onorm", "w_proj_a", "w_proj_b", "w_out", "g_pre2", "g_post2",
          "w_gu", "w_down"]
OUTPUTS = {
    "y_prompt": (1, TP, D), "y_sample": (NSEQ, TS, D),
    "state_p": (1, 1, HH, DK, DK), "state_s": (1, NSEQ, HH, DK, DK),
    "k_prompt": (1, 1, TP, AH, DH), "v_prompt": (1, 1, TP, AH, DH),
    "k_sample": (1, NSEQ, TS, AH, DH), "v_sample": (1, NSEQ, TS, AH, DH),
}


def kernel(**inputs):
    import concourse.bacc as bacc
    from concourse.bass_utils import run_bass_kernel_spmd

    nc = bacc.Bacc("TRN2", target_bir_lowering=False, num_devices=1)
    arrays = {k: np.ascontiguousarray(inputs[k]) for k in INPUTS}
    arrays["cache_k"] = arrays["cache_k"].reshape(1, -1, PAGE, AH * DH)
    arrays["cache_v"] = arrays["cache_v"].reshape(1, -1, PAGE, AH * DH)
    arrays["const"] = constants()[0]
    arrays["lvl"] = level_masks()
    inp = {k: nc.dram_tensor(k, a.shape, mybir.dt.from_np(a.dtype), kind="ExternalInput").ap() for k, a in arrays.items()}
    out = {k: nc.dram_tensor("out_" + k, s, F32, kind="ExternalOutput").ap() for k, s in OUTPUTS.items()}
    build(nc, inp, out)
    r = run_bass_kernel_spmd(nc, [arrays], core_ids=[0]).results[0]
    return tuple(r["out_" + k] for k in OUTPUTS)
```

```python
from contextlib import ExitStack

import numpy as np
import concourse.bass as bass
from concourse import mybir

F32 = mybir.dt.float32
F32R = mybir.dt.float32r
I32 = mybir.dt.int32
U8 = mybir.dt.uint8
ALU = mybir.AluOpType
ACT = mybir.ActivationFunctionType
AX = mybir.AxisListType.X

P = 128
D = 1024
DT = D // P
TP = 256
NSEQ, TS = 8, 4
TSA = NSEQ * TS
T = TP + TSA
CC = 1 + NSEQ
HH, DK = 4, 128
AH, DH = 8, 64
PAIRS = AH // 2
PAST, PAGE = 2048, 128
NPG = PAST // PAGE
MB = 256
NB = PAST // MB
TOPK = 3
DFF = 2816
EPS = 1e-6
NEG = -1.0e30
INW = 5632
PT_ = INW // P
HQ, HF, HI, HG, AQ, AK, AV, UA, UB = 0, 4, 8, 12, 16, 20, 24, 28, 36
NSLOT = 4
BK = 4
BC = 512
KEYS = PAST + 32
SW = KEYS // 4 + 24
SW = 17 * 32
WQ = 17 * P
LEVELS = [64, 32, 16, 8, 4, 2, 1]

R_ADA, R_PRE1, R_POST1, R_PRE2, R_POST2, R_LB, R_ON, R_ALL = 0, 48, 56, 64, 72, 80, 88, 89


def constants():
    p = np.arange(P)
    c = {}
    c["ident"] = np.eye(P)
    c["foldc"] = np.zeros((P, CC))
    for i in range(2 * CC):
        c["foldc"][i, i % CC] = 1
    c["ones"] = np.ones((P, P))
    c["eps"] = np.full((P, 1), EPS)
    c["fold"] = (p[:, None] % 32 == p[None, :] % 32).astype(float)
    swap = np.zeros((P, P))
    swap[p ^ 32, p] = 1
    c["swap"] = swap
    for s in range(4):
        c[f"spread{s}"] = c["fold"] * (p[:, None] // 32 == s)
    half = DH // 2
    pos = np.concatenate([np.arange(TP), np.tile(PAST + np.arange(TS), NSEQ)]).astype(np.float32)
    inv = np.float32(10000.0) ** (-np.arange(half, dtype=np.float32) / np.float32(half))
    ang = pos[None, :] * inv[p % half][:, None]
    c["cos"] = np.cos(ang)
    c["sin"] = np.sin(ang) * np.where(p % DH < half, -1.0, 1.0)[:, None]
    start = np.ones(T)
    start[[0, P]] = 0
    start[TP::TS] = 0
    c["carry"] = np.tile(start, (P, 1))
    c["causal"] = np.where(p[None, :] <= p[:, None], 0.0, NEG)
    own = np.full((P, NSEQ, TSA), NEG)
    for r in range(32):
        for b in range(NSEQ):
            for k in range(r % TS + 1):
                own[r, b, b * TS + k] = 0
    c["own"] = own.reshape(P, -1)
    tie = (np.arange(NB)[None, :] < np.arange(NB)[:, None]).astype(float)
    c["tie"] = np.tile(tie.reshape(1, -1), (P, 1))
    c["ownhead"] = (p[:, None] % 32 // TS == np.arange(AH)[None, :]).astype(float)
    c["sumheads"] = ((p[:, None] // 32 == np.arange(16)[None, :] // TS) & (p[:, None] % TS == np.arange(16)[None, :] % TS)).astype(float)
    c["seq"] = (p[:, None] // TS == np.arange(NSEQ)[None, :]).astype(float)
    at, n = {}, 0
    c["pad"] = np.zeros((P, -sum(v.shape[1] for v in c.values()) % 8))
    for k, v in c.items():
        at[k] = (n, n + v.shape[1])
        n += v.shape[1]
    return np.concatenate(list(c.values()), 1).astype(np.float32), at


def level_masks():
    s, t = np.arange(P)[:, None], np.arange(P)[None, :]
    lv = [(s // (2 * m) == t // (2 * m)) & (s % (2 * m) < m) & (t % (2 * m) >= m) for m in LEVELS]
    return np.stack(lv + [s == t], 1).astype(np.int32)


def build(nc, inp, out):
    _, at = constants()
    NCONST = max(e for _, e in at.values())
    FIRST = at["eps"][1]

    base = (nc.sbuf_base + 31) // 32 * 32
    place = {}

    def sb(name, shape, dt=F32, over=None, off=0):
        nonlocal base
        size = int(np.prod(shape[1:])) * (1 if dt == U8 else 4)
        if over is None:
            o = base
            base += (size + 31) // 32 * 32
        else:
            o = place[over][0] + off
            assert off + size <= place[over][1], (name, off + size, place[over])
        place[name] = (o, size)
        return nc.alloc_sbuf_tensor_at(name, shape, dt, offset=o)

    const = sb("const", [P, NCONST])

    def C(name, rows=P):
        a, e = at[name]
        return const[0:rows, a:e]

    lvl = sb("lvl", [P, 8, P], U8)
    cols = sb("cols", [P, R_ALL])
    modT = sb("modT", [P, 48, CC])
    gain = sb("gain", [P, DT, CC])
    cst = sb("cst", [P, DT, 2 * CC], F32R)
    cs = sb("cs", [P, DT, CC])
    lbt = sb("lbt", [P, 6, HH])
    rs = sb("rs", [P, T])
    xT = sb("xT", [P, DT, T])
    stat = sb("stat", [P, 400])
    nmx = sb("nmx", [P, 2, 2])
    den = sb("den", [P, 2, 2])
    vtok = sb("vtok", [P, 3, AH * DH])
    pgt = sb("pgt", [1, NSEQ * NPG], I32)
    ring = sb("ring", [P, NSLOT, BK * BC])
    sb("split_area", [P, 4 * BK * BC])
    sb("proj_area", [P, PT_, T])
    sb("a_area", [P, 2, DT, T])
    sb("s_area", [P, 2, DT, T])
    hqt = sb("hqt", [P, HH, T])
    hA = sb("hA", [P, 2, HH, P])
    hAs = sb("hAs", [TSA, HH, TSA])
    sb("w_area", [P, 2, WQ])
    TB = T * 4

    w_hi = sb("w_hi", [P, 2, BK, BC], F32R, "split_area")
    w_lo = sb("w_lo", [P, 2, BK, BC], F32R, "split_area", 2 * BK * BC * 4)
    KT = sb("KT", [P, 2, 4, 512], F32, "split_area")
    proj = sb("proj", [P, PT_, T], F32, "proj_area")
    xtok = sb("xtok", [P, 3, D], F32, "proj_area")
    prow = sb("prow", [P, P], F32, "proj_area", 3 * D * 4)
    crow = sb("crow", [CC, D], F32, "proj_area", 3 * D * 4 + P * 4)
    h_hi = sb("h_hi", [P, DT, T], F32R, "a_area")
    h_lo = sb("h_lo", [P, DT, T], F32R, "a_area", DT * TB)
    h32 = sb("h32", [P, DT, T], F32, "s_area")
    sq = sb("sq", [P, DT, T], F32, "s_area", DT * TB)
    arow = sb("arow", [2 * CC, BC], F32, "w_area")
    lvl_i = sb("lvl_i", [P, 8, P], I32, "w_area", BC * 4)
    Qrep = sb("Qrep", [P, PAIRS, 4, TSA], F32, "a_area")
    Qbd = sb("Qbd", [P, PAIRS, NSEQ, 32], F32, "a_area", 2048)
    ktok = sb("ktok", [P, 3, AH * DH], F32, "a_area", 6144)
    cmp1 = sb("cmp1", [P, NSEQ, NB, NB], F32, "a_area", 6144)
    cmp2 = sb("cmp2", [P, NSEQ, NB, NB], F32, "a_area", 8192)
    S = sb("S", [P, NSEQ, SW], F32, "s_area")
    Wq = sb("Wq", [P, 2, WQ], F32, "w_area")
    Pt = sb("Pt", [P, NSEQ, SW // 32, 32], F32, "a_area")
    hb = sb("hb", [P, HH, T], F32, "split_area", 16384)
    hx = [sb(f"hx{i}", [P, HH, T], F32, "split_area", 16384 + (1 + i) * HH * TB) for i in range(2)]
    D0 = sb("D0", [P, HH, DK], F32, "split_area", 16384 + 3 * HH * TB)
    hkt = sb("hkt", [P, HH, T], F32, "proj_area", AV * TB)
    hktok = sb("hktok", [P, 2, HH, DK], F32, "a_area", 12288)
    hvtok = sb("hvtok", [P, 2, HH, DK], F32, "proj_area", HI * TB)
    hks = sb("hks", [TSA, HH, DK], F32, "proj_area", AV * TB)
    hvs = sb("hvs", [TSA, HH, DK], F32, "proj_area", AV * TB + 2048)
    S0 = sb("S0", [P, NSEQ, HH, DK], F32, "w_area")
    Sfin = sb("Sfin", [P, HH, DK], F32, "s_area", 2 * HH * TB)
    vms = sb("vms", [TSA, NSEQ, DK], F32, "s_area", 2 * HH * TB + 2048)
    om = sb("om", [P, AH, DH], F32, "s_area", 3 * HH * TB)
    pa = sb("pa", [P, 2, 384], F32, "proj_area", HF * TB)
    paT = sb("paT", [P, 384], F32, "proj_area", HF * TB + 3072)
    oa_hi = sb("oa_hi", [P, HH, T], F32R, "s_area")
    oa_lo = sb("oa_lo", [P, HH, T], F32R, "s_area", HH * TB)
    ob_hi = sb("ob_hi", [P, PAIRS, T], F32R, "s_area", 2 * HH * TB)
    ob_lo = sb("ob_lo", [P, PAIRS, T], F32R, "s_area", 3 * HH * TB)
    m_hi = sb("m_hi", [P, DT, T], F32R, "a_area")
    m_lo = sb("m_lo", [P, DT, T], F32R, "a_area", DT * TB)
    f_hi = sb("f_hi", [P, DFF // P, T], F32R, "proj_area")
    f_lo = sb("f_lo", [P, DFF // P, T], F32R, "proj_area", DFF // P * TB)
    y2 = sb("y2", [P, DT, T], F32, "w_area")
    fa = sb("fa", [P, 2, T], F32, "w_area", DT * TB)
    fu = sb("fu", [P, 2, T], F32, "w_area", DT * TB + 2 * TB)
    ytok = sb("ytok", [P, 3, D], F32, "s_area")
    assert base <= nc.sbuf_usable_end, base

    ps = nc.alloc_psum_tensor("ps", [P, 8, 512], F32)
    made = {}

    def sem(name):
        if name not in made:
            made[name] = nc.alloc_semaphore(name)
        return made[name]

    def over(ap, axis, n):
        a = ap.unsqueeze(axis)
        shape = list(a.shape)
        shape[axis] = n
        return a.broadcast_to(shape)

    ident, ones, fold = C("ident"), C("ones"), C("fold")
    pools = {k: inp[k] for k in ("cache_k", "cache_v")}
    AQK = PAIRS
    NA = 46
    SAMP = slice(TP, T)
    TURN = (6, 3)

    A_ORDER = [("ada", g) for g in range(4)] + [("in", 0)]
    for i in range(7):
        A_ORDER += [("ada", 4 + i), ("in", 1 + i)]
    A_ORDER += [("ada", 11), ("in", 8), ("in", 9), ("in", 10)]
    KV_SLOT = [(NA + j) % NSLOT for j in range(4)]
    B0 = NA + 64

    def w_src(name, row, col, rows=BK * P, width=BC):
        return inp[name][0, bass.ds(row, rows), bass.ds(col, width)].rearrange("(k p) n -> p k n", p=P)

    def slot4(s):
        return ring[:, s, :].rearrange("p (k n) -> p k n", n=BC)

    def load_pages(queue, pool, b, j, which, landed):
        for q in which:
            pg = queue.value_load(pgt[0:1, bass.ds(b * NPG + (4 * j + q), 1)], min_val=0, max_val=pools[pool].shape[1] - 1)
            queue.dma_start(ring[:, KV_SLOT[j], q * 512:(q + 1) * 512], pools[pool][0, bass.ds(pg, 1), :, :].rearrange("o p n -> p (o n)"))\
                .then_inc(sem(f"{landed}{j}"), 16)

    block = nc.Block()
    with block:

        @block.sync
        def _(sp):
            n = 0
            for kind, g in A_ORDER[:5]:
                for k in range(2):
                    if n >= NSLOT:
                        sp.wait_ge(sem("lo_split"), n - NSLOT + 1)
                    sp.dma_start(slot4(n % NSLOT), w_src("w_" + kind, k * BK * P, g * BC)).then_inc(sem(f"w_landed{n % NSLOT}"), 16)
                    n += 1
            with sp.Fori(0, 7) as i:
                for j, (kind, g0, k) in enumerate([("ada", 4, 0), ("ada", 4, 1), ("in", 1, 0), ("in", 1, 1)]):
                    s = (n + j) % NSLOT
                    sp.wait_ge(sem("lo_split"), i * 4 + (n + j - NSLOT + 1))
                    sp.dma_start(slot4(s), w_src("w_" + kind, k * BK * P, (i + g0) * BC)).then_inc(sem(f"w_landed{s}"), 16)
            n += 28
            for kind, g in A_ORDER[19:]:
                for k in range(2):
                    sp.wait_ge(sem("lo_split"), n - NSLOT + 1)
                    sp.dma_start(slot4(n % NSLOT), w_src("w_" + kind, k * BK * P, g * BC)).then_inc(sem(f"w_landed{n % NSLOT}"), 16)
                    n += 1
            assert n == NA

            sp.wait_ge(sem("table_landed"), 16)
            with sp.Fori(0, NSEQ) as b:
                for j in range(4):
                    sp.wait_ge(sem("key_slots"), b * 4 + (j + 1))
                    load_pages(sp, "cache_k", b, j, range(3), "k_landed")
            sp.wait_ge(sem("kt_used"), 4 * NSEQ)
            for g in range(4):
                sp.dma_start(S0[:, 2 * g:2 * g + 2], inp["state_hgrn"][0, 2 * g:2 * g + 2].rearrange("b h d e -> d b h e")).then_inc(sem("s0_landed"), 16)
            with sp.Fori(0, NSEQ) as b:
                for j in range(4):
                    sp.wait_ge(sem("value_slots"), b * 4 + (j + 1))
                    load_pages(sp, "cache_v", b, j, range(3), "v_landed")
            n = B0
            for cg in range(2):
                for name in ("w_proj_a", "w_proj_b"):
                    sp.wait_ge(sem("value_slots"), NSLOT + n - NSLOT - (NA + 32) + 1)
                    sp.dma_start(slot4(n % NSLOT), w_src(name, 0, cg * BC)).then_inc(sem(f"w_landed{n % NSLOT}"), 16)
                    n += 1
            for cg in range(2):
                for k in range(2):
                    sp.wait_ge(sem("lo_split"), n - NSLOT - 64 + 1)
                    sp.dma_start(slot4(n % NSLOT), w_src("w_out", k * BK * P, cg * BC)).then_inc(sem(f"w_landed{n % NSLOT}"), 16)
                    n += 1

            def load_gu(n_of, s, g, k):
                sp.wait_ge(sem("lo_split"), n_of)
                for half in range(2):
                    sp.dma_start(slot4(s)[:, :, half * 256:(half + 1) * 256], w_src("w_gu", k * BK * P, half * DFF + g * 256, width=256))\
                        .then_inc(sem(f"gu_landed{s}"), 16)

            for k in range(2):
                load_gu(n - NSLOT - 64 + 1, n % NSLOT, 0, k)
                n += 1
            with sp.Fori(0, 5) as i:
                for j in range(4):
                    load_gu(i * 4 + (n + j - NSLOT - 64 + 1), (n + j) % NSLOT, i * 2 + (1 + j // 2), j % 2)
            n += 20
            for cg in range(2):
                for c in range(6):
                    rows = min(BK, DFF // P - BK * c)
                    sp.wait_ge(sem("lo_split"), n - NSLOT - 64 + 1)
                    sp.dma_start(slot4(n % NSLOT)[:, 0:rows, :], w_src("w_down", c * BK * P, cg * BC, rows=rows * P))\
                        .then_inc(sem(f"w_landed{n % NSLOT}"), 16)
                    n += 1
            for tt in range(3):
                sp.wait_ge(sem("y_tok"), tt + 1)
                if tt < 2:
                    sp.dma_start(out["y_prompt"][0, tt * P:(tt + 1) * P, :], ytok[:, tt, :]).then_inc(sem("y_stored"), 16)
                else:
                    sp.dma_start(out["y_sample"].rearrange("b t d -> (b t) d"), ytok[0:TSA, 2, :]).then_inc(sem("y_stored"), 16)
            sp.wait_ge(sem("y_stored"), 48)

        @block.gpsimd
        def _(pool):
            pool.wait_ge(sem("lvl_landed"), 16)
            pool.tensor_copy(lvl[:, :, :], lvl_i[:, :, :]).then_inc(sem("lvl_ready"), 1)
            pool.wait_ge(sem("lvl_ready"), 1)
            pool.wait_ge(sem("mod_rows_turned"), 12)
            pool.memset(Wq[:, :, :], 0.0).then_inc(sem("wq_zero"), 1)
            pool.wait_ge(sem("wq_zero"), 1)
            pool.wait_ge(sem("v_tok"), 1)
            pool.dma_start(out["v_prompt"][0, 0].rearrange("(t p) h d -> p t (h d)", p=P), vtok[:, 0:2, :]).then_inc(sem("v_stored"), 16)
            pool.dma_start(out["v_sample"][0].rearrange("b t h d -> (b t) (h d)"), vtok[0:TSA, 2, :]).then_inc(sem("v_stored"), 16)

            def queries(b, levels=0):
                if b >= 2:
                    pool.wait_ge(sem("kt_used"), 4 * (b - 1))
                for a in range(4):
                    rows = slice(32 * a, 32 * a + 32)
                    step = 2 * P + TS
                    dst = Wq[rows, b % 2, a * 32:a * 32 + AH * step].rearrange("p (h x) -> p h x", x=step)[:, :, 0:2 * P]
                    if a == 0 and b >= 2:
                        pool.wait_ge(sem("lv_diff"), min(levels + 2, 7))
                        if levels:
                            pool.wait_ge(sem("lv_ready"), levels)
                    ins = pool.tensor_copy(dst.rearrange("p h (c y) -> p h c y", y=P)[:, :, :, 0:TS],
                                           Qrep[rows].rearrange("p a s t -> p (a s) t").rearrange("p (h c) t -> p h c t", c=2)[:, :, :, b * TS:(b + 1) * TS])
                ins.then_inc(sem("wq_ready"), 1)
                pool.wait_ge(sem("wq_ready"), b + 1)

            def diff(li):
                m, x = LEVELS[li], hx[li % 2]
                r = TP if m > 2 else T
                bv = hb[:, :, 0:r].rearrange("p h (n k) -> p h n k", k=2 * m)
                xv = x[:, :, 0:r].rearrange("p h (n k) -> p h n k", k=2 * m)
                mid = bv[:, :, :, m - 1:m].broadcast_to([P, HH, r // (2 * m), m])
                if li >= 2:
                    pool.wait_ge(sem("gram_done"), li)
                pool.tensor_tensor(xv[:, :, :, m:2 * m], bv[:, :, :, m:2 * m], mid, ALU.subtract)
                pool.tensor_tensor(xv[:, :, :, 0:m], mid, bv[:, :, :, 0:m], ALU.subtract).then_inc(sem("lv_diff"), 1)

            def scale_level(li):
                m, x = LEVELS[li], hx[li % 2]
                r = TP if m > 2 else T
                pool.wait_ge(sem("lv_exp"), li + 1)
                for half, src in ((1, proj[:, HQ:HQ + 4, :]), (0, proj[:, HF:HF + 4, :])):
                    sv = src[:, :, 0:r].rearrange("p h (n k) -> p h n k", k=2 * m)[:, :, :, half * m:half * m + m]
                    xv = x[:, :, 0:r].rearrange("p h (n k) -> p h n k", k=2 * m)[:, :, :, half * m:half * m + m]
                    ins = pool.tensor_tensor(xv, xv, sv, ALU.mult)
                ins.then_inc(sem("lv_ready"), 1)

            pool.wait_ge(sem("q_spread"), 1)
            queries(0)
            queries(1)
            pool.wait_ge(sem("b_ready"), 1)
            diff(0)
            diff(1)
            queries(2)
            pool.wait_ge(sem("kin_ready"), 1)
            for li in range(7):
                scale_level(li)
                if li + 2 < 7:
                    diff(li + 2)
                if li % 2 == 0:
                    queries(3 + li // 2, li + 1)
            queries(7, 7)
            def last_pages(first, last):
                with pool.Fori(first, last) as b:
                    for j in range(4):
                        pool.wait_ge(sem("value_slots"), b * 4 + (j + 1))
                        load_pages(pool, "cache_v", b, j, [3], "v3_landed")

            last_pages(0, NSEQ)
            pool.wait_ge(sem("v_stored"), 32)
            pool.wait_ge(sem("k_stored"), 32)

        @block.scalar
        def _(act):
            step = [0]

            def link(ins):
                step[0] += 1
                ins.then_inc(sem("act_step"), 1)
                act.wait_ge(sem("act_step"), step[0])

            act.dma_start(const[:, 0:FIRST], inp["const"][:, 0:FIRST]).then_inc(sem("const0_landed"), 16)
            act.dma_start(crow[0:1, :], inp["c_prompt"]).then_inc(sem("c_landed"), 16)
            act.dma_start(crow[1:CC, :], inp["c_sample"]).then_inc(sem("c_landed"), 16)
            act.dma_start(prow[R_ADA:R_ADA + 48, :], inp["b_ada"].rearrange("o (r n) -> (o r) n", n=P)).then_inc(sem("par_landed"), 16)
            for r, name in ((R_PRE1, "g_pre1"), (R_POST1, "g_post1"), (R_PRE2, "g_pre2"), (R_POST2, "g_post2")):
                act.dma_start(prow[r:r + 8, :], inp[name].rearrange("o (r n) -> (o r) n", n=P)).then_inc(sem("par_landed"), 16)
            act.dma_start(prow[R_LB:R_LB + 8, :], inp["hg_lb"].rearrange("o (r n) -> (o r) n", n=P)).then_inc(sem("par_landed"), 16)
            act.dma_start(prow[R_ON:R_ON + 1, :], inp["g_onorm"]).then_inc(sem("par_landed"), 16)
            act.dma_start(xtok[:, 0:2, :], inp["x_prompt"][0].rearrange("(t p) d -> p t d", p=P)).then_inc(sem("x_landed"), 16)
            act.dma_start(xtok[0:TSA, 2, :], inp["x_sample"].rearrange("b t d -> (b t) d")).then_inc(sem("x_landed"), 16)
            act.dma_start(pgt[:, :], inp["page_table"].rearrange("(o a) b -> o (a b)", o=1)).then_inc(sem("table_landed"), 16)
            act.dma_start(const[:, FIRST:], inp["const"][:, FIRST:]).then_inc(sem("const1_landed"), 16)
            act.dma_start(lvl_i[:, :, :], inp["lvl"]).then_inc(sem("lvl_landed"), 16)

            act.wait_ge(sem("rows_turned"), 1)
            act.activation(cols[:, :], ps[:, 6, 0:R_ALL], ACT.Copy).then_inc(sem("cols_ready"), 1)
            act.wait_ge(sem("rows_turned"), 2)
            link(act.activation(cs[:, :, :], ps[:, 7, 0:DT * CC].rearrange("p (k c) -> p k c", c=CC), ACT.Silu))
            act.activation(cst[:, :, 0:CC], cs[:, :, :], ACT.Copy).then_inc(sem("c_hi"), 1)

            def hi(w, landed, s, count, par, rows=BK):
                act.wait_ge(sem(f"{landed}{s}"), count)
                if not isinstance(w, int) or w >= 2:
                    act.wait_ge(sem("w_used"), w - 1)
                act.activation(w_hi[:, par, 0:rows, :], slot4(s)[:, 0:rows, :], ACT.Copy).then_inc(sem("hi_split"), 1)

            def hi_a(n):
                hi(n, "w_landed", n % NSLOT, 16 * (n // NSLOT + 1), n % 2)

            def evac_ada(g, w):
                act.wait_ge(sem("w_used"), w + 1)
                if not isinstance(g, int) or g >= 1:
                    act.wait_ge(sem("mod_rows_turned"), g)
                act.activation(arow[:, :], ps[0:2 * CC, 4, :], ACT.Copy).then_inc(sem("ada_rows"), 1)

            def evac_in(g, w):
                for j in range(4):
                    if j < 3:
                        act.wait_ge(sem("tile_done"), g * 3 + (j + 1))
                    else:
                        act.wait_ge(sem("w_used"), w + 1)
                    act.activation(proj[:, bass.ds(g * 4 + j, 1), :], ps[:, j:j + 1, 0:T], ACT.Copy).then_inc(sem("tile_out"), 1)

            hi_a(0)
            hi_a(1)
            for k in range(DT):
                act.wait_ge(sem("x_turned"), k + 1)
                act.activation(xT[:, k, :], ps[:, k % 4, 0:T], ACT.Copy).then_inc(sem("x_ready"), 1)
            for g in range(1, 4):
                hi_a(2 * g)
                evac_ada(g - 1, 2 * g - 1)
                hi_a(2 * g + 1)
            act.wait_ge(sem("x_sum"), 1)
            act.wait_ge(sem("const0_landed"), 16)
            act.activation(rs[:, :], ps[:, 7, 0:T], ACT.Sqrt, scale=1.0 / D, bias=C("eps")).then_inc(sem("root"), 1)
            evac_ada(3, 7)
            act.wait_ge(sem("h_ready"), 1)
            act.activation(h_hi[:, :, :], h32[:, :, :], ACT.Copy).then_inc(sem("h_hi"), 1)
            act.wait_ge(sem("lb_arg"), 1)
            act.activation(lbt[:, 1:3, :], lbt[:, 1:3, :], ACT.Exp).then_inc(sem("lb_exp"), 1)
            hi_a(8)
            hi_a(9)
            with act.Fori(0, 7) as i:
                hi(i * 4 + 10, "w_landed", 2, i * 16 + 48, 0)
                evac_in(i, i * 4 + 9)
                hi(i * 4 + 11, "w_landed", 3, i * 16 + 48, 1)
                hi(i * 4 + 12, "w_landed", 0, i * 16 + 64, 0)
                evac_ada(i + 4, i * 4 + 11)
                hi(i * 4 + 13, "w_landed", 1, i * 16 + 64, 1)
            hi_a(38)
            evac_in(7, 37)
            hi_a(39)
            hi_a(40)
            evac_ada(11, 39)
            hi_a(41)
            hi_a(42)
            evac_in(8, 41)
            hi_a(43)
            hi_a(44)
            evac_in(9, 43)
            hi_a(45)
            evac_in(10, 45)

            act.wait_ge(sem("table_landed"), 16)
            for j in range(4):
                act.wait_ge(sem("key_slots"), j + 1)
                load_pages(act, "cache_k", 0, j, [3], "k3_landed")
            act.wait_ge(sem("tile_out"), 44)
            act.activation(proj[:, HF:HF + 4, :], proj[:, HF:HF + 4, :], ACT.Sigmoid).then_inc(sem("sig_f"), 1)
            act.wait_ge(sem("v_turned"), 1)
            act.activation(vtok[:, 0:2, :], ps[:, 0:2, :], ACT.Copy)
            act.activation(vtok[0:TSA, 2, :], ps[0:TSA, 2, :], ACT.Copy).then_inc(sem("v_tok"), 1)
            act.wait_ge(sem("k_turned_tok"), 1)
            act.activation(ktok[:, 0:2, :], ps[:, 4:6, :], ACT.Copy)
            act.activation(ktok[0:TSA, 2, :], ps[0:TSA, 6, :], ACT.Copy).then_inc(sem("k_tok"), 1)
            act.wait_ge(sem("k_tok"), 1)
            act.dma_start(out["k_prompt"][0, 0].rearrange("(t p) h d -> p t (h d)", p=P), ktok[:, 0:2, :]).then_inc(sem("k_stored"), 16)
            act.dma_start(out["k_sample"][0].rearrange("b t h d -> (b t) (h d)"), ktok[0:TSA, 2, :]).then_inc(sem("k_stored"), 16)
            act.activation(proj[:, UA:UA + 16, :], proj[:, UA:UA + 16, :], ACT.Sigmoid).then_inc(sem("sig_u"), 1)
            act.activation(proj[:, HG:HG + 4, :], proj[:, HG:HG + 4, :], ACT.Silu).then_inc(sem("silu_g"), 1)

            def keys(b, *blocks):
                for j in blocks:
                    act.wait_ge(sem("key_slots"), 4 * b + j + 1)
                    load_pages(act, "cache_k", b, j, [3], "k3_landed")

            act.wait_ge(sem("f_ready"), 1)
            act.activation(hkt[:, :, :], proj[:, HF:HF + 4, :], ACT.Ln).then_inc(sem("logf"), 1)
            keys(1, 0, 1)
            act.wait_ge(sem("b_ready"), 1)
            act.activation(hqt[:, :, :], hb[:, :, :], ACT.Exp).then_inc(sem("eb"), 1)
            keys(1, 2)
            act.wait_ge(sem("kd_ready"), 1)
            act.activation(hkt[:, :, :], hkt[:, :, :], ACT.Exp).then_inc(sem("ekd"), 1)

            def scores(b):
                act.wait_ge(sem("kt_used"), 4 * (b + 1))
                act.activation(S[:, b, 0:512], ps[:, b % 2, :], ACT.Copy).then_inc(sem("scores_out"), 1)

            def level_exp(li):
                r = TP if LEVELS[li] > 2 else T
                act.wait_ge(sem("lv_diff"), li + 1)
                act.activation(hx[li % 2][:, :, 0:r], hx[li % 2][:, :, 0:r], ACT.Exp).then_inc(sem("lv_exp"), 1)

            keys(1, 3)
            level_exp(0)
            keys(2, 0)
            scores(0)
            level_exp(1)
            keys(2, 1, 2, 3)
            act.wait_ge(sem("h_turned"), 1)
            act.activation(hktok[:, :, :, :], ps[:, 2:4, :].rearrange("p t (h d) -> p t h d", h=HH), ACT.Copy)
            act.activation(hvtok[:, :, :, :], ps[:, 4:6, :].rearrange("p t (h d) -> p t h d", h=HH), ACT.Copy)
            act.activation(hks[:, :, :], ps[0:TSA, 6, :].rearrange("p (h d) -> p h d", h=HH), ACT.Copy)
            act.activation(hvs[:, :, :], ps[0:TSA, 7, :].rearrange("p (h d) -> p h d", h=HH), ACT.Copy).then_inc(sem("h_tok"), 1)
            keys(3, 0)
            scores(1)
            for b in range(2, 7):
                if b > 2:
                    keys(b + 1, 0)
                    scores(b - 1)
                    if 2 * b - 3 < 7:
                        level_exp(2 * b - 3)
                keys(b + 1, 1, 2)
                if 2 * b - 2 < 7:
                    level_exp(2 * b - 2)
                keys(b + 1, 3)
            scores(6)
            act.wait_ge(sem("d_done"), 1)
            act.activation(D0[:, :, :], ps[:, 2, :].rearrange("p (h d) -> p h d", h=HH), ACT.Copy).then_inc(sem("d0_ready"), 1)
            scores(7)
            act.wait_ge(sem("shift_ready"), 1)
            for b in range(NSEQ):
                act.wait_ge(sem("s_chosen"), b + 1)
                act.activation(S[:, b, :], S[:, b, :], ACT.Exp, bias=stat[:, 304 + b:305 + b], accum_out=stat[:, 320 + b:321 + b]).then_inc(sem("s_exp"), 1)
            act.wait_ge(sem("o_done"), 1)
            for t in range(2):
                act.activation(hb[:, :, t * P:(t + 1) * P], ps[:, 4 + t, :].rearrange("p (h d) -> p h d", h=HH), ACT.Copy)
            link(act.activation(hb[:, :, SAMP], ps[:, 6, 0:HH * TSA].rearrange("p (h d) -> p h d", h=HH), ACT.Copy))
            act.activation(hx[0][:, :, :], hb[:, :, :], ACT.Square).then_inc(sem("o_sq"), 1)
            act.wait_ge(sem("o_sum"), 1)
            for t in range(2):
                act.activation(hx[1][:, :, t * P:(t + 1) * P], ps[:, 4 + t, :].rearrange("p (h d) -> p h d", h=HH), ACT.Sqrt, scale=1.0 / DK, bias=C("eps"))
            act.activation(hx[1][:, :, SAMP], ps[:, 6, 0:HH * TSA].rearrange("p (h d) -> p h d", h=HH), ACT.Sqrt, scale=1.0 / DK, bias=C("eps")).then_inc(sem("o_root"), 1)
            act.wait_ge(sem("oa_ready"), 1)
            act.activation(oa_hi[:, :, :], proj[:, HQ:HQ + 4, :], ACT.Copy).then_inc(sem("oab_hi"), 1)

            act.wait_ge(sem("state_p"), 1)
            act.dma_start(out["state_p"][0, 0].rearrange("h d e -> d h e"), Sfin[:, :, :]).then_inc(sem("st_stored"), 16)
            act.wait_ge(sem("state_s"), HH)
            for g in range(4):
                act.dma_start(out["state_s"][0, 2 * g:2 * g + 2].rearrange("b h d e -> d b h e"), S0[:, 2 * g:2 * g + 2]).then_inc(sem("st_stored"), 16)

            def pa_pair(a):
                act.wait_ge(sem("pv_done"), 2 * a + 2)
                act.activation(proj[:, AQ + a, 0:TP], ps[:, 7, 0:TP], ACT.Copy).then_inc(sem("ob_p"), 1)

            for h in range(AH + 1):
                if h < AH:
                    act.wait_ge(sem("pa_masked"), h + 1)
                    for t in range(2):
                        a, e = (0, P) if t == 0 else (P, 3 * P)
                        ins = act.activation(pa[:, h % 2, a:e], pa[:, h % 2, a:e], ACT.Exp, bias=nmx[:, h % 2, t:t + 1], accum_out=den[:, h % 2, t:t + 1])
                    ins.then_inc(sem("pa_exp"), 1)
                if h >= 1:
                    act.wait_ge(sem("pa_turned"), h)
                    if h >= 2:
                        act.wait_ge(sem("pv_done"), h - 1)
                    if h >= 3 and h % 2 == 1:
                        pa_pair((h - 3) // 2)
                    act.activation(paT[:, :], ps[:, TURN[(h - 1) % 2], 0:384], ACT.Copy).then_inc(sem("paT_ready"), 1)
            pa_pair(PAIRS - 1)

            def hi_b(w, rows=BK):
                n = w + 64
                s = n % NSLOT
                before = (NA + NSLOT - 1 - s) // NSLOT + (2 if w >= 76 else 0)
                hi(w, "w_landed", s, 16 * (before + (n - (B0 if w < 76 else 76 + 64)) // NSLOT + 1), w % 2, rows)

            act.wait_ge(sem("oa_ready"), 1)
            hi_b(46)
            act.wait_ge(sem("st_stored"), 80)
            act.wait_ge(sem("ob_p"), PAIRS)
            act.wait_ge(sem("ob_s"), 2)
            act.activation(ob_hi[:, :, :], proj[:, AQ:AQ + 4, :], ACT.Copy).then_inc(sem("oab_hi"), 1)

            def m_split(cg):
                act.wait_ge(sem("merged"), cg + 1)
                act.activation(m_hi[:, 4 * cg:4 * cg + 4, :], proj[:, UA + 4 * cg:UA + 4 * cg + 4, :], ACT.Copy).then_inc(sem("m_hi"), 1)

            def y_evac(cg):
                for j in range(4 * cg, 4 * cg + 4):
                    if j % 4 < 3:
                        act.wait_ge(sem("y1_done"), 3 * cg + j % 4 + 1)
                    else:
                        act.wait_ge(sem("w_used"), 52 + 2 * cg)
                    act.activation(proj[:, j, :], ps[:, j % 4, 0:T], ACT.Copy).then_inc(sem("y1_out"), 1)

            hi_b(47)
            hi_b(48)
            m_split(0)
            hi_b(49)
            hi_b(50)
            m_split(1)
            hi_b(51)
            hi_b(52)
            y_evac(0)
            hi_b(53)
            hi(54, "gu_landed", 2, 32, 0)
            y_evac(1)
            hi(55, "gu_landed", 3, 32, 1)
            act.wait_ge(sem("y1_sum"), 1)
            act.activation(rs[:, :], ps[:, 4, 0:T], ACT.Sqrt, scale=1.0 / D, bias=C("eps")).then_inc(sem("root"), 1)
            act.wait_ge(sem("x1_ready"), 1)
            act.activation(sq[:, :, :], xT[:, :, :], ACT.Square).then_inc(sem("x1_sq"), 1)
            act.wait_ge(sem("x1_sum"), 1)
            act.activation(rs[:, :], ps[:, 5, 0:T], ACT.Sqrt, scale=1.0 / D, bias=C("eps")).then_inc(sem("root"), 1)
            act.wait_ge(sem("h_ready"), 2)
            act.activation(h_hi[:, :, :], h32[:, :, :], ACT.Copy).then_inc(sem("h_hi"), 1)

            def gates(g, base):
                act.wait_ge(sem("gu_done"), g * 3 + 2)
                act.wait_ge(sem("fu_ready"), g + 1)
                act.activation(fa[:, :, :], ps[:, base:base + 2, 0:T], ACT.Silu).then_inc(sem("silu_done"), 1)

            def f_split(g):
                act.wait_ge(sem("fu_ready"), g + 2)
                act.activation(f_hi[:, bass.ds(g * 2, 2), :], fu[:, :, :], ACT.Copy).then_inc(sem("f_hi"), 1)

            with act.Fori(0, 5) as i:
                hi(i * 4 + 56, "gu_landed", 0, i * 32 + 32, 0)
                gates(i * 2, 0)
                hi(i * 4 + 57, "gu_landed", 1, i * 32 + 32, 1)
                f_split(i * 2)
                hi(i * 4 + 58, "gu_landed", 2, i * 32 + 64, 0)
                gates(i * 2 + 1, 4)
                hi(i * 4 + 59, "gu_landed", 3, i * 32 + 64, 1)
                f_split(i * 2 + 1)

            def hi_d(i):
                hi_b(76 + i, 2 if i % 6 == 5 else BK)

            def y2_evac(cg):
                for j in range(4):
                    if j < 3:
                        act.wait_ge(sem("y2_done"), 3 * cg + j + 1)
                    else:
                        act.wait_ge(sem("w_used"), 82 + 6 * cg)
                    act.activation(y2[:, 4 * cg + j, :], ps[:, 4 * (1 - cg) + j, 0:T], ACT.Copy).then_inc(sem("y2_out"), 1)

            hi_d(0)
            gates(10, 0)
            hi_d(1)
            f_split(10)
            for i in range(2, 7):
                hi_d(i)
            y2_evac(0)
            for i in range(7, 12):
                hi_d(i)
            y2_evac(1)
            act.wait_ge(sem("y2_sum"), 1)
            act.activation(rs[:, :], ps[:, 4, 0:T], ACT.Sqrt, scale=1.0 / D, bias=C("eps")).then_inc(sem("root"), 1)
            for tt in range(3):
                rows = P if tt < 2 else TSA
                act.wait_ge(sem("y_turned"), tt + 1)
                b0 = (0, 2, 5)[tt]
                act.activation(ytok[0:rows, tt, :], ps[0:rows, b0:b0 + 2, :], ACT.Copy).then_inc(sem("y_tok"), 1)

        @block.vector
        def _(dve):
            step = [0]

            def link(ins):
                step[0] += 1
                ins.then_inc(sem("dve_step"), 1)
                dve.wait_ge(sem("dve_step"), step[0])

            def lo(w, s, par, rows=BK):
                dve.wait_ge(sem("hi_split"), w + 1)
                dve.tensor_tensor(w_lo[:, par, 0:rows, :], slot4(s)[:, 0:rows, :], w_hi[:, par, 0:rows, :].bitcast(F32), ALU.subtract).then_inc(sem("lo_split"), 1)

            def lo_a(n):
                lo(n, n % NSLOT, n % 2)

            def mod_add(g):
                dve.wait_ge(sem("mod_rows_turned"), g + 1)
                dve.tensor_tensor(modT[:, bass.ds(g * 4, 4), :], ps[:, 5, 0:4 * CC].rearrange("p (k c) -> p k c", c=CC),
                                  over(cols[:, bass.ds(g * 4 + R_ADA, 4)], 2, CC), ALU.add).then_inc(sem("mod_ready"), 1)

            def scaled(dst, src, g, s, res):
                for k in range(DT):
                    if res is None:
                        ins = dve.tensor_scalar(dst[:, k, 0:TP], src[:, k, 0:TP], g[:, k, 0:1], s[:, k, 0:1], ALU.mult, ALU.add)
                    else:
                        ins = dve.scalar_tensor_tensor(dst[:, k, 0:TP], src[:, k, 0:TP], g[:, k, 0:1], res[:, k, 0:TP], ALU.mult, ALU.add)
                v = src[:, :, SAMP].rearrange("p k (b t) -> p k b t", t=TS)
                link(dve.tensor_tensor(v, v, over(g[:, :, 1:CC], 3, TS), ALU.mult))
                other = over(s[:, :, 1:CC], 3, TS) if res is None else res[:, :, SAMP].rearrange("p k (b t) -> p k b t", t=TS)
                return dve.tensor_tensor(dst[:, :, SAMP].rearrange("p k (b t) -> p k b t", t=TS), v, other, ALU.add)

            def part(k):
                return modT[:, 8 * k:8 * k + 8, :]

            dve.wait_ge(sem("c_hi"), 1)
            dve.tensor_tensor(cst[:, :, CC:2 * CC], cs[:, :, :], cst[:, :, 0:CC].bitcast(F32), ALU.subtract).then_inc(sem("c_lo"), 1)
            lo_a(0)
            lo_a(1)
            dve.wait_ge(sem("x_ready"), DT)
            dve.tensor_tensor(sq[:, :, :], xT[:, :, :], xT[:, :, :], ALU.mult).then_inc(sem("x_sq"), 1)
            for g in range(1, 4):
                lo_a(2 * g)
                lo_a(2 * g + 1)
                mod_add(g - 1)
            dve.wait_ge(sem("root"), 1)
            link(dve.reciprocal(rs[:, :], rs[:, :]))
            link(dve.tensor_tensor(sq[:, :, :], xT[:, :, :], over(rs[:, :], 1, DT), ALU.mult))
            lb0, lb1 = cols[:, R_LB:R_LB + 4], cols[:, R_LB + 4:R_LB + 8]
            link(dve.tensor_tensor(lbt[:, 0, :], lb0, lb1, ALU.max))
            dve.tensor_tensor(lbt[:, 1, :], lb0, lbt[:, 0, :], ALU.subtract)
            dve.tensor_tensor(lbt[:, 2, :], lb1, lbt[:, 0, :], ALU.subtract).then_inc(sem("lb_arg"), 1)
            mod_add(3)
            dve.wait_ge(sem("mod_ready"), 4)
            link(dve.scalar_tensor_tensor(gain[:, :, :], part(1), 1.0, over(cols[:, R_PRE1:R_PRE1 + DT], 2, CC), ALU.add, ALU.mult))
            scaled(h32, sq, gain, part(0), None).then_inc(sem("h_ready"), 1)
            dve.wait_ge(sem("h_hi"), 1)
            dve.tensor_tensor(h_lo[:, :, :], h32[:, :, :], h_hi[:, :, :].bitcast(F32), ALU.subtract).then_inc(sem("h_lo"), 1)
            lo_a(8)
            lo_a(9)
            with dve.Fori(0, 7) as i:
                lo(i * 4 + 10, 2, 0)
                lo(i * 4 + 11, 3, 1)
                lo(i * 4 + 12, 0, 0)
                lo(i * 4 + 13, 1, 1)
                mod_add(i + 4)
            for n in range(38, 42):
                lo_a(n)
            mod_add(11)
            for n in range(42, 46):
                lo_a(n)
            dve.wait_ge(sem("lb_exp"), 1)
            link(dve.tensor_tensor(lbt[:, 3, :], lbt[:, 1, :], lbt[:, 2, :], ALU.add))
            link(dve.reciprocal(lbt[:, 3, :], lbt[:, 3, :]))
            link(dve.tensor_tensor(lbt[:, 4, :], lbt[:, 1, :], lbt[:, 3, :], ALU.mult))
            link(dve.tensor_scalar(lbt[:, 5, :], lbt[:, 4, :], -1.0, 1.0, ALU.mult, ALU.add))
            dve.wait_ge(sem("lo_split"), NA)
            dve.nop().then_inc(sem("key_slots"), NSLOT)

            cosb, sinb = over(C("cos"), 1, 4), over(C("sin"), 1, 4)
            dve.wait_ge(sem("const1_landed"), 16)
            for j, (t0, scale) in enumerate(((AQ, DH ** -0.5), (AK, 1.0))):
                dve.wait_ge(sem("swapped"), j + 1)
                x = proj[:, t0:t0 + 4, :]
                link(dve.scalar_tensor_tensor(sq[:, 4 * j:4 * j + 4, :], ps[:, 4 * j:4 * j + 4, 0:T], scale, sinb, ALU.mult, ALU.mult))
                dve.nop().then_inc(sem("swap_used"), 1)
                link(dve.scalar_tensor_tensor(x, x, scale, cosb, ALU.mult, ALU.mult))
                dve.tensor_tensor(x, x, sq[:, 4 * j:4 * j + 4, :], ALU.add).then_inc(sem("roped"), 1)
            dve.wait_ge(sem("w_used"), NA)
            link(dve.memset(Qbd[:, :, :, :], 0.0))
            dve.wait_ge(sem("roped"), 1)
            for pair in range(PAIRS):
                for hl in range(2):
                    rows = slice(64 * hl, 64 * hl + 64)
                    c = (2 * pair + hl) * TS
                    ins = dve.tensor_copy(Qbd[rows, pair, :, c:c + TS], proj[rows, AQ + pair, SAMP].rearrange("p (b t) -> p b t", t=TS))
            ins.then_inc(sem("q_blocks"), 1)
            dve.wait_ge(sem("spread_done"), 1)
            dve.tensor_copy(Qrep[:, :, :, :].rearrange("p a s t -> p s a t"), ps[:, 3, :].rearrange("p (s a t) -> p s a t", s=4, a=PAIRS)).then_inc(sem("q_spread"), 1)
            dve.wait_ge(sem("own_scored"), 1)
            link(dve.memset(S[:, :, 512:SW], NEG))
            dve.tensor_tensor(S[0:32, :, 512:SW], ps[0:32, 7, 0:256].rearrange("p (b k) -> p b k", b=NSEQ),
                              C("own", 32).rearrange("p (b k) -> p b k", b=NSEQ), ALU.add).then_inc(sem("own_out"), 1)

            def turn_keys(u):
                dve.wait_ge(sem(f"k_landed{u % 4}"), (u // 4 + 1) * 48)
                dve.wait_ge(sem(f"k3_landed{u % 4}"), (u // 4 + 1) * 16)
                if u >= 2:
                    dve.wait_ge(sem("kt_used"), u - 1)
                dve.transpose(KT[:, u % 2, :, :], ring[:, KV_SLOT[u % 4], :].rearrange("p (g n) -> p g n", n=512)).then_inc(sem("key_slots"), 1)

            def st(k, n=NSEQ * NB):
                return stat[:, k:k + n]
            gpart, gate, pen, bmax = st(0), st(64), st(128), st(192)
            rmax, lane4, omax, shift = st(256, 8), st(264, 32), st(296, 8), st(304, 8)
            rden, total, rrow = st(312, 8), st(320, 8), st(364, 2)
            bn = "p (b n) -> p b n"
            cached = S[:, :, 0:512].rearrange("p b (n k) -> p b n k", n=NB)

            def block_sums(b):
                dve.wait_ge(sem("scores_out"), b + 1)
                dve.tensor_reduce(gpart[:, b * NB:(b + 1) * NB], cached[:, b], AX, ALU.add).then_inc(sem("gate_parts"), 1)
                dve.tensor_reduce(bmax[:, b * NB:(b + 1) * NB], cached[:, b], AX, ALU.max)

            def keep(gi):
                dve.wait_ge(sem("gram_done"), gi + 1)
                if gi:
                    dve.wait_ge(sem("kept"), gi)
                li = gi - 1
                mask = lvl[:, 7 if gi == 0 else li, :]
                b0 = 2 + 2 * (gi % 2)
                ins = dve.copy_predicated(hA[:, :, :, :].rearrange("p t h s -> p (t h) s"), over(mask, 1, 2 * HH),
                                          ps[:, b0:b0 + 2, :].rearrange("p t (h s) -> p (t h) s", h=HH))
                if gi == 0 or LEVELS[li] <= 2:
                    link(ins)
                    ins = dve.copy_predicated(hAs[:, :, :], over(mask[0:TSA, 0:TSA], 1, HH),
                                              ps[0:TSA, 6 + gi % 2, 0:HH * TSA].rearrange("p (h s) -> p h s", h=HH))
                ins.then_inc(sem("kept"), 1)

            kin, q = proj[:, HF:HF + 4, :], proj[:, HQ:HQ + 4, :]
            turn_keys(0)
            dve.wait_ge(sem("own_out"), 1)
            dve.tensor_reduce(omax, S[:, :, 512:SW], AX, ALU.max)
            dve.wait_ge(sem("sig_f"), 1)
            for h in range(HH):
                ins = dve.tensor_scalar(proj[:, HF + h, :], proj[:, HF + h, :], lbt[:, 5, h:h + 1], lbt[:, 4, h:h + 1], ALU.mult, ALU.add)
            ins.then_inc(sem("f_ready"), 1)
            turn_keys(1)
            turn_keys(2)
            dve.wait_ge(sem("logf"), 1)
            dve.tensor_scalar(kin, kin, -1.0, 1.0, ALU.mult, ALU.add).then_inc(sem("kin_ready"), 1)
            for h in range(HH):
                ins = dve.tensor_tensor_scan(hb[:, h, :], C("carry"), hkt[:, h, :], 0.0, ALU.mult, ALU.add)
            ins.then_inc(sem("b_ready"), 1)
            turn_keys(3)
            dve.wait_ge(sem("b_ready"), 1)
            bp, bs = hb[:, :, 0:TP].rearrange("p h (n k) -> p h n k", k=P), hb[:, :, SAMP].rearrange("p h (n k) -> p h n k", k=TS)
            kp, ks = hkt[:, :, 0:TP].rearrange("p h (n k) -> p h n k", k=P), hkt[:, :, SAMP].rearrange("p h (n k) -> p h n k", k=TS)
            dve.tensor_tensor(kp, bp[:, :, :, P - 1:P].broadcast_to([P, HH, 2, P]), bp, ALU.subtract)
            dve.tensor_tensor(ks, bs[:, :, :, TS - 1:TS].broadcast_to([P, HH, NSEQ, TS]), bs, ALU.subtract).then_inc(sem("kd_ready"), 1)
            turn_keys(4)
            dve.memset(hA[:, :, :, :], 0.0)
            dve.memset(hAs[:, :, :], 0.0)
            dve.wait_ge(sem("eb"), 1)
            dve.tensor_copy(stat[:, 328:332], hqt[:, :, TP - 1])
            link(dve.tensor_copy(stat[:, 332:332 + HH * NSEQ].rearrange("p (h b) -> p h b", h=HH),
                                 hqt[:, :, SAMP].rearrange("p h (b t) -> p h b t", t=TS)[:, :, :, TS - 1]))
            dve.tensor_tensor(hqt[:, :, :], hqt[:, :, :], q, ALU.mult).then_inc(sem("qt_ready"), 1)
            turn_keys(5)
            dve.wait_ge(sem("ekd"), 1)
            dve.wait_ge(sem("kin_ready"), 1)
            dve.tensor_tensor(hkt[:, :, :], hkt[:, :, :], kin, ALU.mult).then_inc(sem("kt_ready"), 1)
            turn_keys(6)
            turn_keys(7)
            block_sums(0)
            dve.wait_ge(sem("lvl_ready"), 1)
            for b in range(2, NSEQ):
                for j in range(4):
                    turn_keys(4 * b + j)
                    if j == 1:
                        block_sums(b - 1)
                    gi = (4 * b + j - 10) // 2
                    if j % 2 == 0 and 0 <= gi < 8:
                        keep(gi)
            dve.wait_ge(sem("key_slots"), NSLOT + 32)
            dve.nop().then_inc(sem("value_slots"), NSLOT)
            block_sums(NSEQ - 1)

            dve.wait_ge(sem("gate_sum"), 1)
            link(dve.tensor_copy(gate, ps[:, 1, 0:64]))
            g3 = gate.rearrange(bn, b=NSEQ)
            g_m, g_n = over(g3, 2, NB), over(g3, 3, NB)
            dve.wait_ge(sem("k_stored"), 32)
            link(dve.tensor_tensor(cmp1[:, :, :, :], g_m, g_n, ALU.is_gt))
            link(dve.tensor_tensor(cmp2[:, :, :, :], g_m, g_n, ALU.is_equal))
            link(dve.tensor_tensor(cmp2[:, :, :, :], cmp2[:, :, :, :], over(C("tie").rearrange("p (n m) -> p n m", n=NB), 1, NSEQ), ALU.mult))
            link(dve.tensor_tensor(cmp1[:, :, :, :], cmp1[:, :, :, :], cmp2[:, :, :, :], ALU.add))
            link(dve.tensor_reduce(pen.rearrange(bn, b=NSEQ), cmp1[:, :, :, :], AX, ALU.add))
            link(dve.tensor_scalar(pen, pen, TOPK - 0.5, NEG, ALU.is_gt, ALU.mult))
            link(dve.tensor_tensor(bmax, bmax, pen, ALU.add))
            link(dve.tensor_reduce(rmax, bmax.rearrange(bn, b=NSEQ), AX, ALU.max))
            link(dve.tensor_tensor(rmax, rmax, omax, ALU.max))
            for a in range(4):
                ins = dve.tensor_copy(lane4[0:32, 8 * a:8 * a + 8], rmax[32 * a:32 * a + 32, :])
            link(ins)
            dve.tensor_reduce(rmax[0:32, :], lane4[0:32, :].rearrange("p (a b) -> p b a", a=4), AX, ALU.max).then_inc(sem("row_max"), 1)

            def choose(b):
                dve.tensor_tensor(cached[:, b], cached[:, b], over(pen[:, b * NB:(b + 1) * NB], 2, 64), ALU.add).then_inc(sem("s_chosen"), 1)

            choose(0)
            choose(1)
            dve.wait_ge(sem("max_spread"), 1)
            dve.tensor_scalar(shift, ps[:, 1, 64:72], -1.0, None, ALU.mult).then_inc(sem("shift_ready"), 1)
            dve.wait_ge(sem("d_done"), 1)
            for b in range(NSEQ):
                if b + 2 < NSEQ:
                    choose(b + 2)
                dve.wait_ge(sem("s_exp"), b + 1)
                dve.transpose(Pt[:, b], S[:, b, :].rearrange("p (c n) -> p c n", n=32)).then_inc(sem("probs_ready"), 1)
            dve.wait_ge(sem("probs_ready"), NSEQ)
            for h in range(HH):
                dve.wait_ge(sem("h_tok"), 1)
                if h >= 1:
                    dve.wait_ge(sem("ds_done"), h)
                dve.tensor_tensor(vms[:, :, :], over(hvs[:, h, :], 1, NSEQ), over(C("seq", TSA), 2, DK), ALU.mult).then_inc(sem("vm_ready"), 1)
                if h == 0:
                    dve.wait_ge(sem("s0_landed"), 64)
                    dve.wait_ge(sem("o_done"), 1)
                eb = over(stat[:, 332 + NSEQ * h:332 + NSEQ * (h + 1)], 2, DK)
                link(dve.tensor_tensor(S0[:, :, h, :], S0[:, :, h, :], eb, ALU.mult))
                dve.wait_ge(sem("ds_done"), h + 1)
                dve.tensor_tensor(S0[:, :, h, :], S0[:, :, h, :], ps[:, 2:4, :].rearrange("p t (b e) -> p (t b) e", e=DK), ALU.add).then_inc(sem("state_s"), 1)
                if h == 0:
                    for hh in range(HH):
                        ins = dve.scalar_tensor_tensor(Sfin[:, hh, :], D0[:, hh, :], stat[:, 328 + hh:329 + hh], ps[:, 7, hh * DK:(hh + 1) * DK], ALU.mult, ALU.add)
                    ins.then_inc(sem("state_p"), 1)
            dve.wait_ge(sem("probs_sum"), 1)
            link(dve.reciprocal(rden, ps[:, 1, 128:136]))
            for j in range(4):
                rows = slice(32 * j, 32 * j + 32)
                ins = dve.tensor_copy(rrow[rows, :], rden[rows, :].rearrange("p (g j) -> p g j", j=4)[:, :, j])
            ins.then_inc(sem("rden_ready"), 1)
            dve.wait_ge(sem("o_root"), 1)
            link(dve.reciprocal(hx[1][:, :, :], hx[1][:, :, :]))
            link(dve.tensor_tensor(hb[:, :, :], hb[:, :, :], hx[1][:, :, :], ALU.mult))
            dve.wait_ge(sem("silu_g"), 1)
            dve.scalar_tensor_tensor(proj[:, HQ:HQ + 4, :], hb[:, :, :], cols[:, R_ON:R_ON + 1], proj[:, HG:HG + 4, :], ALU.mult, ALU.mult).then_inc(sem("oa_ready"), 1)
            dve.wait_ge(sem("oab_hi"), 1)
            dve.tensor_tensor(oa_lo[:, :, :], proj[:, HQ:HQ + 4, :], oa_hi[:, :, :].bitcast(F32), ALU.subtract).then_inc(sem("oab_lo"), 1)

            def sample_out(g):
                dve.wait_ge(sem("v_summed"), g + 1)
                dve.scalar_tensor_tensor(om[:, :, :], ps[:, g, :].rearrange("p (h d) -> p h d", h=AH), rrow[:, g:g + 1],
                                         over(C("ownhead"), 2, DH), ALU.mult, ALU.mult).then_inc(sem("om_ready"), 1)
                dve.wait_ge(sem("ob_turned"), g + 1)
                dve.tensor_copy(proj[:, AQ:AQ + 4, TP + 16 * g:TP + 16 * g + 16], ps[:, (2, 7)[g], 0:64].rearrange("p (a t) -> p a t", a=PAIRS)).then_inc(sem("ob_s"), 1)

            def pa_mask(h):
                bank = 4 + h % 2
                if h >= 2:
                    dve.wait_ge(sem("pa_turned"), h - 1)
                dve.wait_ge(sem("pa_scored"), h + 1)
                dve.tensor_tensor(pa[:, h % 2, 0:P], ps[:, bank, 0:P], C("causal"), ALU.add)
                dve.tensor_copy(pa[:, h % 2, P:2 * P], ps[:, bank, P:2 * P])
                link(dve.tensor_tensor(pa[:, h % 2, 2 * P:3 * P], ps[:, bank, 2 * P:3 * P], C("causal"), ALU.add))
                dve.tensor_reduce(nmx[:, h % 2, 0:1], pa[:, h % 2, 0:P], AX, ALU.max, negate=True)
                dve.tensor_reduce(nmx[:, h % 2, 1:2], pa[:, h % 2, P:3 * P], AX, ALU.max, negate=True).then_inc(sem("pa_masked"), 1)

            def pa_norm(h):
                dve.wait_ge(sem("pa_exp"), h + 1)
                link(dve.reciprocal(den[:, h % 2, :], den[:, h % 2, :]))
                dve.tensor_scalar(pa[:, h % 2, 0:P], pa[:, h % 2, 0:P], den[:, h % 2, 0:1], None, ALU.mult)
                dve.tensor_scalar(pa[:, h % 2, P:3 * P], pa[:, h % 2, P:3 * P], den[:, h % 2, 1:2], None, ALU.mult).then_inc(sem("pa_ready"), 1)

            for h in range(AH):
                if h >= 1:
                    pa_norm(h - 1)
                pa_mask(h)
                if h == 3:
                    sample_out(0)
            pa_norm(AH - 1)

            def lo_b(w, rows=BK):
                lo(w, (w + 64) % NSLOT, w % 2, rows)

            def gated(cg, j):
                u = proj[:, (UA, UB)[j] + 4 * cg:(UA, UB)[j] + 4 * cg + 4, :]
                dve.wait_ge(sem("w_used"), 46 + 2 * cg + j + 1)
                dve.tensor_tensor(u, ps[:, 4 * j:4 * j + 4, 0:T], u, ALU.mult).then_inc(sem("gated"), 1)

            def merge(cg):
                ua, ub = proj[:, UA + 4 * cg:UA + 4 * cg + 4, :], proj[:, UB + 4 * cg:UB + 4 * cg + 4, :]
                dve.wait_ge(sem("gated"), 2 * cg + 2)
                dve.tensor_tensor(ua, ua, ub, ALU.add).then_inc(sem("merged"), 1)

            def m_lower(cg):
                dve.wait_ge(sem("m_hi"), cg + 1)
                dve.tensor_tensor(m_lo[:, 4 * cg:4 * cg + 4, :], proj[:, UA + 4 * cg:UA + 4 * cg + 4, :],
                                  m_hi[:, 4 * cg:4 * cg + 4, :].bitcast(F32), ALU.subtract).then_inc(sem("m_lo"), 1)

            def y1_squares(cg):
                dve.wait_ge(sem("y1_out"), 4 * cg + 4)
                y = proj[:, 4 * cg:4 * cg + 4, :]
                dve.tensor_tensor(proj[:, 8 + 4 * cg:12 + 4 * cg, :], y, y, ALU.mult).then_inc(sem("y1_sq"), 1)

            sample_out(1)
            lo_b(46)
            dve.wait_ge(sem("oab_hi"), 2)
            dve.tensor_tensor(ob_lo[:, :, :], proj[:, AQ:AQ + 4, :], ob_hi[:, :, :].bitcast(F32), ALU.subtract).then_inc(sem("oab_lo"), 1)
            lo_b(47)
            dve.wait_ge(sem("sig_u"), 1)
            gated(0, 0)
            lo_b(48)
            gated(0, 1)
            merge(0)
            lo_b(49)
            m_lower(0)
            gated(1, 0)
            lo_b(50)
            gated(1, 1)
            merge(1)
            m_lower(1)
            lo_b(51)
            lo_b(52)
            y1_squares(0)
            lo_b(53)
            lo_b(54)
            y1_squares(1)
            lo_b(55)
            dve.wait_ge(sem("root"), 2)
            link(dve.reciprocal(rs[:, :], rs[:, :]))
            link(dve.tensor_tensor(gain[:, :, :], part(2), over(cols[:, R_POST1:R_POST1 + DT], 2, CC), ALU.mult))
            link(dve.tensor_tensor(proj[:, 8:16, :], proj[:, 0:8, :], over(rs[:, :], 1, DT), ALU.mult))
            scaled(xT, proj[:, 8:16, :], gain, None, xT).then_inc(sem("x1_ready"), 1)
            link(dve.scalar_tensor_tensor(gain[:, :, :], part(4), 1.0, over(cols[:, R_PRE2:R_PRE2 + DT], 2, CC), ALU.add, ALU.mult))
            dve.wait_ge(sem("root"), 3)
            link(dve.reciprocal(rs[:, :], rs[:, :]))
            link(dve.tensor_tensor(sq[:, :, :], xT[:, :, :], over(rs[:, :], 1, DT), ALU.mult))
            scaled(h32, sq, gain, part(3), None).then_inc(sem("h_ready"), 1)
            dve.wait_ge(sem("h_hi"), 2)
            dve.tensor_tensor(h_lo[:, :, :], h32[:, :, :], h_hi[:, :, :].bitcast(F32), ALU.subtract).then_inc(sem("h_lo"), 1)

            def product(g, base):
                dve.wait_ge(sem("silu_done"), g + 1)
                dve.wait_ge(sem("w_used"), g * 2 + 56)
                dve.wait_ge(sem("f_lo"), g + 1)
                dve.tensor_tensor(fu[:, :, :], ps[:, base + 2:base + 4, 0:T], fa[:, :, :], ALU.mult).then_inc(sem("fu_ready"), 1)

            def f_lower(g):
                dve.wait_ge(sem("f_hi"), g + 1)
                dve.tensor_tensor(f_lo[:, bass.ds(g * 2, 2), :], fu[:, :, :], f_hi[:, bass.ds(g * 2, 2), :].bitcast(F32), ALU.subtract).then_inc(sem("f_lo"), 1)

            dve.nop().then_inc(sem("fu_ready"), 1)
            dve.nop().then_inc(sem("f_lo"), 1)
            with dve.Fori(0, 5) as i:
                lo(i * 4 + 56, 0, 0)
                product(i * 2, 0)
                lo(i * 4 + 57, 1, 1)
                f_lower(i * 2)
                lo(i * 4 + 58, 2, 0)
                product(i * 2 + 1, 4)
                lo(i * 4 + 59, 3, 1)
                f_lower(i * 2 + 1)

            def y2_squares(cg):
                dve.wait_ge(sem("y2_out"), 4 * cg + 4)
                y = y2[:, 4 * cg:4 * cg + 4, :]
                dve.tensor_tensor(sq[:, 4 * cg:4 * cg + 4, :], y, y, ALU.mult).then_inc(sem("y2_sq"), 1)

            def lo_d(i):
                lo_b(76 + i, 2 if i % 6 == 5 else BK)

            lo_d(0)
            product(10, 0)
            lo_d(1)
            f_lower(10)
            for i in range(2, 7):
                lo_d(i)
            lo_d(7)
            y2_squares(0)
            for i in range(8, 12):
                lo_d(i)
            y2_squares(1)
            link(dve.tensor_tensor(gain[:, :, :], part(5), over(cols[:, R_POST2:R_POST2 + DT], 2, CC), ALU.mult))
            dve.wait_ge(sem("root"), 4)
            link(dve.reciprocal(rs[:, :], rs[:, :]))
            link(dve.tensor_tensor(y2[:, :, :], y2[:, :, :], over(rs[:, :], 1, DT), ALU.mult))
            scaled(xT, y2, gain, None, xT).then_inc(sem("x2_ready"), 1)

        @block.tensor
        def _(pe):
            def three(dst, w, kt, lhs, x_hi, x_lo, first, last):
                h, l = lhs
                pe.matmul(dst, h, x_hi, start=first, stop=False)
                pe.matmul(dst, h, x_lo, start=False, stop=False)
                return pe.matmul(dst, l, x_hi, start=False, stop=last)

            def ada(w, par, k, g=None):
                pe.wait_ge(sem("lo_split"), w + 1)
                if k == 0 and g is not None:
                    pe.wait_ge(sem("ada_rows"), g)
                for kt in range(BK):
                    c = k * BK + kt
                    pe.matmul(ps[0:2 * CC, 4, :], cst[:, c, :], w_hi[:, par, kt, :], start=c == 0, stop=False)
                    ins = pe.matmul(ps[0:2 * CC, 4, :], cst[:, c, :], w_lo[:, par, kt, :], start=False, stop=c == DT - 1)
                ins.then_inc(sem("w_used"), 1)

            def turn_ada(g):
                pe.wait_ge(sem("ada_rows"), g + 1)
                if not isinstance(g, int) or g >= 1:
                    pe.wait_ge(sem("mod_ready"), g)
                for j in range(4):
                    ins = pe.matmul(ps[:, 5, j * CC:(j + 1) * CC], arow[:, j * P:(j + 1) * P], C("foldc", 2 * CC), start=True, stop=True)
                ins.then_inc(sem("mod_rows_turned"), 1)

            def dense(w, par, x_hi, x_lo, kts, first, last, done, bank0=0, free=None, rows=BK):
                pe.wait_ge(sem("lo_split"), w + 1)
                for j in range(4):
                    if free is not None:
                        pe.wait_ge(sem(free[0]), free[1] + (j + 1 if len(free) == 2 else free[2][j]))
                    for kt in range(rows):
                        ins = three(ps[:, bank0 + j, 0:T], None, None, (w_hi[:, par, kt, j * P:(j + 1) * P], w_lo[:, par, kt, j * P:(j + 1) * P]),
                                    x_hi[:, kts + kt, :], x_lo[:, kts + kt, :], first and kt == 0, last and kt == rows - 1)
                    if j == 3:
                        ins.then_inc(sem("w_used"), 1)
                    elif last:
                        ins.then_inc(sem(done), 1)

            pe.wait_ge(sem("const0_landed"), 16)
            pe.wait_ge(sem("par_landed"), 112)
            pe.transpose(ps[:, 6, 0:R_ALL], prow[0:R_ALL, :], C("ident", R_ALL)[:, 0:R_ALL]).then_inc(sem("rows_turned"), 1)
            pe.wait_ge(sem("c_landed"), 32)
            for k in range(DT):
                ins = pe.transpose(ps[:, 7, k * CC:(k + 1) * CC], crow[:, k * P:(k + 1) * P], C("ident", CC)[:, 0:CC])
            ins.then_inc(sem("rows_turned"), 1)
            pe.wait_ge(sem("c_lo"), 1)
            ada(0, 0, 0)
            ada(1, 1, 1)
            pe.wait_ge(sem("x_landed"), 32)
            for k in range(DT):
                if k >= 4:
                    pe.wait_ge(sem("x_ready"), k - 3)
                for tt in range(3):
                    rows = P if tt < 2 else TSA
                    ins = pe.transpose(ps[:, k % 4, tt * P:tt * P + rows], xtok[0:rows, tt, k * P:(k + 1) * P], C("ident", rows)[:, 0:rows])
                ins.then_inc(sem("x_turned"), 1)
            for g in range(1, 4):
                ada(2 * g, 0, 0, g)
                turn_ada(g - 1)
                ada(2 * g + 1, 1, 1)
                if g == 1:
                    pe.wait_ge(sem("x_sq"), 1)
                    for k in range(DT):
                        ins = pe.matmul(ps[:, 7, 0:T], ones, sq[:, k, :], start=k == 0, stop=k == DT - 1)
                    ins.then_inc(sem("x_sum"), 1)
            turn_ada(3)
            pe.wait_ge(sem("h_lo"), 1)
            dense(8, 0, h_hi, h_lo, 0, True, False, "tile_done")
            dense(9, 1, h_hi, h_lo, 4, False, True, "tile_done")
            with pe.Fori(0, 7) as i:
                ada(i * 4 + 10, 0, 0, i + 4)
                ada(i * 4 + 11, 1, 1)
                dense(i * 4 + 12, 0, h_hi, h_lo, 0, True, False, "tile_done", free=("tile_out", i * 4))
                turn_ada(i + 4)
                dense(i * 4 + 13, 1, h_hi, h_lo, 4, False, True, "tile_done")
            ada(38, 0, 0, 11)
            ada(39, 1, 1)
            dense(40, 0, h_hi, h_lo, 0, True, False, "tile_done", free=("tile_out", 28))
            turn_ada(11)
            dense(41, 1, h_hi, h_lo, 4, False, True, "tile_done")
            for g in (9, 10):
                dense(24 + 2 * g, 0, h_hi, h_lo, 0, True, False, "tile_done", free=("tile_out", 4 * g - 4))
                dense(25 + 2 * g, 1, h_hi, h_lo, 4, False, True, "tile_done")

            pe.wait_ge(sem("tile_out"), 44)
            pe.wait_ge(sem("mod_ready"), 12)
            pe.wait_ge(sem("const1_landed"), 16)
            for j, t0 in enumerate((AQ, AK)):
                for k in range(4):
                    ins = pe.matmul(ps[:, 4 * j + k, 0:T], C("swap"), proj[:, t0 + k, :], start=True, stop=True)
                ins.then_inc(sem("swapped"), 1)
            pe.wait_ge(sem("swap_used"), 1)
            for tt in range(3):
                rows = P if tt < 2 else TSA
                for a in range(PAIRS):
                    ins = pe.transpose(ps[0:rows, tt, a * P:(a + 1) * P], proj[:, AV + a, tt * P:tt * P + rows], ident)
            ins.then_inc(sem("v_turned"), 1)
            pe.wait_ge(sem("roped"), 1)
            for s in range(4):
                ins = pe.matmul(ps[:, 3, s * P:(s + 1) * P], C(f"spread{s}"), proj[:, AQ:AQ + 4, SAMP], start=True, stop=True)
            ins.then_inc(sem("spread_done"), 1)
            pe.wait_ge(sem("roped"), 2)
            for tt in range(3):
                rows = P if tt < 2 else TSA
                for a in range(PAIRS):
                    ins = pe.transpose(ps[0:rows, 4 + tt, a * P:(a + 1) * P], proj[:, AK + a, tt * P:tt * P + rows], ident)
            ins.then_inc(sem("k_turned_tok"), 1)
            pe.wait_ge(sem("q_blocks"), 1)
            for b in range(NSEQ):
                for a in range(PAIRS):
                    ins = pe.matmul(ps[0:32, 7, b * TSA:(b + 1) * TSA], Qbd[:, a, b, :], proj[:, AK + a, SAMP], start=a == 0, stop=a == PAIRS - 1)
            ins.then_inc(sem("own_scored"), 1)

            def cached_keys(u):
                b, j = u // 4, u % 4
                if j == 0:
                    pe.wait_ge(sem("wq_ready"), b + 1)
                    if b >= 2:
                        pe.wait_ge(sem("scores_out"), b - 1)
                pe.wait_ge(sem("key_slots"), u + 1 + NSLOT)
                for c in range(16):
                    ins = pe.matmul(ps[:, b % 2, j * P:(j + 1) * P], Wq[:, b % 2, c * P:(c + 1) * P], KT[:, u % 2, :, c * 32:(c + 1) * 32],
                                    start=c == 0, stop=c == 15)
                ins.then_inc(sem("kt_used"), 1)

            def values(b, j):
                rows = slice(32 * (b % 4), 32 * (b % 4) + 32)
                if j == 0:
                    pe.wait_ge(sem("probs_ready"), b + 1)
                    if b == 4:
                        pe.wait_ge(sem("rden_ready"), 1)
                pe.wait_ge(sem(f"v_landed{j}"), 48 * (b + 1))
                pe.wait_ge(sem(f"v3_landed{j}"), 16 * (b + 1))
                for q in range(4):
                    ins = pe.matmul(ps[rows, b // 4, :], Pt[:, b, 4 * j + q, :], ring[:, KV_SLOT[j], q * 512:(q + 1) * 512],
                                    start=j + q == 0, stop=False)
                ins.then_inc(sem("value_slots"), 1)
                if j == 3:
                    ins = pe.matmul(ps[rows, b // 4, :], Pt[0:32, b, 16, :], vtok[0:32, 2, :], start=False, stop=True)
                    if b % 4 == 3:
                        ins.then_inc(sem("v_summed"), 1)

            def turn_hgrn():
                pe.wait_ge(sem("kt_ready"), 1)
                for x, b0 in ((hkt, 2), (proj[:, HI:HI + 4, :], 4)):
                    for tt in range(3):
                        rows = P if tt < 2 else TSA
                        bank = b0 + tt if tt < 2 else 6 + (b0 // 4)
                        for h in range(HH):
                            ins = pe.transpose(ps[0:rows, bank, h * P:(h + 1) * P], x[:, h, tt * P:tt * P + rows], ident)
                ins.then_inc(sem("h_turned"), 1)

            def gram(gi):
                li = gi - 1
                if gi == 0:
                    pe.wait_ge(sem("h_tok"), 1)
                else:
                    pe.wait_ge(sem("lv_ready"), li + 1)
                if gi >= 2:
                    pe.wait_ge(sem("kept"), gi - 1)
                left, right = (proj[:, HF:HF + 4, :], proj[:, HQ:HQ + 4, :]) if gi == 0 else (hx[li % 2], hx[li % 2])
                for tt in range(2):
                    for h in range(HH):
                        ins = pe.matmul(ps[:, 2 + 2 * (gi % 2) + tt, h * P:(h + 1) * P], left[:, h, tt * P:(tt + 1) * P], right[:, h, tt * P:(tt + 1) * P], start=True, stop=True)
                if gi == 0 or LEVELS[li] <= 2:
                    for h in range(HH):
                        ins = pe.matmul(ps[0:TSA, 6 + gi % 2, h * TSA:(h + 1) * TSA], left[:, h, SAMP], right[:, h, SAMP], start=True, stop=True)
                ins.then_inc(sem("gram_done"), 1)

            def hgrn_states():
                pe.wait_ge(sem("kept"), 8)
                for tt, bank in ((0, 2), (1, 7)):
                    for h in range(HH):
                        ins = pe.matmul(ps[:, bank, h * DK:(h + 1) * DK], hktok[:, tt, h, :], hvtok[:, tt, h, :], start=True, stop=True)
                ins.then_inc(sem("d_done"), 1)

            def hgrn_out():
                pe.wait_ge(sem("d0_ready"), 1)
                pe.wait_ge(sem("qt_ready"), 1)
                for h in range(HH):
                    for tt in range(2):
                        dst = ps[:, 4 + tt, h * P:(h + 1) * P]
                        pe.matmul(dst, hvtok[:, tt, h, :], hA[:, tt, h, :], start=True, stop=tt == 0)
                        if tt:
                            pe.matmul(dst, D0[:, h, :], hqt[:, h, P:TP], start=False, stop=True)

            def hgrn_sample_out():
                pe.wait_ge(sem("s0_landed"), 64)
                for h in range(HH):
                    pe.matmul(ps[:, 6, h * TSA:(h + 1) * TSA], hvs[:, h, :], hAs[:, h, :], start=True, stop=False, skip_group_check=True)
                    for b in range(NSEQ):
                        c = h * TSA + b * TS
                        ins = pe.matmul(ps[:, 6, c:c + TS], S0[:, b, h, :], hqt[:, h, TP + b * TS:TP + (b + 1) * TS], start=False, stop=b == NSEQ - 1, skip_group_check=True)
                ins.then_inc(sem("o_done"), 1)

            def sample_states(h):
                pe.wait_ge(sem("vm_ready"), h + 1)
                if h >= 1:
                    pe.wait_ge(sem("state_s"), h)
                for g in range(2):
                    ins = pe.matmul(ps[:, 2 + g, :], hks[:, h, :], vms[:, 4 * g:4 * g + 4, :], start=True, stop=True)
                ins.then_inc(sem("ds_done"), 1)

            def o_sum():
                pe.wait_ge(sem("o_sq"), 1)
                for tt in range(3):
                    n = P if tt < 2 else TSA
                    ins = pe.matmul(ps[:, 4 + tt, 0:HH * n], ones, hx[0][:, :, tt * P:tt * P + n], start=True, stop=True)
                ins.then_inc(sem("o_sum"), 1)

            def sample_out(g):
                pe.wait_ge(sem("om_ready"), g + 1)
                if g:
                    pe.wait_ge(sem("ob_p"), PAIRS)
                else:
                    pe.wait_ge(sem("state_s"), HH)
                for a in range(PAIRS):
                    ins = pe.matmul(ps[:, (2, 7)[g], a * 16:(a + 1) * 16], om[:, 2 * a:2 * a + 2, :], C("sumheads"), start=True, stop=True)
                ins.then_inc(sem("ob_turned"), 1)

            def pa_scores(h):
                rows = slice(64 * (h % 2), 64 * (h % 2) + 64)
                bank = 4 + h % 2
                if h == 0:
                    pe.wait_ge(sem("o_root"), 1)
                if h >= 2:
                    pe.wait_ge(sem("pa_masked"), h - 1)
                qt, kt = proj[rows, AQ + h // 2, :], proj[rows, AK + h // 2, :]
                pe.matmul(ps[:, bank, 0:P], qt[:, 0:P], kt[:, 0:P], start=True, stop=True)
                pe.matmul(ps[:, bank, P:3 * P], qt[:, P:TP], kt[:, 0:TP], start=True, stop=True).then_inc(sem("pa_scored"), 1)

            def pa_turn(h):
                pe.wait_ge(sem("pa_ready"), h + 1)
                if h == 1:
                    pe.wait_ge(sem("state_s"), HH)
                if h >= 2:
                    pe.wait_ge(sem("paT_ready"), h - 1)
                for c in range(3):
                    ins = pe.transpose(ps[:, TURN[h % 2], c * P:(c + 1) * P], pa[:, h % 2, c * P:(c + 1) * P], ident)
                ins.then_inc(sem("pa_turned"), 1)

            def pa_values(h):
                pe.wait_ge(sem("paT_ready"), h + 1)
                if h == 0:
                    pe.wait_ge(sem("state_p"), 1)
                if h >= 2 and h % 2 == 0:
                    pe.wait_ge(sem("ob_p"), h // 2)
                rows = slice(64 * (h % 2), 64 * (h % 2) + 64)
                v = lambda tt: vtok[:, tt, h * DH:(h + 1) * DH]
                pe.matmul(ps[rows, 7, 0:P], v(0), paT[:, 0:P], start=True, stop=True)
                pe.matmul(ps[rows, 7, P:TP], v(0), paT[:, P:2 * P], start=True, stop=False)
                pe.matmul(ps[rows, 7, P:TP], v(1), paT[:, 2 * P:3 * P], start=False, stop=True).then_inc(sem("pv_done"), 1)

            pe.wait_ge(sem("v_tok"), 1)
            between = {6: [turn_hgrn], 24: [hgrn_states]}
            for gi in range(8):
                between[8 + 2 * gi] = [lambda gi=gi: gram(gi)]
            for u in range(4 * NSEQ):
                cached_keys(u)
                for step in between.get(u, ()):
                    step()

            pe.wait_ge(sem("gate_parts"), NSEQ)
            pe.matmul(ps[:, 1, 0:64], fold, stat[:, 0:64], start=True, stop=True).then_inc(sem("gate_sum"), 1)
            hgrn_out()
            pe.wait_ge(sem("row_max"), 1)
            pe.matmul(ps[:, 1, 64:72], fold[0:32, :], stat[0:32, 256:264], start=True, stop=True).then_inc(sem("max_spread"), 1)
            hgrn_sample_out()

            after = {(0, 3): lambda: probs_sum(), (1, 1): lambda: sample_states(0), (1, 3): lambda: sample_states(1),
                     (2, 0): lambda: sample_states(2), (2, 1): lambda: o_sum(), (2, 3): lambda: sample_states(3)}

            def probs_sum():
                pe.wait_ge(sem("s_exp"), NSEQ)
                pe.matmul(ps[:, 1, 128:136], fold, stat[:, 320:328], start=True, stop=True).then_inc(sem("probs_sum"), 1)

            def prompt_step(k):
                if 1 <= k <= AH:
                    pa_turn(k - 1)
                if k < AH:
                    pa_scores(k)
                if 2 <= k <= AH + 1:
                    pa_values(k - 2)

            k = 0
            for b in range(NSEQ):
                for j in range(4):
                    values(b, j)
                    if (b, j) in after:
                        after[b, j]()
                    if j % 2 == 1 and b >= 3 and k < AH + 2:
                        prompt_step(k)
                        k += 1
                    if (b, j) == (4, 3):
                        sample_out(0)
            sample_out(1)

            for cg in range(2):
                for j, (x_hi, x_lo) in enumerate(((oa_hi, oa_lo), (ob_hi, ob_lo))):
                    w = 46 + 2 * cg + j
                    if cg == 0:
                        pe.wait_ge(sem("oab_lo"), j + 1)
                        if j:
                            pe.wait_ge(sem("ob_s"), 2)
                    else:
                        pe.wait_ge(sem("gated"), 2 * (cg - 1) + j + 1)
                    dense(w, w % 2, x_hi, x_lo, 0, True, True, "ab_tiles", 4 * j)
            pe.wait_ge(sem("gated"), 3)
            pe.wait_ge(sem("m_lo"), 1)

            def sum_squares(src, which, first, last, bank, done):
                for k in which:
                    ins = pe.matmul(ps[:, bank, 0:T], ones, src[:, k, :], start=k == first, stop=k == last)
                if which[-1] == last:
                    ins.then_inc(sem(done), 1)

            y1sq = proj[:, 8:16, :]
            dense(50, 0, m_hi, m_lo, 0, True, False, "y1_done")
            pe.wait_ge(sem("m_lo"), 2)
            dense(51, 1, m_hi, m_lo, 4, False, True, "y1_done")
            dense(52, 0, m_hi, m_lo, 0, True, False, "y1_done", free=("y1_out", 0))
            pe.wait_ge(sem("y1_sq"), 1)
            sum_squares(y1sq, range(0, 4), 0, 7, 4, "y1_sum")
            dense(53, 1, m_hi, m_lo, 4, False, True, "y1_done")
            pe.wait_ge(sem("y1_sq"), 2)
            sum_squares(y1sq, range(4, 8), 0, 7, 4, "y1_sum")
            pe.wait_ge(sem("x1_sq"), 1)
            sum_squares(sq, range(0, 8), 0, 7, 5, "x1_sum")
            pe.wait_ge(sem("h_lo"), 2)

            pe.wait_ge(sem("y1_out"), 8)
            dense(54, 0, h_hi, h_lo, 0, True, False, "gu_done")
            dense(55, 1, h_hi, h_lo, 4, False, True, "gu_done")
            pe.wait_ge(sem("root"), 3)
            with pe.Fori(0, 5) as i:
                pe.wait_ge(sem("fu_ready"), i * 2 + 1)
                dense(i * 4 + 56, 0, h_hi, h_lo, 0, True, False, "gu_done", 4)
                dense(i * 4 + 57, 1, h_hi, h_lo, 4, False, True, "gu_done", 4)
                pe.wait_ge(sem("fu_ready"), i * 2 + 2)
                dense(i * 4 + 58, 0, h_hi, h_lo, 0, True, False, "gu_done")
                dense(i * 4 + 59, 1, h_hi, h_lo, 4, False, True, "gu_done")
            for cg in range(2):
                for c in range(6):
                    w = 76 + 6 * cg + c
                    if cg == 0:
                        pe.wait_ge(sem("f_lo"), min(2 * c + 3, 12))
                        if c == 0:
                            pe.wait_ge(sem("fu_ready"), 11)
                    elif c == 0:
                        pe.wait_ge(sem("fu_ready"), 12)
                    dense(w, w % 2, f_hi, f_lo, 4 * c, c == 0, c == 5, "y2_done", 4 * (1 - cg), rows=2 if c == 5 else BK)
                    if cg == 1 and c == 1:
                        pe.wait_ge(sem("y2_sq"), 1)
                        sum_squares(sq, range(0, 4), 0, 7, 4, "y2_sum")
            pe.wait_ge(sem("y2_sq"), 2)
            sum_squares(sq, range(4, 8), 0, 7, 4, "y2_sum")
            pe.wait_ge(sem("x2_ready"), 1)
            pe.wait_ge(sem("y2_out"), 8)
            pe.wait_ge(sem("root"), 4)
            for tt, b0 in ((0, 0), (1, 2), (2, 5)):
                rows = P if tt < 2 else TSA
                for k in range(DT):
                    ins = pe.transpose(ps[0:rows, b0 + k // 4, (k % 4) * P:(k % 4 + 1) * P], xT[:, k, tt * P:tt * P + rows], ident)
                ins.then_inc(sem("y_turned"), 1)


INPUTS = ["x_prompt", "x_sample", "c_prompt", "c_sample", "state_hgrn", "cache_k", "cache_v", "page_table", "hg_lb",
          "w_ada", "b_ada", "g_pre1", "g_post1", "w_in", "g_onorm", "w_proj_a", "w_proj_b", "w_out", "g_pre2", "g_post2",
          "w_gu", "w_down"]
OUTPUTS = {
    "y_prompt": (1, TP, D), "y_sample": (NSEQ, TS, D),
    "state_p": (1, 1, HH, DK, DK), "state_s": (1, NSEQ, HH, DK, DK),
    "k_prompt": (1, 1, TP, AH, DH), "v_prompt": (1, 1, TP, AH, DH),
    "k_sample": (1, NSEQ, TS, AH, DH), "v_sample": (1, NSEQ, TS, AH, DH),
}


def kernel(**inputs):
    import concourse.bacc as bacc
    from concourse.bass_utils import run_bass_kernel_spmd

    nc = bacc.Bacc("TRN2", target_bir_lowering=False, num_devices=1)
    arrays = {k: np.ascontiguousarray(inputs[k]) for k in INPUTS}
    arrays["cache_k"] = arrays["cache_k"].reshape(1, -1, PAGE, AH * DH)
    arrays["cache_v"] = arrays["cache_v"].reshape(1, -1, PAGE, AH * DH)
    arrays["const"] = constants()[0]
    arrays["lvl"] = level_masks()
    inp = {k: nc.dram_tensor(k, a.shape, mybir.dt.from_np(a.dtype), kind="ExternalInput").ap() for k, a in arrays.items()}
    out = {k: nc.dram_tensor("out_" + k, s, F32, kind="ExternalOutput").ap() for k, s in OUTPUTS.items()}
    build(nc, inp, out)
    r = run_bass_kernel_spmd(nc, [arrays], core_ids=[0]).results[0]
    return tuple(r["out_" + k] for k in OUTPUTS)
```

```python
from contextlib import ExitStack

import numpy as np
import concourse.bass as bass
from concourse import mybir

F32 = mybir.dt.float32
F32R = mybir.dt.float32r
I32 = mybir.dt.int32
U8 = mybir.dt.uint8
ALU = mybir.AluOpType
ACT = mybir.ActivationFunctionType
AX = mybir.AxisListType.X

P = 128
D = 1024
DT = D // P
TP = 256
NSEQ, TS = 8, 4
TSA = NSEQ * TS
T = TP + TSA
CC = 1 + NSEQ
HH, DK = 4, 128
AH, DH = 8, 64
PAIRS = AH // 2
PAST, PAGE = 2048, 128
NPG = PAST // PAGE
MB = 256
NB = PAST // MB
TOPK = 3
DFF = 2816
EPS = 1e-6
NEG = -1.0e30
INW = 5632
PT_ = INW // P
HQ, HF, HI, HG, AQ, AK, AV, UA, UB = 0, 4, 8, 12, 16, 20, 24, 28, 36
NSLOT = 4
BK = 4
BC = 512
SW = (NPG + 1) * 32
WQ = 17 * P
LEVELS = [64, 32, 16, 8, 4, 2, 1]

R_ADA, R_PRE1, R_POST1, R_PRE2, R_POST2, R_LB, R_ON, R_ALL = 0, 48, 56, 64, 72, 80, 88, 89


def constants():
    p = np.arange(P)
    c = {}
    c["ident"] = np.eye(P)
    c["foldc"] = np.zeros((P, CC))
    for i in range(2 * CC):
        c["foldc"][i, i % CC] = 1
    c["ones"] = np.ones((P, P))
    c["eps"] = np.full((P, 1), EPS)
    c["fold"] = (p[:, None] % 32 == p[None, :] % 32).astype(float)
    swap = np.zeros((P, P))
    swap[p ^ 32, p] = 1
    c["swap"] = swap
    for s in range(4):
        c[f"spread{s}"] = c["fold"] * (p[:, None] // 32 == s)
    half = DH // 2
    pos = np.concatenate([np.arange(TP), np.tile(PAST + np.arange(TS), NSEQ)]).astype(np.float32)
    inv = np.float32(10000.0) ** (-np.arange(half, dtype=np.float32) / np.float32(half))
    ang = pos[None, :] * inv[p % half][:, None]
    c["cos"] = np.cos(ang)
    c["sin"] = np.sin(ang) * np.where(p % DH < half, -1.0, 1.0)[:, None]
    start = np.ones(T)
    start[[0, P]] = 0
    start[TP::TS] = 0
    c["carry"] = np.tile(start, (P, 1))
    c["causal"] = np.where(p[None, :] <= p[:, None], 0.0, NEG)
    own = np.full((P, NSEQ, TSA), NEG)
    for r in range(32):
        for b in range(NSEQ):
            for k in range(r % TS + 1):
                own[r, b, b * TS + k] = 0
    c["own"] = own.reshape(P, -1)
    tie = (np.arange(NB)[None, :] < np.arange(NB)[:, None]).astype(float)
    c["tie"] = np.tile(tie.reshape(1, -1), (P, 1))
    c["ownhead"] = (p[:, None] % 32 // TS == np.arange(AH)[None, :]).astype(float)
    c["sumheads"] = ((p[:, None] // 32 == np.arange(16)[None, :] // TS) & (p[:, None] % TS == np.arange(16)[None, :] % TS)).astype(float)
    c["seq"] = (p[:, None] // TS == np.arange(NSEQ)[None, :]).astype(float)
    at, n = {}, 0
    c["pad"] = np.zeros((P, -sum(v.shape[1] for v in c.values()) % 8))
    for k, v in c.items():
        at[k] = (n, n + v.shape[1])
        n += v.shape[1]
    return np.concatenate(list(c.values()), 1).astype(np.float32), at


def level_masks():
    s, t = np.arange(P)[:, None], np.arange(P)[None, :]
    lv = [(s // (2 * m) == t // (2 * m)) & (s % (2 * m) < m) & (t % (2 * m) >= m) for m in LEVELS]
    return np.stack(lv + [s == t], 1).astype(np.int32)


def build(nc, inp, out):
    _, at = constants()
    NCONST = max(e for _, e in at.values())
    FIRST = at["eps"][1]

    base = (nc.sbuf_base + 31) // 32 * 32
    place = {}

    def sb(name, shape, dt=F32, over=None, off=0):
        nonlocal base
        size = int(np.prod(shape[1:])) * (1 if dt == U8 else 4)
        if over is None:
            o = base
            base += (size + 31) // 32 * 32
        else:
            o = place[over][0] + off
            assert off + size <= place[over][1], (name, off + size, place[over])
        place[name] = (o, size)
        return nc.alloc_sbuf_tensor_at(name, shape, dt, offset=o)

    const = sb("const", [P, NCONST])

    def C(name, rows=P):
        a, e = at[name]
        return const[0:rows, a:e]

    lvl = sb("lvl", [P, 8, P], U8)
    cols = sb("cols", [P, R_ALL])
    modT = sb("modT", [P, 48, CC])
    gain = sb("gain", [P, DT, CC])
    cst = sb("cst", [P, DT, 2 * CC], F32R)
    cs = sb("cs", [P, DT, CC])
    lbt = sb("lbt", [P, 6, HH])
    rs = sb("rs", [P, T])
    xT = sb("xT", [P, DT, T])
    stat = sb("stat", [P, 400])
    nmx = sb("nmx", [P, 2, 2])
    den = sb("den", [P, 2, 2])
    vtok = sb("vtok", [P, 3, AH * DH])
    pgt = sb("pgt", [1, NSEQ * NPG], I32)
    ring = sb("ring", [P, NSLOT, BK * BC])
    sb("split_area", [P, 4 * BK * BC])
    sb("proj_area", [P, PT_, T])
    sb("a_area", [P, 2, DT, T])
    sb("s_area", [P, 2, DT, T])
    hqt = sb("hqt", [P, HH, T])
    hA = sb("hA", [P, 2, HH, P])
    hAs = sb("hAs", [TSA, HH, TSA])
    sb("w_area", [P, 2, WQ])
    TB = T * 4

    w_hi = sb("w_hi", [P, 2, BK, BC], F32R, "split_area")
    w_lo = sb("w_lo", [P, 2, BK, BC], F32R, "split_area", 2 * BK * BC * 4)
    KT = sb("KT", [P, 2, 4, 512], F32, "split_area")
    proj = sb("proj", [P, PT_, T], F32, "proj_area")
    xtok = sb("xtok", [P, 3, D], F32, "proj_area")
    prow = sb("prow", [P, P], F32, "proj_area", 3 * D * 4)
    crow = sb("crow", [CC, D], F32, "proj_area", 3 * D * 4 + P * 4)
    h_hi = sb("h_hi", [P, DT, T], F32R, "a_area")
    h_lo = sb("h_lo", [P, DT, T], F32R, "a_area", DT * TB)
    h32 = sb("h32", [P, DT, T], F32, "s_area")
    sq = sb("sq", [P, DT, T], F32, "s_area", DT * TB)
    arow = sb("arow", [2 * CC, BC], F32, "w_area")
    lvl_i = sb("lvl_i", [P, 8, P], I32, "w_area", BC * 4)
    Qrep = sb("Qrep", [P, PAIRS, 4, TSA], F32, "a_area")
    Qbd = sb("Qbd", [P, PAIRS, NSEQ, 32], F32, "hA")
    ktok = sb("ktok", [P, 3, AH * DH], F32, "a_area", 6144)
    cmp1 = sb("cmp1", [P, NSEQ, NB, NB], F32, "a_area", 6144)
    cmp2 = sb("cmp2", [P, NSEQ, NB, NB], F32, "a_area", 8192)
    S = sb("S", [P, NSEQ, SW], F32, "s_area")
    Wq = sb("Wq", [P, 2, WQ], F32, "w_area")
    Pt = sb("Pt", [P, NSEQ, SW // 32, 32], F32, "a_area")
    hb = sb("hb", [P, HH, T], F32, "split_area", 16384)
    hx = [sb(f"hx{i}", [P, HH, T], F32, "split_area", 16384 + (1 + i) * HH * TB) for i in range(2)]
    D0 = sb("D0", [P, HH, DK], F32, "split_area", 16384 + 3 * HH * TB)
    hkt = sb("hkt", [P, HH, T], F32, "proj_area", AV * TB)
    hktok = sb("hktok", [P, 2, HH, DK], F32, "a_area", 12288)
    hvtok = sb("hvtok", [P, 2, HH, DK], F32, "proj_area", HI * TB)
    hks = sb("hks", [TSA, HH, DK], F32, "proj_area", AV * TB)
    hvs = sb("hvs", [TSA, HH, DK], F32, "proj_area", AV * TB + 2048)
    S0 = sb("S0", [P, NSEQ, HH, DK], F32, "w_area")
    Sfin = sb("Sfin", [P, HH, DK], F32, "s_area", 2 * HH * TB)
    vms = sb("vms", [TSA, NSEQ, DK], F32, "s_area", 2 * HH * TB + 2048)
    om = sb("om", [P, AH, DH], F32, "s_area", 3 * HH * TB)
    pa = sb("pa", [P, 2, 384], F32, "proj_area", HF * TB)
    paT = sb("paT", [P, 384], F32, "proj_area", HF * TB + 3072)
    oa_hi = sb("oa_hi", [P, HH, T], F32R, "s_area")
    oa_lo = sb("oa_lo", [P, HH, T], F32R, "s_area", HH * TB)
    ob_hi = sb("ob_hi", [P, PAIRS, T], F32R, "s_area", 2 * HH * TB)
    ob_lo = sb("ob_lo", [P, PAIRS, T], F32R, "s_area", 3 * HH * TB)
    m_hi = sb("m_hi", [P, DT, T], F32R, "a_area")
    m_lo = sb("m_lo", [P, DT, T], F32R, "a_area", DT * TB)
    f_hi = sb("f_hi", [P, DFF // P, T], F32R, "proj_area")
    f_lo = sb("f_lo", [P, DFF // P, T], F32R, "proj_area", DFF // P * TB)
    y2 = sb("y2", [P, DT, T], F32, "w_area")
    fa = sb("fa", [P, 2, T], F32, "w_area", DT * TB)
    fu = sb("fu", [P, 2, T], F32, "w_area", DT * TB + 2 * TB)
    ytok = sb("ytok", [P, 3, D], F32, "s_area")
    assert base <= nc.sbuf_usable_end, base

    ps = nc.alloc_psum_tensor("ps", [P, 8, 512], F32)
    made = {}

    def sem(name):
        if name not in made:
            made[name] = nc.alloc_semaphore(name)
        return made[name]

    def over(ap, axis, n):
        a = ap.unsqueeze(axis)
        shape = list(a.shape)
        shape[axis] = n
        return a.broadcast_to(shape)

    ident, ones, fold = C("ident"), C("ones"), C("fold")
    pools = {k: inp[k] for k in ("cache_k", "cache_v")}
    NA = 46
    SAMP = slice(TP, T)
    YB = (0, 2, 5)

    A_ORDER = [("ada", g) for g in range(4)] + [("in", 0)]
    for i in range(7):
        A_ORDER += [("ada", 4 + i), ("in", 1 + i)]
    A_ORDER += [("ada", 11), ("in", 8), ("in", 9), ("in", 10)]
    KV_SLOT = [(NA + j) % NSLOT for j in range(4)]
    B0 = NA + 64

    def w_src(name, row, col, rows=BK * P, width=BC):
        return inp[name][0, bass.ds(row, rows), bass.ds(col, width)].rearrange("(k p) n -> p k n", p=P)

    def slot4(s):
        return ring[:, s, :].rearrange("p (k n) -> p k n", n=BC)

    def load_pages(queue, pool, b, j, which, landed):
        for q in which:
            pg = queue.value_load(pgt[0:1, bass.ds(b * NPG + (4 * j + q), 1)], min_val=0, max_val=pools[pool].shape[1] - 1)
            queue.dma_start(ring[:, KV_SLOT[j], q * 512:(q + 1) * 512], pools[pool][0, bass.ds(pg, 1), :, :].rearrange("o p n -> p (o n)"))\
                .then_inc(sem(f"{landed}{j}"), 16)

    block = nc.Block()
    with block:

        @block.sync
        def _(sp):
            sp.dma_start(crow[0:1, :], inp["c_prompt"]).then_inc(sem("c_landed"), 16)
            sp.dma_start(crow[1:CC, :], inp["c_sample"]).then_inc(sem("c_landed"), 16)
            n = 0
            for kind, g in A_ORDER[:5]:
                for k in range(2):
                    if n == 2:
                        sp.dma_start(xtok[:, 0:2, :], inp["x_prompt"][0].rearrange("(t p) d -> p t d", p=P)).then_inc(sem("x_landed"), 16)
                        sp.dma_start(xtok[0:TSA, 2, :], inp["x_sample"].rearrange("b t d -> (b t) d")).then_inc(sem("x_landed"), 16)
                    if n >= NSLOT:
                        sp.wait_ge(sem("lo_split"), 2 * (n - NSLOT + 1))
                    sp.dma_start(slot4(n % NSLOT), w_src("w_" + kind, k * BK * P, g * BC)).then_inc(sem(f"w_landed{n % NSLOT}"), 16)
                    n += 1
            with sp.Fori(0, 7) as i:
                for j, (kind, g0, k) in enumerate([("ada", 4, 0), ("ada", 4, 1), ("in", 1, 0), ("in", 1, 1)]):
                    s = (n + j) % NSLOT
                    sp.wait_ge(sem("lo_split"), i * 8 + 2 * (n + j - NSLOT + 1))
                    sp.dma_start(slot4(s), w_src("w_" + kind, k * BK * P, (i + g0) * BC)).then_inc(sem(f"w_landed{s}"), 16)
            n += 28
            for kind, g in A_ORDER[19:]:
                for k in range(2):
                    sp.wait_ge(sem("lo_split"), 2 * (n - NSLOT + 1))
                    sp.dma_start(slot4(n % NSLOT), w_src("w_" + kind, k * BK * P, g * BC)).then_inc(sem(f"w_landed{n % NSLOT}"), 16)
                    n += 1
            assert n == NA

            sp.wait_ge(sem("table_landed"), 16)
            for j in range(4):
                sp.wait_ge(sem("lo_split"), 2 * (NA - NSLOT + j + 1))
                load_pages(sp, "cache_k", 0, j, range(3), "k_landed")
            with sp.Fori(1, NSEQ) as b:
                for j in range(4):
                    sp.wait_ge(sem("key_slots"), b * 4 + (j - 3))
                    load_pages(sp, "cache_k", b, j, range(3), "k_landed")
            for j in range(4):
                sp.wait_ge(sem("key_slots"), 4 * NSEQ - 3 + j)
                load_pages(sp, "cache_v", 0, j, range(2), "v_landed")
            sp.wait_ge(sem("kt_used"), 4 * NSEQ)
            for g in range(4):
                sp.dma_start(S0[:, 2 * g:2 * g + 2], inp["state_hgrn"][0, 2 * g:2 * g + 2].rearrange("b h d e -> d b h e")).then_inc(sem("s0_landed"), 16)
            with sp.Fori(1, NSEQ) as b:
                for j in range(4):
                    sp.wait_ge(sem("value_slots"), b * 4 + (j - 3))
                    load_pages(sp, "cache_v", b, j, range(2), "v_landed")
            n = B0
            for cg in range(2):
                for name in ("w_proj_a", "w_proj_b"):
                    sp.wait_ge(sem("value_slots"), n - NSLOT - (NA + 32) + 1)
                    sp.dma_start(slot4(n % NSLOT), w_src(name, 0, cg * BC)).then_inc(sem(f"w_landed{n % NSLOT}"), 16)
                    n += 1
            for cg in range(2):
                for k in range(2):
                    sp.wait_ge(sem("lo_split"), 2 * (n - NSLOT - 64 + 1))
                    sp.dma_start(slot4(n % NSLOT), w_src("w_out", k * BK * P, cg * BC)).then_inc(sem(f"w_landed{n % NSLOT}"), 16)
                    n += 1

            def load_gu(n_of, s, g, k):
                sp.wait_ge(sem("lo_split"), n_of * 2)
                for half in range(2):
                    sp.dma_start(slot4(s)[:, :, half * 256:(half + 1) * 256], w_src("w_gu", k * BK * P, half * DFF + g * 256, width=256))\
                        .then_inc(sem(f"gu_landed{s}"), 16)

            for k in range(2):
                load_gu(n - NSLOT - 64 + 1, n % NSLOT, 0, k)
                n += 1
            with sp.Fori(0, 5) as i:
                for j in range(4):
                    load_gu(i * 4 + (n + j - NSLOT - 64 + 1), (n + j) % NSLOT, i * 2 + (1 + j // 2), j % 2)
            n += 20
            for cg in range(2):
                for c in range(6):
                    rows = min(BK, DFF // P - BK * c)
                    sp.wait_ge(sem("lo_split"), 2 * (n - NSLOT - 64 + 1))
                    sp.dma_start(slot4(n % NSLOT)[:, 0:rows, :], w_src("w_down", c * BK * P, cg * BC, rows=rows * P))\
                        .then_inc(sem(f"w_landed{n % NSLOT}"), 16)
                    n += 1
            for half in range(2):
                c = slice(half * 512, half * 512 + 512)
                for tt in (0, 2, 1):
                    sp.wait_ge(sem("y_tok1" if tt == 1 else "y_tok02"), half + 1 if tt == 1 else 2 * half + 1 + tt // 2)
                    if tt < 2:
                        sp.dma_start(out["y_prompt"][0, tt * P:(tt + 1) * P, c], ytok[:, tt, c]).then_inc(sem("y_stored"), 16)
                    else:
                        sp.dma_start(out["y_sample"].rearrange("b t d -> (b t) d")[:, c], ytok[0:TSA, 2, c]).then_inc(sem("y_stored"), 16)
            sp.wait_ge(sem("y_stored"), 96)

        @block.gpsimd
        def _(pool):
            pool.dma_start(prow[R_ADA:R_ADA + 48, :], inp["b_ada"].rearrange("o (r n) -> (o r) n", n=P)).then_inc(sem("par_landed"), 16)
            for r, name in ((R_PRE1, "g_pre1"), (R_POST1, "g_post1"), (R_PRE2, "g_pre2"), (R_POST2, "g_post2")):
                pool.dma_start(prow[r:r + 8, :], inp[name].rearrange("o (r n) -> (o r) n", n=P)).then_inc(sem("par_landed"), 16)
            pool.dma_start(prow[R_LB:R_LB + 8, :], inp["hg_lb"].rearrange("o (r n) -> (o r) n", n=P)).then_inc(sem("par_landed"), 16)
            pool.dma_start(prow[R_ON:R_ON + 1, :], inp["g_onorm"]).then_inc(sem("par_landed"), 16)
            pool.dma_start(pgt[:, :], inp["page_table"].rearrange("(o a) b -> o (a b)", o=1)).then_inc(sem("table_landed"), 16)
            pool.dma_start(const[:, FIRST:], inp["const"][:, FIRST:]).then_inc(sem("const1_landed"), 16)
            pool.dma_start(lvl_i[:, :, :], inp["lvl"]).then_inc(sem("lvl_landed"), 16)

            def h_lower(time):
                for k in range(DT):
                    pool.wait_ge(sem("h_hi"), time * DT + k + 1)
                    pool.tensor_tensor(h_lo[:, k, :], h32[:, k, :], h_hi[:, k, :].bitcast(F32), ALU.subtract).then_inc(sem("h_lo"), 1)

            pool.wait_ge(sem("x_sq"), 1)
            for i, n in enumerate((4, 2, 1)):
                if i:
                    pool.wait_ge(sem("x_folded"), i)
                pool.tensor_tensor(sq[:, 0:n, :], sq[:, 0:n, :], sq[:, n:2 * n, :], ALU.add).then_inc(sem("x_folded"), 1)
            pool.wait_ge(sem("lo_split"), 16)
            for half in range(2):
                pool.wait_ge(sem("hi_split"), 16 + half + 1)
                k = slice(half * 2, half * 2 + 2)
                pool.tensor_tensor(w_lo[:, 0, k, :], slot4(0)[:, k, :], w_hi[:, 0, k, :].bitcast(F32), ALU.subtract).then_inc(sem("lo_split"), 1)
            h_lower(0)
            pool.wait_ge(sem("lvl_landed"), 16)
            pool.tensor_copy(lvl[:, :, :], lvl_i[:, :, :]).then_inc(sem("lvl_ready"), 1)
            pool.wait_ge(sem("lvl_ready"), 1)
            pool.wait_ge(sem("mod_rows_turned"), 12)
            pool.memset(Wq[:, :, :], 0.0).then_inc(sem("wq_zero"), 1)
            pool.wait_ge(sem("wq_zero"), 1)
            pool.wait_ge(sem("v_tok"), 1)
            pool.dma_start(out["v_prompt"][0, 0].rearrange("(t p) h d -> p t (h d)", p=P), vtok[:, 0:2, :]).then_inc(sem("v_stored"), 16)
            pool.dma_start(out["v_sample"][0].rearrange("b t h d -> (b t) (h d)"), vtok[0:TSA, 2, :]).then_inc(sem("v_stored"), 16)

            def queries(b, levels=0):
                if b >= 2:
                    pool.wait_ge(sem("kt_used"), 4 * (b - 1))
                for a in range(4):
                    rows = slice(32 * a, 32 * a + 32)
                    step = 2 * P + TS
                    dst = Wq[rows, b % 2, a * 32:a * 32 + AH * step].rearrange("p (h x) -> p h x", x=step)[:, :, 0:2 * P]
                    if a == 0 and b >= 2:
                        pool.wait_ge(sem("lv_diff"), min(levels + 2, 7))
                        if levels:
                            pool.wait_ge(sem("lv_ready"), levels)
                    ins = pool.tensor_copy(dst.rearrange("p h (c y) -> p h c y", y=P)[:, :, :, 0:TS],
                                           Qrep[rows].rearrange("p a s t -> p (a s) t").rearrange("p (h c) t -> p h c t", c=2)[:, :, :, b * TS:(b + 1) * TS])
                ins.then_inc(sem("wq_ready"), 1)
                pool.wait_ge(sem("wq_ready"), b + 1)

            def diff(li):
                m, x = LEVELS[li], hx[li % 2]
                r = TP if m > 2 else T
                bv = hb[:, :, 0:r].rearrange("p h (n k) -> p h n k", k=2 * m)
                xv = x[:, :, 0:r].rearrange("p h (n k) -> p h n k", k=2 * m)
                mid = bv[:, :, :, m - 1:m].broadcast_to([P, HH, r // (2 * m), m])
                if li >= 2:
                    pool.wait_ge(sem("gram_done"), li)
                pool.tensor_tensor(xv[:, :, :, m:2 * m], bv[:, :, :, m:2 * m], mid, ALU.subtract)
                pool.tensor_tensor(xv[:, :, :, 0:m], mid, bv[:, :, :, 0:m], ALU.subtract).then_inc(sem("lv_diff"), 1)

            def scale_level(li):
                m, x = LEVELS[li], hx[li % 2]
                r = TP if m > 2 else T
                pool.wait_ge(sem("lv_exp"), li + 1)
                for half, src in ((1, proj[:, HQ:HQ + 4, :]), (0, proj[:, HF:HF + 4, :])):
                    sv = src[:, :, 0:r].rearrange("p h (n k) -> p h n k", k=2 * m)[:, :, :, half * m:half * m + m]
                    xv = x[:, :, 0:r].rearrange("p h (n k) -> p h n k", k=2 * m)[:, :, :, half * m:half * m + m]
                    ins = pool.tensor_tensor(xv, xv, sv, ALU.mult)
                ins.then_inc(sem("lv_ready"), 1)

            pool.wait_ge(sem("q_spread"), 1)
            queries(0)
            queries(1)
            pool.wait_ge(sem("b_ready"), 1)
            diff(0)
            diff(1)
            queries(2)
            pool.wait_ge(sem("kin_ready"), 1)
            for li in range(7):
                scale_level(li)
                if li + 2 < 7:
                    diff(li + 2)
                if li % 2 == 0:
                    queries(3 + li // 2, li + 1)
            queries(7, 7)
            for j in range(4):
                pool.wait_ge(sem("key_slots"), 4 * NSEQ - 3 + j)
                load_pages(pool, "cache_v", 0, j, [3], "v3_landed")
            with pool.Fori(1, NSEQ) as b:
                for j in range(4):
                    pool.wait_ge(sem("value_slots"), b * 4 + (j - 3))
                    load_pages(pool, "cache_v", b, j, [3], "v3_landed")
            pool.wait_ge(sem("v_stored"), 32)
            pool.wait_ge(sem("k_stored"), 32)
            h_lower(1)

        @block.scalar
        def _(act):
            step = [0]

            def link(ins):
                step[0] += 1
                ins.then_inc(sem("act_step"), 1)
                act.wait_ge(sem("act_step"), step[0])

            act.dma_start(const[:, 0:FIRST], inp["const"][:, 0:FIRST]).then_inc(sem("const0_landed"), 16)

            act.wait_ge(sem("rows_turned"), 1)
            link(act.activation(cs[:, :, :], ps[:, 7, 0:DT * CC].rearrange("p (k c) -> p k c", c=CC), ACT.Silu))
            act.activation(cst[:, :, 0:CC], cs[:, :, :], ACT.Copy).then_inc(sem("c_hi"), 1)

            def hi(w, landed, s, count, par, rows=BK):
                act.wait_ge(sem(f"{landed}{s}"), count)
                for half in range(2):
                    if not isinstance(w, int) or w >= 2:
                        act.wait_ge(sem("w_used"), w * 2 + (half - 3))
                    k = slice(half * rows // 2, (half + 1) * rows // 2)
                    act.activation(w_hi[:, par, k, :], slot4(s)[:, k, :], ACT.Copy).then_inc(sem("hi_split"), 1)

            def hi_a(n):
                hi(n, "w_landed", n % NSLOT, 16 * (n // NSLOT + 1), n % 2)

            def evac_ada(g, w):
                act.wait_ge(sem("w_used"), w * 2 + 2)
                if not isinstance(g, int) or g >= 1:
                    act.wait_ge(sem("mod_rows_turned"), g)
                act.activation(arow[:, :], ps[0:2 * CC, 4, :], ACT.Copy).then_inc(sem("ada_rows"), 1)

            def evac_in(g, w):
                for j in range(4):
                    if j < 3:
                        act.wait_ge(sem("tile_done"), g * 3 + (j + 1))
                    else:
                        act.wait_ge(sem("w_used"), w * 2 + 2)
                    act.activation(proj[:, bass.ds(g * 4 + j, 1), :], ps[:, j:j + 1, 0:T], ACT.Copy).then_inc(sem("tile_out"), 1)

            def h_upper(time):
                for k in range(DT):
                    act.wait_ge(sem("h_ready"), time * DT + k + 1)
                    act.activation(h_hi[:, k, :], h32[:, k, :], ACT.Copy).then_inc(sem("h_hi"), 1)

            hi_a(0)
            hi_a(1)
            for k in range(0, DT, 2):
                act.wait_ge(sem("x_turned"), k + 2)
                act.activation(xT[:, k:k + 2, :], ps[:, k % 4:k % 4 + 2, 0:T], ACT.Copy).then_inc(sem("x_ready"), 1)
            act.wait_ge(sem("rows_turned"), 2)
            act.activation(cols[:, :], ps[:, 6, 0:R_ALL], ACT.Copy).then_inc(sem("cols_ready"), 1)
            for g in range(1, 4):
                hi_a(2 * g)
                evac_ada(g - 1, 2 * g - 1)
                hi_a(2 * g + 1)
                if g == 2:
                    act.wait_ge(sem("x_sum"), 1)
                    act.wait_ge(sem("const0_landed"), 16)
                    act.activation(rs[:, :], ps[:, 7, 0:T], ACT.Sqrt, scale=1.0 / D, bias=C("eps")).then_inc(sem("root"), 1)
            hi_a(8)
            evac_ada(3, 7)
            h_upper(0)
            hi_a(9)
            with act.Fori(0, 7) as i:
                hi(i * 4 + 10, "w_landed", 2, i * 16 + 48, 0)
                evac_in(i, i * 4 + 9)
                hi(i * 4 + 11, "w_landed", 3, i * 16 + 48, 1)
                hi(i * 4 + 12, "w_landed", 0, i * 16 + 64, 0)
                evac_ada(i + 4, i * 4 + 11)
                hi(i * 4 + 13, "w_landed", 1, i * 16 + 64, 1)
            act.wait_ge(sem("lb_arg"), 1)
            act.activation(lbt[:, 1:3, :], lbt[:, 1:3, :], ACT.Exp).then_inc(sem("lb_exp"), 1)
            hi_a(38)
            evac_in(7, 37)
            hi_a(39)
            hi_a(40)
            evac_ada(11, 39)
            hi_a(41)
            hi_a(42)
            evac_in(8, 41)
            hi_a(43)

            def keys(b, *blocks):
                for j in blocks:
                    if b == 0:
                        act.wait_ge(sem("lo_split"), 2 * (NA - NSLOT + j + 1))
                    else:
                        act.wait_ge(sem("key_slots"), 4 * b + j - 3)
                    load_pages(act, "cache_k", b, j, [3], "k_landed")

            hi_a(44)
            act.wait_ge(sem("table_landed"), 16)
            keys(0, 0)
            evac_in(9, 43)
            hi_a(45)
            act.wait_ge(sem("v_turned"), 1)
            act.activation(vtok[:, 0:2, :], ps[:, 4:6, :], ACT.Copy)
            act.activation(vtok[0:TSA, 2, :], ps[0:TSA, 6, :], ACT.Copy).then_inc(sem("v_tok"), 1)
            keys(0, 1)
            act.activation(proj[:, HF:HF + 4, :], proj[:, HF:HF + 4, :], ACT.Sigmoid).then_inc(sem("sig_f"), 1)
            keys(0, 2)
            evac_in(10, 45)
            keys(0, 3)
            act.wait_ge(sem("k_turned_tok"), 1)
            act.activation(ktok[:, 0:2, :], ps[:, 4:6, :], ACT.Copy)
            act.activation(ktok[0:TSA, 2, :], ps[0:TSA, 6, :], ACT.Copy).then_inc(sem("k_tok"), 1)
            act.wait_ge(sem("k_tok"), 1)
            act.dma_start(out["k_prompt"][0, 0].rearrange("(t p) h d -> p t (h d)", p=P), ktok[:, 0:2, :]).then_inc(sem("k_stored"), 16)
            act.dma_start(out["k_sample"][0].rearrange("b t h d -> (b t) (h d)"), ktok[0:TSA, 2, :]).then_inc(sem("k_stored"), 16)
            act.activation(proj[:, UA:UA + 16, :], proj[:, UA:UA + 16, :], ACT.Sigmoid).then_inc(sem("sig_u"), 1)
            act.activation(proj[:, HG:HG + 4, :], proj[:, HG:HG + 4, :], ACT.Silu).then_inc(sem("silu_g"), 1)

            act.wait_ge(sem("f_ready"), 1)
            act.activation(hkt[:, :, :], proj[:, HF:HF + 4, :], ACT.Ln).then_inc(sem("logf"), 1)
            keys(1, 0, 1)
            act.wait_ge(sem("b_ready"), 1)
            act.activation(hqt[:, :, :], hb[:, :, :], ACT.Exp).then_inc(sem("eb"), 1)
            keys(1, 2)
            act.wait_ge(sem("kd_ready"), 1)
            act.activation(hkt[:, :, :], hkt[:, :, :], ACT.Exp).then_inc(sem("ekd"), 1)

            def scores(b):
                act.wait_ge(sem("kt_used"), 4 * (b + 1))
                act.activation(S[:, b, 0:512], ps[:, b % 2, :], ACT.Copy).then_inc(sem("scores_out"), 1)

            def level_exp(li):
                r = TP if LEVELS[li] > 2 else T
                act.wait_ge(sem("lv_diff"), li + 1)
                act.activation(hx[li % 2][:, :, 0:r], hx[li % 2][:, :, 0:r], ACT.Exp).then_inc(sem("lv_exp"), 1)

            keys(1, 3)
            level_exp(0)
            keys(2, 0)
            scores(0)
            level_exp(1)
            keys(2, 1, 2, 3)
            act.wait_ge(sem("h_turned"), 1)
            act.activation(hktok[:, :, :, :], ps[:, 2:4, :].rearrange("p t (h d) -> p t h d", h=HH), ACT.Copy)
            act.activation(hvtok[:, :, :, :], ps[:, 4:6, :].rearrange("p t (h d) -> p t h d", h=HH), ACT.Copy)
            act.activation(hks[:, :, :], ps[0:TSA, 6, :].rearrange("p (h d) -> p h d", h=HH), ACT.Copy)
            act.activation(hvs[:, :, :], ps[0:TSA, 7, :].rearrange("p (h d) -> p h d", h=HH), ACT.Copy).then_inc(sem("h_tok"), 1)
            keys(3, 0)
            scores(1)
            for b in range(2, 7):
                if b > 2:
                    keys(b + 1, 0)
                    scores(b - 1)
                    if 2 * b - 3 < 7:
                        level_exp(2 * b - 3)
                keys(b + 1, 1, 2)
                if 2 * b - 2 < 7:
                    level_exp(2 * b - 2)
                keys(b + 1, 3)
            scores(6)

            def value_pages(b, *blocks):
                for j in blocks:
                    if b == 0:
                        act.wait_ge(sem("key_slots"), 4 * NSEQ - 3 + j)
                    else:
                        act.wait_ge(sem("value_slots"), 4 * b + j - 3)
                    load_pages(act, "cache_v", b, j, [2], "v_landed")

            value_pages(0, 0)
            act.wait_ge(sem("d_done"), 1)
            act.activation(D0[:, :, :], ps[:, 2, :].rearrange("p (h d) -> p h d", h=HH), ACT.Copy).then_inc(sem("d0_ready"), 1)
            value_pages(0, 1, 2, 3)
            scores(7)
            act.wait_ge(sem("shift_ready"), 1)
            for b in range(NSEQ):
                act.wait_ge(sem("s_chosen"), b + 1)
                act.activation(S[:, b, :], S[:, b, :], ACT.Exp, bias=stat[:, 304 + b:305 + b], accum_out=stat[:, 320 + b:321 + b]).then_inc(sem("s_exp"), 1)
            value_pages(1, 0, 1, 2, 3)
            value_pages(2, 0, 1, 2)
            act.wait_ge(sem("o_done"), 1)
            for t in range(2):
                act.activation(hb[:, :, t * P:(t + 1) * P], ps[:, 4 + t, :].rearrange("p (h d) -> p h d", h=HH), ACT.Copy)
            link(act.activation(hb[:, :, SAMP], ps[:, 6, 0:HH * TSA].rearrange("p (h d) -> p h d", h=HH), ACT.Copy))
            act.activation(hx[0][:, :, :], hb[:, :, :], ACT.Square).then_inc(sem("o_sq"), 1)
            value_pages(2, 3)
            value_pages(3, 0)
            act.wait_ge(sem("o_sum"), 1)
            for t in range(2):
                act.activation(hx[1][:, :, t * P:(t + 1) * P], ps[:, 4 + t, :].rearrange("p (h d) -> p h d", h=HH), ACT.Sqrt, scale=1.0 / DK, bias=C("eps"))
            act.activation(hx[1][:, :, SAMP], ps[:, 6, 0:HH * TSA].rearrange("p (h d) -> p h d", h=HH), ACT.Sqrt, scale=1.0 / DK, bias=C("eps")).then_inc(sem("o_root"), 1)
            value_pages(3, 1, 2)

            act.wait_ge(sem("state_p"), 1)
            act.dma_start(out["state_p"][0, 0].rearrange("h d e -> d h e"), Sfin[:, :, :]).then_inc(sem("st_stored"), 16)

            def pa_pair(a):
                act.wait_ge(sem("pv_done"), 2 * a + 2)
                act.activation(proj[:, AQ + a, 0:TP], ps[:, 7, 0:TP], ACT.Copy).then_inc(sem("ob_p"), 1)

            for h in range(AH + 1):
                if h == 0:
                    value_pages(3, 3)
                else:
                    value_pages(4 + (h - 1) // 2, 2 * ((h - 1) % 2), 2 * ((h - 1) % 2) + 1)
                if h == 5:
                    act.wait_ge(sem("oa_ready"), HH)
                    act.activation(oa_hi[:, :, :], proj[:, HQ:HQ + 4, :], ACT.Copy).then_inc(sem("oab_hi"), 1)
                if h < AH:
                    act.wait_ge(sem("pa_masked"), h + 1)
                    for t in range(2):
                        a, e = (0, P) if t == 0 else (P, 3 * P)
                        ins = act.activation(pa[:, h % 2, a:e], pa[:, h % 2, a:e], ACT.Exp, bias=nmx[:, h % 2, t:t + 1], accum_out=den[:, h % 2, t:t + 1])
                    ins.then_inc(sem("pa_exp"), 1)
                if h >= 1:
                    act.wait_ge(sem("pa_turned"), h)
                    if h >= 2:
                        act.wait_ge(sem("pv_done"), h - 1)
                    if h >= 3 and h % 2 == 1:
                        pa_pair((h - 3) // 2)
                    act.activation(paT[:, :], ps[:, 6, 0:384], ACT.Copy).then_inc(sem("paT_ready"), 1)
            pa_pair(PAIRS - 1)

            def hi_b(w, rows=BK):
                n = w + 64
                s = n % NSLOT
                before = (NA + NSLOT - 1 - s) // NSLOT + (2 if w >= 76 else 0)
                hi(w, "w_landed", s, 16 * (before + (n - (B0 if w < 76 else 76 + 64)) // NSLOT + 1), w % 2, rows)

            act.wait_ge(sem("oa_ready"), HH)
            hi_b(46)
            act.wait_ge(sem("st_stored"), 16)
            act.wait_ge(sem("ob_p"), PAIRS)
            act.wait_ge(sem("ob_s"), 2)
            act.activation(ob_hi[:, :, :], proj[:, AQ:AQ + 4, :], ACT.Copy).then_inc(sem("oab_hi"), 1)

            def m_split(cg):
                act.wait_ge(sem("merged"), cg + 1)
                act.activation(m_hi[:, 4 * cg:4 * cg + 4, :], proj[:, UA + 4 * cg:UA + 4 * cg + 4, :], ACT.Copy).then_inc(sem("m_hi"), 1)

            def y_evac(cg):
                for j in range(4 * cg, 4 * cg + 4):
                    if j % 4 < 3:
                        act.wait_ge(sem("y1_done"), 3 * cg + j % 4 + 1)
                    else:
                        act.wait_ge(sem("w_used"), 104 + 4 * cg)
                    act.activation(proj[:, j, :], ps[:, j % 4, 0:T], ACT.Copy).then_inc(sem("y1_out"), 1)

            hi_b(47)
            hi_b(48)
            act.wait_ge(sem("state_s"), HH)
            for g in range(4):
                act.dma_start(out["state_s"][0, 2 * g:2 * g + 2].rearrange("b h d e -> d b h e"), S0[:, 2 * g:2 * g + 2]).then_inc(sem("st_stored"), 16)
            m_split(0)
            hi_b(49)
            hi_b(50)
            m_split(1)
            hi_b(51)
            hi_b(52)
            y_evac(0)
            hi_b(53)
            hi(54, "gu_landed", 2, 32, 0)
            y_evac(1)
            hi(55, "gu_landed", 3, 32, 1)
            act.wait_ge(sem("y1_sum"), 1)
            act.activation(rs[:, :], ps[:, 4, 0:T], ACT.Sqrt, scale=1.0 / D, bias=C("eps")).then_inc(sem("root"), 1)
            for k in range(DT):
                act.wait_ge(sem("x1_ready"), k + 1)
                act.activation(sq[:, k, :], xT[:, k, :], ACT.Square).then_inc(sem("x1_sq"), 1)
            act.wait_ge(sem("x1_sum"), 1)
            act.activation(rs[:, :], ps[:, 5, 0:T], ACT.Sqrt, scale=1.0 / D, bias=C("eps")).then_inc(sem("root"), 1)
            h_upper(1)

            def gates(g, base):
                act.wait_ge(sem("gu_done"), g * 3 + 2)
                act.wait_ge(sem("fu_ready"), g + 1)
                act.activation(fa[:, :, :], ps[:, base:base + 2, 0:T], ACT.Silu).then_inc(sem("silu_done"), 1)

            def f_split(g):
                act.wait_ge(sem("fu_ready"), g + 2)
                act.activation(f_hi[:, bass.ds(g * 2, 2), :], fu[:, :, :], ACT.Copy).then_inc(sem("f_hi"), 1)

            act.wait_ge(sem("st_stored"), 80)
            with act.Fori(0, 5) as i:
                hi(i * 4 + 56, "gu_landed", 0, i * 32 + 32, 0)
                gates(i * 2, 0)
                hi(i * 4 + 57, "gu_landed", 1, i * 32 + 32, 1)
                f_split(i * 2)
                hi(i * 4 + 58, "gu_landed", 2, i * 32 + 64, 0)
                gates(i * 2 + 1, 4)
                hi(i * 4 + 59, "gu_landed", 3, i * 32 + 64, 1)
                f_split(i * 2 + 1)

            def hi_d(i):
                hi_b(76 + i, 2 if i % 6 == 5 else BK)

            def y2_evac(cg):
                for j in range(4):
                    if j < 3:
                        act.wait_ge(sem("y2_done"), 3 * cg + j + 1)
                    else:
                        act.wait_ge(sem("w_used"), 164 + 12 * cg)
                    act.activation(y2[:, 4 * cg + j, :], ps[:, 4 * (1 - cg) + j, 0:T], ACT.Copy).then_inc(sem("y2_out"), 1)

            hi_d(0)
            gates(10, 0)
            hi_d(1)
            f_split(10)
            for i in range(2, 7):
                hi_d(i)
            y2_evac(0)
            for i in range(7, 12):
                hi_d(i)
            y2_evac(1)
            act.wait_ge(sem("y2_sum"), 1)
            act.activation(rs[:, :], ps[:, 4, 0:T], ACT.Sqrt, scale=1.0 / D, bias=C("eps")).then_inc(sem("root"), 1)
            for half in range(2):
                act.wait_ge(sem("y_turned"), half + 1)
                act.activation(ytok[:, 0, half * 512:(half + 1) * 512], ps[:, YB[0] + half, :], ACT.Copy).then_inc(sem("y_tok02"), 1)
                act.activation(ytok[0:TSA, 2, half * 512:(half + 1) * 512], ps[0:TSA, YB[2] + half, :], ACT.Copy).then_inc(sem("y_tok02"), 1)

        @block.vector
        def _(dve):
            step = [0]

            def link(ins):
                step[0] += 1
                ins.then_inc(sem("dve_step"), 1)
                dve.wait_ge(sem("dve_step"), step[0])

            def lo(w, s, par, rows=BK):
                for half in range(2):
                    dve.wait_ge(sem("hi_split"), w * 2 + (half + 1))
                    k = slice(half * rows // 2, (half + 1) * rows // 2)
                    dve.tensor_tensor(w_lo[:, par, k, :], slot4(s)[:, k, :], w_hi[:, par, k, :].bitcast(F32), ALU.subtract).then_inc(sem("lo_split"), 1)

            def lo_a(n):
                lo(n, n % NSLOT, n % 2)

            def mod_add(g):
                dve.wait_ge(sem("mod_rows_turned"), g + 1)
                dve.tensor_tensor(modT[:, bass.ds(g * 4, 4), :], ps[:, 5, 0:4 * CC].rearrange("p (k c) -> p k c", c=CC),
                                  over(cols[:, bass.ds(g * 4 + R_ADA, 4)], 2, CC), ALU.add).then_inc(sem("mod_ready"), 1)

            def mark(ins):
                step[0] += 1
                ins.then_inc(sem("dve_step"), 1)
                return step[0]

            def need(n):
                dve.wait_ge(sem("dve_step"), n)

            def normed(dst, src, tmp, g, s, root, done):
                sv = lambda x: x[:, :, SAMP].rearrange("p k (b t) -> p k b t", t=TS)
                link(dve.tensor_tensor(sv(tmp), sv(src), over(g[:, :, 1:CC], 3, TS), ALU.mult))
                if root is None:
                    dve.wait_ge(sem("rs_ready"), 1)
                else:
                    dve.wait_ge(sem("root"), root)
                    link(dve.reciprocal(rs[:, :], rs[:, :]))
                link(dve.tensor_tensor(tmp[:, :, SAMP], tmp[:, :, SAMP], over(rs[:, SAMP], 1, DT), ALU.mult))
                at = mark(dve.tensor_tensor(sv(dst), sv(tmp), sv(dst) if s is None else over(s[:, :, 1:CC], 3, TS), ALU.add))
                t = [mark(dve.tensor_tensor(tmp[:, 0, 0:TP], src[:, 0, 0:TP], rs[:, 0:TP], ALU.mult))]
                for k in range(DT):
                    if k + 1 < DT:
                        t.append(mark(dve.tensor_tensor(tmp[:, k + 1, 0:TP], src[:, k + 1, 0:TP], rs[:, 0:TP], ALU.mult)))
                    need(t[k])
                    if s is None:
                        ins = dve.scalar_tensor_tensor(dst[:, k, 0:TP], tmp[:, k, 0:TP], g[:, k, 0:1], dst[:, k, 0:TP], ALU.mult, ALU.add)
                    else:
                        ins = dve.tensor_scalar(dst[:, k, 0:TP], tmp[:, k, 0:TP], g[:, k, 0:1], s[:, k, 0:1], ALU.mult, ALU.add)
                    ins.then_inc(sem(done), 1)

            def part(k):
                return modT[:, 8 * k:8 * k + 8, :]

            dve.wait_ge(sem("c_hi"), 1)
            dve.tensor_tensor(cst[:, :, CC:2 * CC], cs[:, :, :], cst[:, :, 0:CC].bitcast(F32), ALU.subtract).then_inc(sem("c_lo"), 1)
            lo_a(0)
            lo_a(1)
            dve.wait_ge(sem("x_ready"), DT // 2)
            dve.tensor_tensor(sq[:, :, :], xT[:, :, :], xT[:, :, :], ALU.mult).then_inc(sem("x_sq"), 1)
            for g in range(1, 4):
                lo_a(2 * g)
                lo_a(2 * g + 1)
                if g == 1:
                    dve.wait_ge(sem("cols_ready"), 1)
                mod_add(g - 1)
                if g == 2:
                    dve.wait_ge(sem("root"), 1)
                    dve.reciprocal(rs[:, :], rs[:, :]).then_inc(sem("rs_ready"), 1)
            mod_add(3)
            dve.wait_ge(sem("mod_ready"), 4)
            link(dve.scalar_tensor_tensor(gain[:, :, :], part(1), 1.0, over(cols[:, R_PRE1:R_PRE1 + DT], 2, CC), ALU.add, ALU.mult))
            normed(h32, xT, h32, gain, part(0), None, "h_ready")
            dve.wait_ge(sem("lo_split"), 18)
            lo_a(9)
            with dve.Fori(0, 7) as i:
                lo(i * 4 + 10, 2, 0)
                lo(i * 4 + 11, 3, 1)
                lo(i * 4 + 12, 0, 0)
                lo(i * 4 + 13, 1, 1)
                mod_add(i + 4)
            lb0, lb1 = cols[:, R_LB:R_LB + 4], cols[:, R_LB + 4:R_LB + 8]
            link(dve.tensor_tensor(lbt[:, 0, :], lb0, lb1, ALU.max))
            dve.tensor_tensor(lbt[:, 1, :], lb0, lbt[:, 0, :], ALU.subtract)
            dve.tensor_tensor(lbt[:, 2, :], lb1, lbt[:, 0, :], ALU.subtract).then_inc(sem("lb_arg"), 1)
            for n in range(38, 42):
                lo_a(n)
            mod_add(11)
            lo_a(42)
            cosb, sinb = over(C("cos"), 1, 4), over(C("sin"), 1, 4)
            dve.wait_ge(sem("const1_landed"), 16)
            for j, (t0, scale) in enumerate(((AQ, DH ** -0.5), (AK, 1.0))):
                dve.wait_ge(sem("swapped"), j + 1)
                x = proj[:, t0:t0 + 4, :]
                link(dve.scalar_tensor_tensor(sq[:, 4 * j:4 * j + 4, :], ps[:, 4:8, 0:T], scale, sinb, ALU.mult, ALU.mult))
                dve.nop().then_inc(sem("swap_used"), 1)
                link(dve.scalar_tensor_tensor(x, x, scale, cosb, ALU.mult, ALU.mult))
                dve.tensor_tensor(x, x, sq[:, 4 * j:4 * j + 4, :], ALU.add).then_inc(sem("roped"), 1)
                lo_a(43 + j)
            link(dve.memset(Qbd[:, :, :, :], 0.0))
            dve.wait_ge(sem("roped"), 2)
            for pair in range(PAIRS):
                for hl in range(2):
                    rows = slice(64 * hl, 64 * hl + 64)
                    c = (2 * pair + hl) * TS
                    ins = dve.tensor_copy(Qbd[rows, pair, :, c:c + TS], proj[rows, AQ + pair, SAMP].rearrange("p (b t) -> p b t", t=TS))
            ins.then_inc(sem("q_blocks"), 1)
            lo_a(45)
            dve.wait_ge(sem("lb_exp"), 1)
            link(dve.tensor_tensor(lbt[:, 3, :], lbt[:, 1, :], lbt[:, 2, :], ALU.add))
            link(dve.reciprocal(lbt[:, 3, :], lbt[:, 3, :]))
            link(dve.tensor_tensor(lbt[:, 4, :], lbt[:, 1, :], lbt[:, 3, :], ALU.mult))
            link(dve.tensor_scalar(lbt[:, 5, :], lbt[:, 4, :], -1.0, 1.0, ALU.mult, ALU.add))
            dve.wait_ge(sem("spread_done"), 1)
            dve.wait_ge(sem("w_used"), 2 * NA)
            dve.tensor_copy(Qrep[:, :, :, :].rearrange("p a s t -> p s a t"), ps[:, 7, :].rearrange("p (s a t) -> p s a t", s=4, a=PAIRS)).then_inc(sem("q_spread"), 1)
            dve.wait_ge(sem("own_scored"), 1)
            link(dve.memset(S[:, :, 512:SW], NEG))
            dve.tensor_tensor(S[0:32, :, 512:SW], ps[0:32, 2, 0:256].rearrange("p (b k) -> p b k", b=NSEQ),
                              C("own", 32).rearrange("p (b k) -> p b k", b=NSEQ), ALU.add).then_inc(sem("own_out"), 1)

            def turn_keys(u):
                dve.wait_ge(sem(f"k_landed{u % 4}"), (u // 4 + 1) * 64)
                if u >= 2:
                    dve.wait_ge(sem("kt_used"), u - 1)
                dve.transpose(KT[:, u % 2, :, :], ring[:, KV_SLOT[u % 4], :].rearrange("p (g n) -> p g n", n=512)).then_inc(sem("key_slots"), 1)

            def st(k, n=NSEQ * NB):
                return stat[:, k:k + n]
            gpart, gate, pen, bmax = st(0), st(64), st(128), st(192)
            rmax, lane4, omax, shift = st(256, 8), st(264, 32), st(296, 8), st(304, 8)
            rden, rrow = st(312, 8), st(364, 2)
            bn = "p (b n) -> p b n"
            cached = S[:, :, 0:512].rearrange("p b (n k) -> p b n k", n=NB)

            def block_sums(b):
                dve.wait_ge(sem("scores_out"), b + 1)
                dve.tensor_reduce(gpart[:, b * NB:(b + 1) * NB], cached[:, b], AX, ALU.add).then_inc(sem("gate_parts"), 1)
                dve.tensor_reduce(bmax[:, b * NB:(b + 1) * NB], cached[:, b], AX, ALU.max)

            def keep(gi):
                dve.wait_ge(sem("gram_done"), gi + 1)
                if gi:
                    dve.wait_ge(sem("kept"), gi)
                li = gi - 1
                mask = lvl[:, 7 if gi == 0 else li, :]
                b0 = 2 + 2 * (gi % 2)
                ins = dve.copy_predicated(hA[:, :, :, :].rearrange("p t h s -> p (t h) s"), over(mask, 1, 2 * HH),
                                          ps[:, b0:b0 + 2, :].rearrange("p t (h s) -> p (t h) s", h=HH))
                if gi == 0 or LEVELS[li] <= 2:
                    link(ins)
                    ins = dve.copy_predicated(hAs[:, :, :], over(mask[0:TSA, 0:TSA], 1, HH),
                                              ps[0:TSA, 6 + gi % 2, 0:HH * TSA].rearrange("p (h s) -> p h s", h=HH))
                ins.then_inc(sem("kept"), 1)

            kin, q = proj[:, HF:HF + 4, :], proj[:, HQ:HQ + 4, :]
            turn_keys(0)
            dve.wait_ge(sem("own_out"), 1)
            dve.tensor_reduce(omax, S[:, :, 512:SW], AX, ALU.max)
            dve.wait_ge(sem("sig_f"), 1)
            for h in range(HH):
                ins = dve.tensor_scalar(proj[:, HF + h, :], proj[:, HF + h, :], lbt[:, 5, h:h + 1], lbt[:, 4, h:h + 1], ALU.mult, ALU.add)
            ins.then_inc(sem("f_ready"), 1)
            turn_keys(1)
            turn_keys(2)
            dve.wait_ge(sem("logf"), 1)
            dve.tensor_scalar(kin, kin, -1.0, 1.0, ALU.mult, ALU.add).then_inc(sem("kin_ready"), 1)
            for h in range(HH):
                ins = dve.tensor_tensor_scan(hb[:, h, :], C("carry"), hkt[:, h, :], 0.0, ALU.mult, ALU.add)
            ins.then_inc(sem("b_ready"), 1)
            turn_keys(3)
            dve.wait_ge(sem("b_ready"), 1)
            bp, bs = hb[:, :, 0:TP].rearrange("p h (n k) -> p h n k", k=P), hb[:, :, SAMP].rearrange("p h (n k) -> p h n k", k=TS)
            kp, ks = hkt[:, :, 0:TP].rearrange("p h (n k) -> p h n k", k=P), hkt[:, :, SAMP].rearrange("p h (n k) -> p h n k", k=TS)
            dve.tensor_tensor(kp, bp[:, :, :, P - 1:P].broadcast_to([P, HH, 2, P]), bp, ALU.subtract)
            dve.tensor_tensor(ks, bs[:, :, :, TS - 1:TS].broadcast_to([P, HH, NSEQ, TS]), bs, ALU.subtract).then_inc(sem("kd_ready"), 1)
            turn_keys(4)
            dve.memset(hA[:, :, :, :], 0.0)
            dve.memset(hAs[:, :, :], 0.0)
            dve.wait_ge(sem("eb"), 1)
            dve.tensor_copy(stat[:, 328:332], hqt[:, :, TP - 1])
            link(dve.tensor_copy(stat[:, 332:332 + HH * NSEQ].rearrange("p (h b) -> p h b", h=HH),
                                 hqt[:, :, SAMP].rearrange("p h (b t) -> p h b t", t=TS)[:, :, :, TS - 1]))
            dve.tensor_tensor(hqt[:, :, :], hqt[:, :, :], q, ALU.mult).then_inc(sem("qt_ready"), 1)
            turn_keys(5)
            dve.wait_ge(sem("ekd"), 1)
            dve.wait_ge(sem("kin_ready"), 1)
            dve.tensor_tensor(hkt[:, :, :], hkt[:, :, :], kin, ALU.mult).then_inc(sem("kt_ready"), 1)
            turn_keys(6)
            turn_keys(7)
            block_sums(0)
            dve.wait_ge(sem("lvl_ready"), 1)
            for b in range(2, NSEQ):
                for j in range(4):
                    turn_keys(4 * b + j)
                    if j == 1:
                        block_sums(b - 1)
                    gi = (4 * b + j - 10) // 2
                    if j % 2 == 0 and 0 <= gi < 8:
                        keep(gi)
            block_sums(NSEQ - 1)

            dve.wait_ge(sem("gate_sum"), 1)
            link(dve.tensor_copy(gate, ps[:, 1, 0:64]))
            g3 = gate.rearrange(bn, b=NSEQ)
            g_m, g_n = over(g3, 2, NB), over(g3, 3, NB)
            dve.wait_ge(sem("k_stored"), 32)
            link(dve.tensor_tensor(cmp1[:, :, :, :], g_m, g_n, ALU.is_gt))
            link(dve.tensor_tensor(cmp2[:, :, :, :], g_m, g_n, ALU.is_equal))
            link(dve.tensor_tensor(cmp2[:, :, :, :], cmp2[:, :, :, :], over(C("tie").rearrange("p (n m) -> p n m", n=NB), 1, NSEQ), ALU.mult))
            link(dve.tensor_tensor(cmp1[:, :, :, :], cmp1[:, :, :, :], cmp2[:, :, :, :], ALU.add))
            link(dve.tensor_reduce(pen.rearrange(bn, b=NSEQ), cmp1[:, :, :, :], AX, ALU.add))
            link(dve.tensor_scalar(pen, pen, TOPK - 0.5, NEG, ALU.is_gt, ALU.mult))
            link(dve.tensor_tensor(bmax, bmax, pen, ALU.add))
            link(dve.tensor_reduce(rmax, bmax.rearrange(bn, b=NSEQ), AX, ALU.max))
            link(dve.tensor_tensor(rmax, rmax, omax, ALU.max))
            for a in range(4):
                ins = dve.tensor_copy(lane4[0:32, 8 * a:8 * a + 8], rmax[32 * a:32 * a + 32, :])
            link(ins)
            dve.tensor_reduce(rmax[0:32, :], lane4[0:32, :].rearrange("p (a b) -> p b a", a=4), AX, ALU.max).then_inc(sem("row_max"), 1)

            def choose(b):
                dve.tensor_tensor(cached[:, b], cached[:, b], over(pen[:, b * NB:(b + 1) * NB], 2, 64), ALU.add).then_inc(sem("s_chosen"), 1)

            choose(0)
            choose(1)
            dve.wait_ge(sem("max_spread"), 1)
            dve.tensor_scalar(shift, ps[:, 1, 64:72], -1.0, None, ALU.mult).then_inc(sem("shift_ready"), 1)
            dve.wait_ge(sem("d_done"), 1)
            for b in range(NSEQ):
                if b + 2 < NSEQ:
                    choose(b + 2)
                dve.wait_ge(sem("s_exp"), b + 1)
                dve.transpose(Pt[:, b], S[:, b, :].rearrange("p (c n) -> p c n", n=32)).then_inc(sem("probs_ready"), 1)
            dve.wait_ge(sem("probs_ready"), NSEQ)
            def sample_values(h):
                dve.tensor_tensor(vms[:, :, :], over(hvs[:, h, :], 1, NSEQ), over(C("seq", TSA), 2, DK), ALU.mult).then_inc(sem("vm_ready"), 1)

            dve.wait_ge(sem("h_tok"), 1)
            sample_values(0)

            def sample_state(h):
                if h == 0:
                    dve.wait_ge(sem("s0_landed"), 64)
                    dve.wait_ge(sem("o_done"), 1)
                eb = over(stat[:, 332 + NSEQ * h:332 + NSEQ * (h + 1)], 2, DK)
                link(dve.tensor_tensor(S0[:, :, h, :], S0[:, :, h, :], eb, ALU.mult))
                if h == 0:
                    for hh in range(HH):
                        ins = dve.scalar_tensor_tensor(Sfin[:, hh, :], D0[:, hh, :], stat[:, 328 + hh:329 + hh], ps[:, 7, hh * DK:(hh + 1) * DK], ALU.mult, ALU.add)
                    ins.then_inc(sem("state_p"), 1)
                dve.wait_ge(sem("ds_done"), h + 1)
                dve.tensor_tensor(S0[:, :, h, :], S0[:, :, h, :], ps[:, 2:4, :].rearrange("p t (b e) -> p (t b) e", e=DK), ALU.add).then_inc(sem("state_s"), 1)
                if h + 1 < HH:
                    sample_values(h + 1)

            dve.wait_ge(sem("probs_sum"), 1)
            link(dve.reciprocal(rden, ps[:, 1, 128:136]))
            for j in range(4):
                rows = slice(32 * j, 32 * j + 32)
                ins = dve.tensor_copy(rrow[rows, :], rden[rows, :].rearrange("p (g j) -> p g j", j=4)[:, :, j])
            ins.then_inc(sem("rden_ready"), 1)
            sample_state(0)
            sample_state(1)
            def o_normed(h):
                if h == 0:
                    dve.wait_ge(sem("o_root"), 1)
                    dve.wait_ge(sem("silu_g"), 1)
                link(dve.reciprocal(hx[1][:, h, :], hx[1][:, h, :]))
                link(dve.tensor_tensor(hb[:, h, :], hb[:, h, :], hx[1][:, h, :], ALU.mult))
                dve.scalar_tensor_tensor(proj[:, HQ + h, :], hb[:, h, :], cols[:, R_ON:R_ON + 1], proj[:, HG + h, :], ALU.mult, ALU.mult).then_inc(sem("oa_ready"), 1)

            def sample_out(g):
                dve.wait_ge(sem("v_summed"), g + 1)
                dve.scalar_tensor_tensor(om[:, :, :], ps[:, g, :].rearrange("p (h d) -> p h d", h=AH), rrow[:, g:g + 1],
                                         over(C("ownhead"), 2, DH), ALU.mult, ALU.mult).then_inc(sem("om_ready"), 1)
                dve.wait_ge(sem("ob_turned"), g + 1)
                dve.tensor_copy(proj[:, AQ:AQ + 4, TP + 16 * g:TP + 16 * g + 16], ps[:, (2, 7)[g], 0:64].rearrange("p (a t) -> p a t", a=PAIRS)).then_inc(sem("ob_s"), 1)

            def pa_mask(h):
                bank = 4 + h % 2
                if h >= 2:
                    dve.wait_ge(sem("pa_turned"), h - 1)
                dve.wait_ge(sem("pa_scored"), h + 1)
                dve.tensor_tensor(pa[:, h % 2, 0:P], ps[:, bank, 0:P], C("causal"), ALU.add)
                dve.tensor_copy(pa[:, h % 2, P:2 * P], ps[:, bank, P:2 * P])
                link(dve.tensor_tensor(pa[:, h % 2, 2 * P:3 * P], ps[:, bank, 2 * P:3 * P], C("causal"), ALU.add))
                dve.tensor_reduce(nmx[:, h % 2, 0:1], pa[:, h % 2, 0:P], AX, ALU.max, negate=True)
                dve.tensor_reduce(nmx[:, h % 2, 1:2], pa[:, h % 2, P:3 * P], AX, ALU.max, negate=True).then_inc(sem("pa_masked"), 1)

            def pa_norm(h):
                dve.wait_ge(sem("pa_exp"), h + 1)
                link(dve.reciprocal(den[:, h % 2, :], den[:, h % 2, :]))
                dve.tensor_scalar(pa[:, h % 2, 0:P], pa[:, h % 2, 0:P], den[:, h % 2, 0:1], None, ALU.mult)
                dve.tensor_scalar(pa[:, h % 2, P:3 * P], pa[:, h % 2, P:3 * P], den[:, h % 2, 1:2], None, ALU.mult).then_inc(sem("pa_ready"), 1)

            for h in range(AH):
                if h in (1, 3):
                    sample_state(2 + h // 2)
                pa_mask(h)
                pa_norm(h)
                if h < HH:
                    o_normed(h)
                if h == 5:
                    dve.wait_ge(sem("oab_hi"), 1)
                    dve.tensor_tensor(oa_lo[:, :, :], proj[:, HQ:HQ + 4, :], oa_hi[:, :, :].bitcast(F32), ALU.subtract).then_inc(sem("oab_lo"), 1)
            sample_out(0)

            def lo_b(w, rows=BK):
                lo(w, (w + 64) % NSLOT, w % 2, rows)

            def gated(cg, j):
                u = proj[:, (UA, UB)[j] + 4 * cg:(UA, UB)[j] + 4 * cg + 4, :]
                dve.wait_ge(sem("w_used"), 2 * (46 + 2 * cg + j + 1))
                dve.tensor_tensor(u, ps[:, 4 * j:4 * j + 4, 0:T], u, ALU.mult).then_inc(sem("gated"), 1)

            def merge(cg):
                ua, ub = proj[:, UA + 4 * cg:UA + 4 * cg + 4, :], proj[:, UB + 4 * cg:UB + 4 * cg + 4, :]
                dve.wait_ge(sem("gated"), 2 * cg + 2)
                dve.tensor_tensor(ua, ua, ub, ALU.add).then_inc(sem("merged"), 1)

            def m_lower(cg):
                dve.wait_ge(sem("m_hi"), cg + 1)
                dve.tensor_tensor(m_lo[:, 4 * cg:4 * cg + 4, :], proj[:, UA + 4 * cg:UA + 4 * cg + 4, :],
                                  m_hi[:, 4 * cg:4 * cg + 4, :].bitcast(F32), ALU.subtract).then_inc(sem("m_lo"), 1)

            def y1_squares(cg):
                for a, e in ((0, 4),) if cg == 0 else ((4, 5), (5, 6), (6, 7), (7, 8)):
                    dve.wait_ge(sem("y1_out"), e)
                    dve.tensor_tensor(proj[:, 8 + a:8 + e, :], proj[:, a:e, :], proj[:, a:e, :], ALU.mult).then_inc(sem("y1_sq"), 1)

            sample_out(1)
            lo_b(46)
            dve.wait_ge(sem("oab_hi"), 2)
            dve.tensor_tensor(ob_lo[:, :, :], proj[:, AQ:AQ + 4, :], ob_hi[:, :, :].bitcast(F32), ALU.subtract).then_inc(sem("oab_lo"), 1)
            lo_b(47)
            dve.wait_ge(sem("sig_u"), 1)
            gated(0, 0)
            lo_b(48)
            gated(0, 1)
            merge(0)
            lo_b(49)
            m_lower(0)
            gated(1, 0)
            lo_b(50)
            gated(1, 1)
            merge(1)
            m_lower(1)
            lo_b(51)
            lo_b(52)
            y1_squares(0)
            lo_b(53)
            lo_b(54)
            y1_squares(1)
            link(dve.tensor_tensor(gain[:, :, :], part(2), over(cols[:, R_POST1:R_POST1 + DT], 2, CC), ALU.mult))
            normed(xT, proj[:, 0:8, :], proj[:, 0:8, :], gain, None, 2, "x1_ready")
            lo_b(55)
            dve.wait_ge(sem("x1_ready"), DT)
            link(dve.scalar_tensor_tensor(gain[:, :, :], part(4), 1.0, over(cols[:, R_PRE2:R_PRE2 + DT], 2, CC), ALU.add, ALU.mult))
            normed(h32, xT, h32, gain, part(3), 3, "h_ready")

            def product(g, base):
                dve.wait_ge(sem("silu_done"), g + 1)
                dve.wait_ge(sem("w_used"), g * 4 + 112)
                dve.wait_ge(sem("f_lo"), g + 1)
                dve.tensor_tensor(fu[:, :, :], ps[:, base + 2:base + 4, 0:T], fa[:, :, :], ALU.mult).then_inc(sem("fu_ready"), 1)

            def f_lower(g):
                dve.wait_ge(sem("f_hi"), g + 1)
                dve.tensor_tensor(f_lo[:, bass.ds(g * 2, 2), :], fu[:, :, :], f_hi[:, bass.ds(g * 2, 2), :].bitcast(F32), ALU.subtract).then_inc(sem("f_lo"), 1)

            dve.nop().then_inc(sem("fu_ready"), 1)
            dve.nop().then_inc(sem("f_lo"), 1)
            with dve.Fori(0, 5) as i:
                lo(i * 4 + 56, 0, 0)
                product(i * 2, 0)
                lo(i * 4 + 57, 1, 1)
                f_lower(i * 2)
                lo(i * 4 + 58, 2, 0)
                product(i * 2 + 1, 4)
                lo(i * 4 + 59, 3, 1)
                f_lower(i * 2 + 1)

            def y2_squares(cg):
                for a, e in ((0, 4),) if cg == 0 else ((4, 5), (5, 6), (6, 7), (7, 8)):
                    dve.wait_ge(sem("y2_out"), e)
                    dve.tensor_tensor(sq[:, a:e, :], y2[:, a:e, :], y2[:, a:e, :], ALU.mult).then_inc(sem("y2_sq"), 1)

            def lo_d(i):
                lo_b(76 + i, 2 if i % 6 == 5 else BK)

            lo_d(0)
            product(10, 0)
            lo_d(1)
            f_lower(10)
            for i in range(2, 7):
                lo_d(i)
            lo_d(7)
            y2_squares(0)
            for i in range(8, 12):
                lo_d(i)
            y2_squares(1)
            link(dve.tensor_tensor(gain[:, :, :], part(5), over(cols[:, R_POST2:R_POST2 + DT], 2, CC), ALU.mult))
            normed(xT, y2, y2, gain, None, 4, "x2_ready")
            for half in range(2):
                dve.wait_ge(sem("y_turned"), half + 1)
                dve.tensor_copy(ytok[:, 1, half * 512:(half + 1) * 512], ps[:, YB[1] + half, :]).then_inc(sem("y_tok1"), 1)

        @block.tensor
        def _(pe):
            def three(dst, lhs, x_hi, x_lo, first, last):
                h, l = lhs
                pe.matmul(dst, h, x_hi, start=first, stop=False)
                pe.matmul(dst, h, x_lo, start=False, stop=False)
                return pe.matmul(dst, l, x_hi, start=False, stop=last)

            def ada(w, par, k, g=None):
                if k == 0 and g is not None:
                    pe.wait_ge(sem("ada_rows"), g)
                for kt in range(BK):
                    if kt % 2 == 0:
                        pe.wait_ge(sem("lo_split"), w * 2 + (kt // 2 + 1))
                    c = k * BK + kt
                    pe.matmul(ps[0:2 * CC, 4, :], cst[:, c, :], w_hi[:, par, kt, :], start=c == 0, stop=False)
                    ins = pe.matmul(ps[0:2 * CC, 4, :], cst[:, c, :], w_lo[:, par, kt, :], start=False, stop=c == DT - 1)
                    if kt % 2 == 1:
                        ins.then_inc(sem("w_used"), 1)

            def turn_ada(g):
                pe.wait_ge(sem("ada_rows"), g + 1)
                if not isinstance(g, int) or g >= 1:
                    pe.wait_ge(sem("mod_ready"), g)
                for j in range(4):
                    ins = pe.matmul(ps[:, 5, j * CC:(j + 1) * CC], arow[:, j * P:(j + 1) * P], C("foldc", 2 * CC), start=True, stop=True)
                ins.then_inc(sem("mod_rows_turned"), 1)

            def dense(w, par, x_hi, x_lo, kts, first, last, done, bank0=0, free=None, rows=BK):
                for half in range(2):
                    pe.wait_ge(sem("lo_split"), w * 2 + (half + 1))
                    for j in range(4):
                        if free is not None and half == 0:
                            pe.wait_ge(sem(free[0]), free[1] + (j + 1))
                        for kt in range(half * rows // 2, (half + 1) * rows // 2):
                            ins = three(ps[:, bank0 + j, 0:T], (w_hi[:, par, kt, j * P:(j + 1) * P], w_lo[:, par, kt, j * P:(j + 1) * P]),
                                        x_hi[:, kts + kt, :], x_lo[:, kts + kt, :], first and kt == 0, last and kt == rows - 1)
                        if j == 3:
                            ins.then_inc(sem("w_used"), 1)
                        elif last and done and half == 1:
                            ins.then_inc(sem(done), 1)

            pe.wait_ge(sem("const0_landed"), 16)
            pe.wait_ge(sem("c_landed"), 32)
            for k in range(DT):
                ins = pe.transpose(ps[:, 7, k * CC:(k + 1) * CC], crow[:, k * P:(k + 1) * P], C("ident", CC)[:, 0:CC])
            ins.then_inc(sem("rows_turned"), 1)
            pe.wait_ge(sem("c_lo"), 1)
            ada(0, 0, 0)
            ada(1, 1, 1)
            pe.wait_ge(sem("x_landed"), 32)
            for k in range(DT):
                if k >= 4 and k % 2 == 0:
                    pe.wait_ge(sem("x_ready"), k // 2 - 1)
                for tt in range(3):
                    rows = P if tt < 2 else TSA
                    ins = pe.transpose(ps[:, k % 4, tt * P:tt * P + rows], xtok[0:rows, tt, k * P:(k + 1) * P], C("ident", rows)[:, 0:rows])
                ins.then_inc(sem("x_turned"), 1)
            pe.wait_ge(sem("par_landed"), 112)
            pe.transpose(ps[:, 6, 0:R_ALL], prow[0:R_ALL, :], C("ident", R_ALL)[:, 0:R_ALL]).then_inc(sem("rows_turned"), 1)
            for g in range(1, 4):
                ada(2 * g, 0, 0, g)
                turn_ada(g - 1)
                ada(2 * g + 1, 1, 1)
                if g == 1:
                    pe.wait_ge(sem("x_folded"), 3)
                    pe.matmul(ps[:, 7, 0:T], ones, sq[:, 0, :], start=True, stop=True).then_inc(sem("x_sum"), 1)
            turn_ada(3)
            pe.wait_ge(sem("h_lo"), 4)
            dense(8, 0, h_hi, h_lo, 0, True, False, "tile_done")
            pe.wait_ge(sem("h_lo"), 8)
            dense(9, 1, h_hi, h_lo, 4, False, True, "tile_done")
            with pe.Fori(0, 7) as i:
                ada(i * 4 + 10, 0, 0, i + 4)
                ada(i * 4 + 11, 1, 1)
                dense(i * 4 + 12, 0, h_hi, h_lo, 0, True, False, "tile_done", free=("tile_out", i * 4))
                turn_ada(i + 4)
                dense(i * 4 + 13, 1, h_hi, h_lo, 4, False, True, "tile_done")
            ada(38, 0, 0, 11)
            ada(39, 1, 1)
            dense(40, 0, h_hi, h_lo, 0, True, False, "tile_done", free=("tile_out", 28))
            turn_ada(11)
            dense(41, 1, h_hi, h_lo, 4, False, True, "tile_done")

            def swap(j, t0):
                if j:
                    pe.wait_ge(sem("swap_used"), 1)
                for k in range(4):
                    ins = pe.matmul(ps[:, 4 + k, 0:T], C("swap"), proj[:, t0 + k, :], start=True, stop=True)
                ins.then_inc(sem("swapped"), 1)

            def to_tokens(t0, done):
                for tt in range(3):
                    rows = P if tt < 2 else TSA
                    for a in range(PAIRS):
                        ins = pe.transpose(ps[0:rows, 4 + tt, a * P:(a + 1) * P], proj[:, t0 + a, tt * P:tt * P + rows], ident)
                ins.then_inc(sem(done), 1)

            pe.wait_ge(sem("tile_out"), 32)
            pe.wait_ge(sem("mod_ready"), 12)
            pe.wait_ge(sem("const1_landed"), 16)
            swap(0, AQ)
            dense(42, 0, h_hi, h_lo, 0, True, False, "tile_done", free=("tile_out", 32))
            swap(1, AK)
            dense(43, 1, h_hi, h_lo, 4, False, True, "tile_done")
            pe.wait_ge(sem("swap_used"), 2)
            to_tokens(AV, "v_turned")
            dense(44, 0, h_hi, h_lo, 0, True, False, "tile_done", free=("tile_out", 36))
            pe.wait_ge(sem("roped"), 2)
            for i in range(4):
                ins = pe.matmul(ps[:, 7, i * P:(i + 1) * P], C(f"spread{i}"), proj[:, AQ:AQ + 4, SAMP], start=True, stop=True)
            ins.then_inc(sem("spread_done"), 1)
            pe.wait_ge(sem("v_tok"), 1)
            to_tokens(AK, "k_turned_tok")
            dense(45, 1, h_hi, h_lo, 4, False, True, "tile_done")
            pe.wait_ge(sem("tile_out"), 44)
            pe.wait_ge(sem("q_blocks"), 1)
            for b in range(NSEQ):
                for a in range(PAIRS):
                    ins = pe.matmul(ps[0:32, 2, b * TSA:(b + 1) * TSA], Qbd[:, a, b, :], proj[:, AK + a, SAMP], start=a == 0, stop=a == PAIRS - 1)
            ins.then_inc(sem("own_scored"), 1)

            def cached_keys(u):
                b, j = u // 4, u % 4
                if j == 0:
                    pe.wait_ge(sem("wq_ready"), b + 1)
                    if b >= 2:
                        pe.wait_ge(sem("scores_out"), b - 1)
                pe.wait_ge(sem("key_slots"), u + 1)
                for c in range(16):
                    ins = pe.matmul(ps[:, b % 2, j * P:(j + 1) * P], Wq[:, b % 2, c * P:(c + 1) * P], KT[:, u % 2, :, c * 32:(c + 1) * 32],
                                    start=c == 0, stop=c == 15)
                ins.then_inc(sem("kt_used"), 1)

            def values(b, j):
                rows = slice(32 * (b % 4), 32 * (b % 4) + 32)
                if j == 0:
                    pe.wait_ge(sem("probs_ready"), b + 1)
                    if b == 4:
                        pe.wait_ge(sem("rden_ready"), 1)
                pe.wait_ge(sem(f"v_landed{j}"), 48 * (b + 1))
                pe.wait_ge(sem(f"v3_landed{j}"), 16 * (b + 1))
                for q in range(4):
                    ins = pe.matmul(ps[rows, b // 4, :], Pt[:, b, 4 * j + q, :], ring[:, KV_SLOT[j], q * 512:(q + 1) * 512],
                                    start=j + q == 0, stop=False)
                ins.then_inc(sem("value_slots"), 1)
                if j == 3:
                    ins = pe.matmul(ps[rows, b // 4, :], Pt[0:32, b, 16, :], vtok[0:32, 2, :], start=False, stop=True)
                    if b % 4 == 3:
                        ins.then_inc(sem("v_summed"), 1)

            def turn_hgrn():
                pe.wait_ge(sem("kt_ready"), 1)
                for x, b0 in ((hkt, 2), (proj[:, HI:HI + 4, :], 4)):
                    for tt in range(3):
                        rows = P if tt < 2 else TSA
                        bank = b0 + tt if tt < 2 else 6 + (b0 // 4)
                        for h in range(HH):
                            ins = pe.transpose(ps[0:rows, bank, h * P:(h + 1) * P], x[:, h, tt * P:tt * P + rows], ident)
                ins.then_inc(sem("h_turned"), 1)

            def gram(gi):
                li = gi - 1
                if gi == 0:
                    pe.wait_ge(sem("h_tok"), 1)
                else:
                    pe.wait_ge(sem("lv_ready"), li + 1)
                if gi >= 2:
                    pe.wait_ge(sem("kept"), gi - 1)
                left, right = (proj[:, HF:HF + 4, :], proj[:, HQ:HQ + 4, :]) if gi == 0 else (hx[li % 2], hx[li % 2])
                for tt in range(2):
                    for h in range(HH):
                        ins = pe.matmul(ps[:, 2 + 2 * (gi % 2) + tt, h * P:(h + 1) * P], left[:, h, tt * P:(tt + 1) * P], right[:, h, tt * P:(tt + 1) * P], start=True, stop=True)
                if gi == 0 or LEVELS[li] <= 2:
                    for h in range(HH):
                        ins = pe.matmul(ps[0:TSA, 6 + gi % 2, h * TSA:(h + 1) * TSA], left[:, h, SAMP], right[:, h, SAMP], start=True, stop=True)
                ins.then_inc(sem("gram_done"), 1)

            def hgrn_states():
                pe.wait_ge(sem("kept"), 8)
                for tt, bank in ((0, 2), (1, 7)):
                    for h in range(HH):
                        ins = pe.matmul(ps[:, bank, h * DK:(h + 1) * DK], hktok[:, tt, h, :], hvtok[:, tt, h, :], start=True, stop=True)
                ins.then_inc(sem("d_done"), 1)

            def hgrn_out():
                pe.wait_ge(sem("d0_ready"), 1)
                pe.wait_ge(sem("qt_ready"), 1)
                for h in range(HH):
                    for tt in range(2):
                        dst = ps[:, 4 + tt, h * P:(h + 1) * P]
                        pe.matmul(dst, hvtok[:, tt, h, :], hA[:, tt, h, :], start=True, stop=tt == 0)
                        if tt:
                            pe.matmul(dst, D0[:, h, :], hqt[:, h, P:TP], start=False, stop=True)

            def hgrn_sample_out(h):
                pe.wait_ge(sem("s0_landed"), 64)
                pe.matmul(ps[:, 6, h * TSA:(h + 1) * TSA], hvs[:, h, :], hAs[:, h, :], start=True, stop=False, skip_group_check=True)
                for b in range(NSEQ):
                    c = h * TSA + b * TS
                    ins = pe.matmul(ps[:, 6, c:c + TS], S0[:, b, h, :], hqt[:, h, TP + b * TS:TP + (b + 1) * TS], start=False, stop=b == NSEQ - 1, skip_group_check=True)
                if h == HH - 1:
                    ins.then_inc(sem("o_done"), 1)

            def sample_states(h):
                pe.wait_ge(sem("vm_ready"), h + 1)
                if h >= 1:
                    pe.wait_ge(sem("state_s"), h)
                for g in range(2):
                    ins = pe.matmul(ps[:, 2 + g, :], hks[:, h, :], vms[:, 4 * g:4 * g + 4, :], start=True, stop=True)
                ins.then_inc(sem("ds_done"), 1)

            def o_sum():
                pe.wait_ge(sem("o_sq"), 1)
                for tt in range(3):
                    n = P if tt < 2 else TSA
                    ins = pe.matmul(ps[:, 4 + tt, 0:HH * n], ones, hx[0][:, :, tt * P:tt * P + n], start=True, stop=True)
                ins.then_inc(sem("o_sum"), 1)

            def sample_out(g):
                pe.wait_ge(sem("om_ready"), g + 1)
                if g:
                    pe.wait_ge(sem("ob_p"), PAIRS)
                else:
                    pe.wait_ge(sem("state_s"), HH)
                for a in range(PAIRS):
                    ins = pe.matmul(ps[:, (2, 7)[g], a * 16:(a + 1) * 16], om[:, 2 * a:2 * a + 2, :], C("sumheads"), start=True, stop=True)
                ins.then_inc(sem("ob_turned"), 1)

            def pa_scores(h):
                rows = slice(64 * (h % 2), 64 * (h % 2) + 64)
                bank = 4 + h % 2
                if h == 0:
                    pe.wait_ge(sem("o_root"), 1)
                if h >= 2:
                    pe.wait_ge(sem("pa_masked"), h - 1)
                qt, kt = proj[rows, AQ + h // 2, :], proj[rows, AK + h // 2, :]
                pe.matmul(ps[:, bank, 0:P], qt[:, 0:P], kt[:, 0:P], start=True, stop=True)
                pe.matmul(ps[:, bank, P:3 * P], qt[:, P:TP], kt[:, 0:TP], start=True, stop=True).then_inc(sem("pa_scored"), 1)

            def pa_turn(h):
                pe.wait_ge(sem("pa_ready"), h + 1)
                if h >= 1:
                    pe.wait_ge(sem("paT_ready"), h)
                for c in range(3):
                    ins = pe.transpose(ps[:, 6, c * P:(c + 1) * P], pa[:, h % 2, c * P:(c + 1) * P], ident)
                ins.then_inc(sem("pa_turned"), 1)

            def pa_values(h):
                pe.wait_ge(sem("paT_ready"), h + 1)
                if h == 0:
                    pe.wait_ge(sem("state_p"), 1)
                if h >= 2 and h % 2 == 0:
                    pe.wait_ge(sem("ob_p"), h // 2)
                rows = slice(64 * (h % 2), 64 * (h % 2) + 64)
                v = lambda tt: vtok[:, tt, h * DH:(h + 1) * DH]
                pe.matmul(ps[rows, 7, 0:P], v(0), paT[:, 0:P], start=True, stop=True)
                pe.matmul(ps[rows, 7, P:TP], v(0), paT[:, P:2 * P], start=True, stop=False)
                pe.matmul(ps[rows, 7, P:TP], v(1), paT[:, 2 * P:3 * P], start=False, stop=True).then_inc(sem("pv_done"), 1)

            pe.wait_ge(sem("v_tok"), 1)
            between = {6: [turn_hgrn], 24: [hgrn_states]}
            for gi in range(8):
                between[8 + 2 * gi] = [lambda gi=gi: gram(gi)]
            for u in range(4 * NSEQ):
                cached_keys(u)
                for step in between.get(u, ()):
                    step()

            pe.wait_ge(sem("gate_parts"), NSEQ)
            pe.matmul(ps[:, 1, 0:64], fold, stat[:, 0:64], start=True, stop=True).then_inc(sem("gate_sum"), 1)
            hgrn_out()
            pe.wait_ge(sem("row_max"), 1)
            pe.matmul(ps[:, 1, 64:72], fold[0:32, :], stat[0:32, 256:264], start=True, stop=True).then_inc(sem("max_spread"), 1)

            after = {(0, 3): lambda: (probs_sum(), hgrn_sample_out(0)), (1, 0): lambda: hgrn_sample_out(1), (1, 1): lambda: hgrn_sample_out(2),
                     (1, 2): lambda: hgrn_sample_out(3), (1, 3): lambda: sample_states(0), (2, 0): lambda: o_sum(),
                     (2, 1): lambda: sample_states(1), (3, 1): lambda: sample_states(2), (4, 1): lambda: sample_states(3)}

            def probs_sum():
                pe.wait_ge(sem("s_exp"), NSEQ)
                pe.matmul(ps[:, 1, 128:136], fold, stat[:, 320:328], start=True, stop=True).then_inc(sem("probs_sum"), 1)

            def prompt_step(k):
                if 1 <= k <= AH:
                    pa_turn(k - 1)
                if k < AH:
                    pa_scores(k)
                if 2 <= k <= AH + 1:
                    pa_values(k - 2)

            k = 0
            for b in range(NSEQ):
                for j in range(4):
                    values(b, j)
                    if (b, j) in after:
                        after[b, j]()
                    if j % 2 == 1 and (b, j) >= (2, 3) and k < AH + 2:
                        prompt_step(k)
                        k += 1
                    if (b, j) == (6, 3):
                        sample_out(0)
            sample_out(1)

            for cg in range(2):
                for j, (x_hi, x_lo) in enumerate(((oa_hi, oa_lo), (ob_hi, ob_lo))):
                    w = 46 + 2 * cg + j
                    if cg == 0:
                        pe.wait_ge(sem("oab_lo"), j + 1)
                        if j:
                            pe.wait_ge(sem("ob_s"), 2)
                    else:
                        pe.wait_ge(sem("gated"), 2 * (cg - 1) + j + 1)
                    dense(w, w % 2, x_hi, x_lo, 0, True, True, None, 4 * j)
            pe.wait_ge(sem("gated"), 3)
            pe.wait_ge(sem("m_lo"), 1)

            def sum_squares(src, which, first, last, bank, done, each=None):
                for i, k in enumerate(which):
                    if each:
                        pe.wait_ge(sem(each[0]), each[1] + i + 1)
                    ins = pe.matmul(ps[:, bank, 0:T], ones, src[:, k, :], start=k == first, stop=k == last)
                if which[-1] == last:
                    ins.then_inc(sem(done), 1)

            y1sq = proj[:, 8:16, :]
            dense(50, 0, m_hi, m_lo, 0, True, False, "y1_done")
            pe.wait_ge(sem("m_lo"), 2)
            dense(51, 1, m_hi, m_lo, 4, False, True, "y1_done")
            dense(52, 0, m_hi, m_lo, 0, True, False, "y1_done", free=("y1_out", 0))
            pe.wait_ge(sem("y1_sq"), 1)
            sum_squares(y1sq, range(0, 4), 0, 7, 4, "y1_sum")
            dense(53, 1, m_hi, m_lo, 4, False, True, "y1_done")
            sum_squares(y1sq, range(4, 8), 0, 7, 4, "y1_sum", ("y1_sq", 1))
            sum_squares(sq, range(0, 8), 0, 7, 5, "x1_sum", ("x1_sq", 0))
            pe.wait_ge(sem("h_lo"), 12)

            pe.wait_ge(sem("y1_out"), 8)
            dense(54, 0, h_hi, h_lo, 0, True, False, "gu_done")
            pe.wait_ge(sem("h_lo"), 16)
            dense(55, 1, h_hi, h_lo, 4, False, True, "gu_done")
            pe.wait_ge(sem("root"), 3)
            with pe.Fori(0, 5) as i:
                pe.wait_ge(sem("fu_ready"), i * 2 + 1)
                dense(i * 4 + 56, 0, h_hi, h_lo, 0, True, False, "gu_done", 4)
                dense(i * 4 + 57, 1, h_hi, h_lo, 4, False, True, "gu_done", 4)
                pe.wait_ge(sem("fu_ready"), i * 2 + 2)
                dense(i * 4 + 58, 0, h_hi, h_lo, 0, True, False, "gu_done")
                dense(i * 4 + 59, 1, h_hi, h_lo, 4, False, True, "gu_done")
            for cg in range(2):
                for c in range(6):
                    w = 76 + 6 * cg + c
                    if cg == 0:
                        pe.wait_ge(sem("f_lo"), min(2 * c + 3, 12))
                        if c == 0:
                            pe.wait_ge(sem("fu_ready"), 11)
                    elif c == 0:
                        pe.wait_ge(sem("fu_ready"), 12)
                    dense(w, w % 2, f_hi, f_lo, 4 * c, c == 0, c == 5, "y2_done", 4 * (1 - cg), rows=2 if c == 5 else BK)
                    if cg == 1 and c == 1:
                        pe.wait_ge(sem("y2_sq"), 1)
                        sum_squares(sq, range(0, 4), 0, 7, 4, "y2_sum")
            sum_squares(sq, range(4, 8), 0, 7, 4, "y2_sum", ("y2_sq", 1))
            pe.wait_ge(sem("y2_out"), 8)
            for k in range(DT):
                pe.wait_ge(sem("x2_ready"), k + 1)
                for tt in range(3):
                    rows = P if tt < 2 else TSA
                    ins = pe.transpose(ps[0:rows, YB[tt] + k // 4, (k % 4) * P:(k % 4 + 1) * P], xT[:, k, tt * P:tt * P + rows], ident)
                if k % 4 == 3:
                    ins.then_inc(sem("y_turned"), 1)


INPUTS = ["x_prompt", "x_sample", "c_prompt", "c_sample", "state_hgrn", "cache_k", "cache_v", "page_table", "hg_lb",
          "w_ada", "b_ada", "g_pre1", "g_post1", "w_in", "g_onorm", "w_proj_a", "w_proj_b", "w_out", "g_pre2", "g_post2",
          "w_gu", "w_down"]
OUTPUTS = {
    "y_prompt": (1, TP, D), "y_sample": (NSEQ, TS, D),
    "state_p": (1, 1, HH, DK, DK), "state_s": (1, NSEQ, HH, DK, DK),
    "k_prompt": (1, 1, TP, AH, DH), "v_prompt": (1, 1, TP, AH, DH),
    "k_sample": (1, NSEQ, TS, AH, DH), "v_sample": (1, NSEQ, TS, AH, DH),
}


def kernel(**inputs):
    import concourse.bacc as bacc
    from concourse.bass_utils import run_bass_kernel_spmd

    nc = bacc.Bacc("TRN2", target_bir_lowering=False, num_devices=1)
    arrays = {k: np.ascontiguousarray(inputs[k]) for k in INPUTS}
    arrays["cache_k"] = arrays["cache_k"].reshape(1, -1, PAGE, AH * DH)
    arrays["cache_v"] = arrays["cache_v"].reshape(1, -1, PAGE, AH * DH)
    arrays["const"] = constants()[0]
    arrays["lvl"] = level_masks()
    inp = {k: nc.dram_tensor(k, a.shape, mybir.dt.from_np(a.dtype), kind="ExternalInput").ap() for k, a in arrays.items()}
    out = {k: nc.dram_tensor("out_" + k, s, F32, kind="ExternalOutput").ap() for k, s in OUTPUTS.items()}
    build(nc, inp, out)
    r = run_bass_kernel_spmd(nc, [arrays], core_ids=[0]).results[0]
    return tuple(r["out_" + k] for k in OUTPUTS)
```
